# Optimizing a Trainium2 kernel written in Bass

```python
import jax, jax.numpy as jnp
from jax import lax
import numpy as np

D_MODEL = 1024
BATCH = 1
SEQ = 512
DEPTH = 2
DEC_BATCH = 8
DEC_SEQ = 16
PAST_LEN = 1024

CHUNK = 64
N_META = 16
Q_BLOCK = 128
EPS = 1e-6
MLA_HEADS = 8
QK_NOPE = 64
QK_ROPE = 32
V_HEAD = 64
Q_LORA = 256
KV_LORA = 128
ROPE_THETA = 10000.0
HG_HEADS = 4
HG_DK = 128
HG_DV = 128
D_FF = 2816
CONV_W = 3

MLA_WIDTH = MLA_HEADS * V_HEAD
HG_KW = HG_HEADS * HG_DK
HG_WIDTH = HG_HEADS * HG_DV
MIX_WIDTH = MLA_WIDTH + HG_WIDTH
IN_WIDTH = Q_LORA + KV_LORA + QK_ROPE + 2 * HG_KW + 2 * HG_WIDTH

kernel_name = 'hymba_mla_hgrn2_convglu_stream_step'

def rmsnorm(x, w):
    xf = x.astype(jnp.float32)
    y = xf * lax.rsqrt(jnp.mean(xf * xf, axis=-1, keepdims=True) + EPS)
    return (y * w.astype(jnp.float32)).astype(x.dtype)

def rope(x, pos):
    half = QK_ROPE // 2
    inv = ROPE_THETA ** (-jnp.arange(half, dtype=jnp.float32) / half)
    ang = pos.astype(jnp.float32)[:, None] * inv
    ang = ang.reshape((ang.shape[0],) + (1,) * (x.ndim - 3) + (half,))
    cos, sin = jnp.cos(ang), jnp.sin(ang)
    xf = x.astype(jnp.float32)
    x1, x2 = xf[..., :half], xf[..., half:]
    return jnp.concatenate([x1 * cos - x2 * sin, x1 * sin + x2 * cos], axis=-1).astype(x.dtype)

def split_in(z):
    sizes = (Q_LORA, KV_LORA, QK_ROPE, HG_KW, HG_KW, HG_WIDTH, HG_WIDTH)
    outs, off = [], 0
    for s in sizes:
        outs.append(z[..., off:off + s])
        off += s
    return outs

def mla_core(q_lat, q_pe, kv_lat, k_pe, q_pos, k_pos):
    scale = (QK_NOPE + QK_ROPE) ** -0.5
    s = (jnp.einsum('bthr,bsr->bhts', q_lat, kv_lat)
         + jnp.einsum('bthp,bsp->bhts', q_pe, k_pe)).astype(jnp.float32) * scale
    allowed = (q_pos // CHUNK)[:, None] >= (k_pos // CHUNK)[None, :]
    s = jnp.where(allowed[None, None], s, -jnp.inf)
    p = jax.nn.softmax(s, axis=-1).astype(kv_lat.dtype)
    return jnp.einsum('bhts,bsr->bthr', p, kv_lat)

def mla_prompt(q_lat, q_pe, kv_lat, k_pe, pos):
    L = q_lat.shape[1]
    outs = []
    for start in range(0, L, Q_BLOCK):
        stop = min(start + Q_BLOCK, L)
        last_chunk = (stop - 1 - N_META) // CHUNK
        kmax = min(L, N_META + (last_chunk + 1) * CHUNK)
        outs.append(mla_core(q_lat[:, start:stop], q_pe[:, start:stop], kv_lat[:, :kmax],
                             k_pe[:, :kmax], pos[start:stop], pos[:kmax]))
    return jnp.concatenate(outs, axis=1)

def hgrn_chunk(S, q, gl, k, v):
    C = q.shape[1]
    G = jnp.cumsum(gl, axis=1)
    G_last = G[:, -1]
    o_inter = jnp.einsum('bthk,bhkv->bthv', q * jnp.exp(G), S)
    tri = jnp.tril(jnp.ones((C, C), dtype=bool))
    diff = G[:, :, None] - G[:, None, :]
    decay = jnp.exp(jnp.where(tri[None, :, :, None, None], diff, -jnp.inf))
    A = jnp.einsum('bthk,btshk,bshk->bhts', q, decay, k)
    o = o_inter + jnp.einsum('bhts,bshv->bthv', A, v)
    S_new = jnp.exp(G_last)[..., None] * S + jnp.einsum('bshk,bshv->bhkv', k * jnp.exp(G_last[:, None] - G), v)
    return S_new, o

def hgrn2(hq, hf, hi, hg, lb, gain, S0, is_prompt):
    B, T, _ = hq.shape
    f32 = jnp.float32
    q = jax.nn.silu(hq.astype(f32)).reshape(B, T, HG_HEADS, HG_DK)
    zf = hf.astype(f32).reshape(B, T, HG_HEADS, HG_DK)
    lbh = lb.reshape(HG_HEADS, HG_DK)
    f = lbh + (1.0 - lbh) * jax.nn.sigmoid(zf)
    gl = jnp.log(f)
    k = (1.0 - lbh) * jax.nn.sigmoid(-zf)
    v = hi.astype(f32).reshape(B, T, HG_HEADS, HG_DV)
    S0 = S0.astype(f32)
    if is_prompt:
        n_pad = (-T) % CHUNK
        n_chunks = (T + n_pad) // CHUNK

        def to_chunks(a):
            a = jnp.pad(a, ((0, 0), (n_pad, 0), (0, 0), (0, 0)))
            return a.reshape(B, n_chunks, CHUNK, HG_HEADS, a.shape[-1]).swapaxes(0, 1)

        def step(S, xs):
            return hgrn_chunk(S, *xs)

        S_new, o = lax.scan(step, S0, (to_chunks(q), to_chunks(gl), to_chunks(k), to_chunks(v)))
        o = o.swapaxes(0, 1).reshape(B, n_chunks * CHUNK, HG_HEADS, HG_DV)[:, n_pad:]
    else:
        S_new, o = hgrn_chunk(S0, q, gl, k, v)
    o = rmsnorm(o, gain) * jax.nn.silu(hg.astype(f32).reshape(B, T, HG_HEADS, HG_DV))
    return o.reshape(B, T, HG_WIDTH).astype(hq.dtype), S_new

def token_mixers(h, pos, p, lb, kv_past, pe_past, past_pos, S0, is_prompt):
    B, T, _ = h.shape
    c_q, c_kv, k_pe, hq, hf, hi, hg = split_in(h @ p['w_in'])
    q = (rmsnorm(c_q, p['q_norm']) @ p['w_uq']).reshape(B, T, MLA_HEADS, QK_NOPE + QK_ROPE)
    q_nope = q[..., :QK_NOPE]
    q_pe = rope(q[..., QK_NOPE:], pos)
    kv_lat = rmsnorm(c_kv, p['kv_norm'])
    k_pe = rope(k_pe, pos)
    q_lat = jnp.einsum('bthd,rhd->bthr', q_nope, p['w_uk'])
    if is_prompt:
        o_lat = mla_prompt(q_lat, q_pe, kv_lat, k_pe, pos)
    else:
        o_lat = mla_core(q_lat, q_pe,
                         jnp.concatenate([kv_past.astype(kv_lat.dtype), kv_lat], axis=1),
                         jnp.concatenate([pe_past.astype(k_pe.dtype), k_pe], axis=1),
                         pos, jnp.concatenate([past_pos, pos]))
    o_a = jnp.einsum('bthr,rhd->bthd', o_lat, p['w_uv']).reshape(B, T, MLA_WIDTH)
    o_b, S_new = hgrn2(hq, hf, hi, hg, lb, p['hg_out_norm'], S0, is_prompt)
    y = jnp.concatenate([o_a, o_b], axis=-1) @ p['w_out']
    return y, kv_lat, k_pe, S_new

def conv_ffn(h, p, buf):
    u = h @ p['w_ffn_up']
    a, v = u[..., :D_FF], u[..., D_FF:]
    T = a.shape[1]
    ext = jnp.concatenate([buf.astype(a.dtype), a], axis=1)
    w = p['ffn_conv_w']
    c = p['ffn_conv_b'] + sum(ext[:, j:j + T] * w[j] for j in range(CONV_W))
    out = (jax.nn.silu(c) * v) @ p['w_ffn_down']
    return out, ext[:, -(CONV_W - 1):]

def layer(x, pos, p, lb, kv_past, pe_past, past_pos, S0, conv_buf, is_prompt):
    h = rmsnorm(x, p['norm_mix_pre'])
    mix, kv_lat, k_pe, S_new = token_mixers(h, pos, p, lb, kv_past, pe_past, past_pos, S0, is_prompt)
    x = x + rmsnorm(mix, p['norm_mix_post'])
    h = rmsnorm(x, p['norm_ffn_pre'])
    f, buf = conv_ffn(h, p, conv_buf)
    x = x + rmsnorm(f, p['norm_ffn_post'])
    return x, kv_lat, k_pe, S_new, buf

def setup_inputs(seed: int = 0) -> dict:
    key = jax.random.key(seed)
    ks = jax.random.split(key, 26)
    f32 = jnp.float32

    def nrm(k, shape, scale=1.0):
        return jax.random.normal(k, shape, f32) * scale

    def gain(k, shape):
        return 1.0 + 0.05 * jax.random.normal(k, shape, f32)

    return {
        'x_prompt': nrm(ks[0], (BATCH, SEQ, D_MODEL)),
        'x_sample': nrm(ks[1], (DEC_BATCH, DEC_SEQ, D_MODEL)),
        'cache_kv_latent': nrm(ks[2], (DEPTH, DEC_BATCH, PAST_LEN, KV_LORA)),
        'cache_k_rope': nrm(ks[3], (DEPTH, DEC_BATCH, PAST_LEN, QK_ROPE)),
        'state_hgrn': nrm(ks[4], (DEPTH, DEC_BATCH, HG_HEADS, HG_DK, HG_DV), 0.5),
        'state_ffn_conv': nrm(ks[5], (DEPTH, DEC_BATCH, CONV_W - 1, D_FF)),
        'meta_tokens': nrm(ks[6], (N_META, D_MODEL)),
        'w_in': nrm(ks[7], (DEPTH, D_MODEL, IN_WIDTH), D_MODEL ** -0.5),
        'norm_mix_pre': gain(ks[8], (DEPTH, D_MODEL)),
        'norm_mix_post': gain(ks[9], (DEPTH, D_MODEL)),
        'q_norm': gain(ks[10], (DEPTH, Q_LORA)),
        'kv_norm': gain(ks[11], (DEPTH, KV_LORA)),
        'w_uq': nrm(ks[12], (DEPTH, Q_LORA, MLA_HEADS * (QK_NOPE + QK_ROPE)), Q_LORA ** -0.5),
        'w_uk': nrm(ks[13], (DEPTH, KV_LORA, MLA_HEADS, QK_NOPE), KV_LORA ** -0.5),
        'w_uv': nrm(ks[14], (DEPTH, KV_LORA, MLA_HEADS, V_HEAD), KV_LORA ** -0.5),
        'hg_lower_bounds': 1.0 + 0.1 * jax.random.normal(ks[15], (DEPTH, HG_KW), f32),
        'hg_out_norm': gain(ks[16], (DEPTH, HG_DV)),
        'w_out': nrm(ks[17], (DEPTH, MIX_WIDTH, D_MODEL), MIX_WIDTH ** -0.5),
        'norm_ffn_pre': gain(ks[18], (DEPTH, D_MODEL)),
        'norm_ffn_post': gain(ks[19], (DEPTH, D_MODEL)),
        'w_ffn_up': nrm(ks[20], (DEPTH, D_MODEL, 2 * D_FF), D_MODEL ** -0.5),
        'ffn_conv_w': nrm(ks[21], (DEPTH, CONV_W, D_FF), CONV_W ** -0.5),
        'ffn_conv_b': nrm(ks[22], (DEPTH, D_FF), 0.01),
        'w_ffn_down': nrm(ks[23], (DEPTH, D_FF, D_MODEL), D_FF ** -0.5),
        'final_norm': gain(ks[24], (D_MODEL,)),
    }

def reference(x_prompt, x_sample, cache_kv_latent, cache_k_rope, state_hgrn, state_ffn_conv,
              meta_tokens, w_in, norm_mix_pre, norm_mix_post, q_norm, kv_norm, w_uq, w_uk, w_uv,
              hg_lower_bounds, hg_out_norm, w_out, norm_ffn_pre, norm_ffn_post, w_ffn_up,
              ffn_conv_w, ffn_conv_b, w_ffn_down, final_norm):
    lb_sm = jax.nn.softmax(hg_lower_bounds.astype(jnp.float32), axis=0)
    lb_all = jnp.cumsum(lb_sm, axis=0) - lb_sm[0]

    B = x_prompt.shape[0]
    Bs, Ts = x_sample.shape[0], x_sample.shape[1]
    meta = jnp.broadcast_to(meta_tokens.astype(x_prompt.dtype)[None], (B, N_META, D_MODEL))
    xp = jnp.concatenate([meta, x_prompt], axis=1)
    pos_p = jnp.arange(xp.shape[1], dtype=jnp.int32) - N_META
    past_pos = jnp.arange(cache_kv_latent.shape[2], dtype=jnp.int32)
    pos_s = cache_kv_latent.shape[2] + jnp.arange(Ts, dtype=jnp.int32)
    xs = x_sample

    p_kv, p_pe, p_S, p_buf = [], [], [], []
    s_kv, s_pe, s_S, s_buf = [], [], [], []
    for l in range(DEPTH):
        p = {'w_in': w_in[l], 'norm_mix_pre': norm_mix_pre[l], 'norm_mix_post': norm_mix_post[l],
             'q_norm': q_norm[l], 'kv_norm': kv_norm[l], 'w_uq': w_uq[l], 'w_uk': w_uk[l],
             'w_uv': w_uv[l], 'hg_out_norm': hg_out_norm[l], 'w_out': w_out[l],
             'norm_ffn_pre': norm_ffn_pre[l], 'norm_ffn_post': norm_ffn_post[l],
             'w_ffn_up': w_ffn_up[l], 'ffn_conv_w': ffn_conv_w[l], 'ffn_conv_b': ffn_conv_b[l],
             'w_ffn_down': w_ffn_down[l]}
        S0_p = jnp.zeros((B, HG_HEADS, HG_DK, HG_DV), jnp.float32)
        buf0_p = jnp.zeros((B, CONV_W - 1, D_FF), xp.dtype)
        xp, kv, pe, S, buf = layer(xp, pos_p, p, lb_all[l], None, None, None, S0_p, buf0_p, True)
        p_kv.append(kv); p_pe.append(pe); p_S.append(S); p_buf.append(buf)
        xs, kv, pe, S, buf = layer(xs, pos_s, p, lb_all[l], cache_kv_latent[l], cache_k_rope[l],
                                   past_pos, state_hgrn[l], state_ffn_conv[l], False)
        s_kv.append(kv); s_pe.append(pe); s_S.append(S); s_buf.append(buf)

    y_prompt = rmsnorm(xp[:, N_META:], final_norm)
    y_sample = rmsnorm(xs, final_norm)
    return (y_prompt, y_sample,
            jnp.stack(p_kv), jnp.stack(p_pe), jnp.stack(p_S), jnp.stack(p_buf),
            jnp.stack(s_kv), jnp.stack(s_pe), jnp.stack(s_S), jnp.stack(s_buf))


_drawn_inputs = setup_inputs


def setup_inputs(seed=0):
    import zlib

    import numpy as np

    out = dict(_drawn_inputs(seed))
    spreads = {}
    factors = {'q_norm': 4.356, 'ffn_conv_b': 6.862}
    for name, (base, spread) in spreads.items():
        noise = np.random.default_rng([zlib.crc32(name.encode()), seed]).standard_normal(out[name].shape)
        drawn = base * np.exp(spread * noise) if base else spread * noise
        out[name] = __import__('jax').numpy.asarray(drawn.astype(out[name].dtype))
    for name, factor in factors.items():
        out[name] = (out[name] * factor).astype(out[name].dtype)
    return out
```

```python
from contextlib import ExitStack

import numpy as np

import concourse.bass as bass
from concourse import mybir

F32 = mybir.dt.float32
F32R = mybir.dt.float32r
U8 = mybir.dt.uint8
ALU = mybir.AluOpType
ACT = mybir.ActivationFunctionType
AX_X = mybir.AxisListType.X

P = 128
D = 1024
KD = D // P
DEPTH = 2
META = 16
SEQ = 512
DB, DT = 8, 16
SAMP = DB * DT
PT = META + SEQ
T = PT + SAMP
HALF = T // 2
PAST = 1024
PC = PAST // P
CH = 64
HM, NOPE, ROPE, VH = 8, 64, 32, 64
QL, KL = 256, 128
HG = 4
FF = 2816
KF = FF // P
FH = KF // 2
EPS = 1e-6
SCALE = float(NOPE + ROPE) ** -0.5
BIG = float(2.0 ** 100)
EXT = PT + 2 + DB * (DT + 2)
LEVELS = [64, 32, 16, 8, 4, 2, 1, 0]

W_PIECE = 1024
N_IN, N_UQ, N_OUT, N_UP, N_DOWN = 20, 2, KD, 2 * FH, FH
PIECES = N_IN + N_UQ + N_OUT + 2 * (N_UP + N_DOWN)
P_UQ = N_IN
P_OUT = P_UQ + N_UQ
P_UP = [P_OUT + N_OUT, P_OUT + N_OUT + N_UP + N_DOWN]
P_DOWN = [p + N_UP for p in P_UP]
RAW, SPL = 2, 3

T_HG = 4
T_UQ = T_HG + 4 * HG
T_UK = T_UQ + HM
T_OUT = T_UK + HM // 2
T_UP = [T_OUT + KD, T_OUT + KD + 2 * FH + KD]
T_DOWN = [t + 2 * FH for t in T_UP]
TILES = T_DOWN[1] + KD

C_MIXPRE, C_MIXPOST, C_FFNPRE, C_FFNPOST = 0, 8, 16, 24
C_QN, C_KVN, C_HGN, C_LB0, C_LB1, C_FIN, C_CB, C_CW = 32, 34, 35, 36, 40, 44, 52, 74
NCOL = C_CW + 3 * KF



def build(nc, a):
    ctx = ExitStack()
    sems = {}

    def sb(stack, name, shape, dt=F32):
        return stack.enter_context(nc.sbuf_tensor(name, shape, dt))

    with ctx:
        def S(name):
            if name not in sems:
                sems[name] = ctx.enter_context(nc.semaphore(name))
            return sems[name]

        X = sb(ctx, "X", [P, KD, T])
        Y = sb(ctx, "Y", [P, KD, T])
        Hh = sb(ctx, "Hh", [P, KD, T], F32R)
        Hl = sb(ctx, "Hl", [P, KD, T], F32R)
        wraw = sb(ctx, "wraw", [P, RAW, W_PIECE])
        whi = sb(ctx, "whi", [P, SPL, W_PIECE], F32R)
        wlo = sb(ctx, "wlo", [P, SPL, W_PIECE], F32R)
        ones = sb(ctx, "ones", [P, P])
        ident = sb(ctx, "ident", [P, P])
        masks = sb(ctx, "masks", [P, len(LEVELS), P], U8)
        reset = sb(ctx, "reset", [P, T])
        rope = sb(ctx, "rope", [P, T])
        cols = sb(ctx, "cols", [P, DEPTH, NCOL])
        ind = sb(ctx, "ind", [P, DB])
        lbs = sb(ctx, "lbs", [P, DEPTH, 2, HG])
        zero = sb(ctx, "zero", [P, 1])
        eps = sb(ctx, "eps", [P, 1])
        mask_f = Y[:, 0:2, 0:P * len(LEVELS) // 2]
        acc = sb(ctx, "acc", [P, T])
        sq = sb(ctx, "sq", [P, 2, T])
        R = sb(ctx, "R", [P, T])
        tmp = sb(ctx, "tmp", [P, 2, T])

        mix = ExitStack()
        kvn = sb(mix, "kvn", [P, T])
        kpe = sb(mix, "kpe", [P, T])
        ob = sb(mix, "ob", [P, HG, T])
        wA = sb(mix, "wA", [P, 1024])
        hg = ExitStack()
        cqh = sb(hg, "cqh", [P, 2, T], F32R)
        cql = sb(hg, "cql", [P, 2, T], F32R)
        gate = sb(hg, "gate", [P, 2, T])
        DE = sb(hg, "DE", [P, 2, T])
        Z = sb(hg, "Z", [P, 2, T])
        Am = sb(hg, "Am", [P, 6 * P])
        vtok = sb(hg, "vtok", [P, 6 * P])
        ktok = sb(hg, "ktok", [P, 6 * P])
        st = sb(hg, "st", [P, 5, P])
        S0 = sb(hg, "S0", [P, 2, DB * P])
        hg.close()
        att = ExitStack()
        ckT = sb(att, "ckT", [P, 2, PAST])
        cpe = sb(att, "cpe", [P, 2, PAST])
        pr = ExitStack()
        KT = sb(pr, "KT", [P, HM, PT])
        vt = sb(pr, "vt", [P, 5, HM * VH])
        Pp = sb(pr, "Pp", [P, 3, PT])
        Pt = sq
        mx = sb(pr, "mx", [P, 3, 4])
        pr.close()
        sa = ExitStack()
        ctok = sb(sa, "ctok", [P, 2, PAST])
        Ps = sb(sa, "Ps", [P, 2, PAST + DT])
        Pts = sb(sa, "Pts", [P, 9 * P])
        ntok = sb(sa, "ntok", [DT, DB * P])
        ql = sb(sa, "ql", [P, DB, HM * DT])
        OL = sb(sa, "OL", [P, HM, SAMP])
        ms = sb(sa, "ms", [P, 2, 8])
        qpe = tmp[64:96, :, :].rearrange("p a n -> p (a n)")[:, 0:DB * HM * DT]
        sa.close()
        att.close()
        mix.close()
        ff = ExitStack()
        gh = sb(ff, "gh", [P, FH, T], F32R)
        gl = sb(ff, "gl", [P, FH, T], F32R)
        ax = sb(ff, "ax", [P, 2, EXT])
        cc = sb(ff, "cc", [P, EXT])
        cst = sb(ff, "cst", [P, KF * DB * 2])
        cout = sb(ff, "cout", [P, KF, 2 + DB * 2])
        ff.close()

        def pb(name):
            return ctx.enter_context(nc.psum_tensor(name, [P, 1024], F32))

        G = [pb("G0"), pb("G1")]
        WA, WB = pb("WA"), pb("WB")

        def halves(ps, n=HALF, p0=0, p1=P):
            return ps[p0:p1, :].rearrange("p (a n) -> p a n", a=2)[:, :, 0:n]

        def two(ap, n=HALF):
            return ap.rearrange("p (a n) -> p a n", n=n)

        def samples(ap, w=DT):
            return ap.rearrange("p (b t) -> p b t", t=w)

        NORM_SQ = [KD, 2, 1, 1, 1, 1, 1, KD, KD, KD]
        N_NORM = len(NORM_SQ)
        N_MIXPRE, N_CQ, N_CKV, N_HG, N_MIXPOST, N_FFNPRE, N_FFNPOST = 0, 1, 2, 3, 7, 8, 9

        def squares(n):
            l, i = divmod(n, N_NORM)
            return l * sum(NORM_SQ) + sum(NORM_SQ[:i])

        LV = len(LEVELS)
        SPLITS = 2 * KD + 2

        def slot_use(tt):
            return tt // 2 + 1

        def piece_end(g):
            l, p = divmod(g, PIECES)
            if p < N_IN:
                return "tile", l * TILES + p + 1
            if p < P_OUT:
                return "tile", l * TILES + T_UQ + 4 * (p - P_UQ) + 4
            if p < P_UP[0]:
                return "tile", l * TILES + T_OUT + p - P_OUT + 1
            for hf in range(2):
                if P_UP[hf] <= p < P_DOWN[hf]:
                    return "tile", l * TILES + T_UP[hf] + p - P_UP[hf] + 1
                if P_DOWN[hf] <= p < P_DOWN[hf] + N_DOWN:
                    i = p - P_DOWN[hf]
                    if i == N_DOWN - 1:
                        return "tile", l * TILES + T_DOWN[hf] + KD
                    return "w_mid", (2 * l + hf) * (N_DOWN - 1) + i + 1

        UNITS = [(h, j) for h in range(HM) for j in range(-1, 4)]
        NU = len(UNITS)

        def unit_q(j):
            return (0, META) if j < 0 else (META + P * j, P)

        def sub_halves(t, m):
            v = t[:, 0:T] if m <= 8 else t[:, META:PT]
            v = v.rearrange("p (b m) -> p b m", m=2 * m)
            nb = v.shape[1]
            return v[:, :, 0:m], v[:, :, m:2 * m], v[:, :, m - 1:m].broadcast_to([P, nb, m])

        def span(t, m):
            return t[:, 0:T] if m <= 8 else t[:, META:PT]

        def hq(h): return Y[:, 4 * (h % 2) + 0, :]
        def hk(h): return Y[:, 4 * (h % 2) + 1, :]
        def hG(h): return Y[:, 4 * (h % 2) + 2, :]
        def hv(h): return Y[:, 4 * (h % 2) + 3, :]

        N_CONST = 7
        block = ctx.enter_context(nc.Block())

        @block.sync
        def _(sp):
            for g in range(DEPTH * PIECES):
                if g >= RAW:
                    sp.wait_ge(S("w_split"), g - RAW + 1)
                sp.dma_start(wraw[:, g % RAW, :], a["wstream"][g // PIECES, g % PIECES])\
                    .then_inc(S(f"w_in{g % RAW}"), 16)

        @block.gpsimd
        def _(pool):
            pool.memset(zero[:, :], 0.0).then_inc(S("zero"), 1)
            pool.wait_ge(S("zero"), 1)
            zb = zero[:, 0:1].broadcast_to([P, W_PIECE])
            for g in range(DEPTH * PIECES):
                pool.wait_ge(S(f"w_in{g % RAW}"), 16 * (g // RAW + 1))
                if g >= SPL:
                    pool.wait_ge(S(piece_end(g - SPL)[0]), piece_end(g - SPL)[1])
                raw, hi, lo = wraw[:, g % RAW, :], whi[:, g % SPL, :], wlo[:, g % SPL, :]
                pool.tensor_tensor(hi, raw, zb, ALU.add).then_inc(S("w_hi"), 1)
                pool.wait_ge(S("w_hi"), g + 1)
                pool.tensor_tensor(lo, raw, hi, ALU.subtract).then_inc(S("w_split"), 1)

        @block.tensor
        def _(pe):
            pe.wait_ge(S("const"), 16 * N_CONST)

            def mm(out, lhsT, rhs, start=True, stop=True):
                return pe.matmul(out, lhsT, rhs, start=start, stop=stop, skip_group_check=True)

            def tr(out, in_):
                n = in_.shape[0]
                return pe.transpose(out, in_, ident[0:n, 0:n])

            def norm_sum(n, ps):
                pe.wait_ge(S("sq_added"), squares(n + 1))
                if n:
                    pe.wait_ge(S("rstd"), n)
                for x in range(2):
                    m = mm(ps[:, 512 * x:512 * x + HALF], ones[:, :], acc[:, HALF * x:HALF * x + HALF])
                m.then_inc(S("ssum"), 1)

            def tile_free(tt):
                if tt >= 2:
                    pe.wait_ge(S(f"evac{tt % 2}"), slot_use(tt) - 1)

            def tile(tt, chunks, rh, rl, ready=None):
                tile_free(tt)
                for i, (g, c) in enumerate(chunks):
                    pe.wait_ge(S("w_split"), g + 1)
                    if ready is not None:
                        ready(i)
                    wh, wl = whi[:, g % SPL, c:c + P], wlo[:, g % SPL, c:c + P]
                    last = i == len(chunks) - 1
                    for x in range(2):
                        o = G[tt % 2][:, 512 * x:512 * x + HALF]
                        cs = slice(HALF * x, HALF * x + HALF)
                        mm(o, wl, rh[:, i, cs], i == 0, False)
                        mm(o, wh, rh[:, i, cs], False, False)
                        m = mm(o, wh, rl[:, i, cs], False, last)
                    if c + P == W_PIECE and not last:
                        m.then_inc(S("w_mid"), 1)
                m.then_inc(S("tile"), 1)

            def head_tile(l, h, i):
                g = l * PIECES + T_HG + 4 * h + i
                tile(l * TILES + T_HG + 4 * h + i, [(g, k * P) for k in range(KD)], Hh, Hl)

            def level(l, h, lv):
                n = (l * HG + h) * LV + lv
                m = LEVELS[lv]
                if m:
                    pe.wait_ge(S("Z"), (l * HG + h) * (LV - 1) + lv + 1)
                    zk = zq = Z[:, lv % 2, :]
                else:
                    zk, zq = hk(h), hq(h)
                if n >= 2:
                    pe.wait_ge(S("A_taken"), n - 1)
                if lv < 2 and (l or h):
                    pe.wait_ge(S("o_taken"), l * HG + h)
                bank = 512 * (lv % 2)
                for j in range(4):
                    cs = slice(META + P * j, META + P * j + P)
                    e = mm(WA[:, bank + P * j:bank + P * j + P], zk[:, cs], zq[:, cs])
                if m <= 8:
                    mm(WB[:, bank:bank + P], zk[:, PT:T], zq[:, PT:T])
                    e = mm(WB[0:META, bank + P:bank + P + META], zk[:, 0:META], zq[:, 0:META])
                e.then_inc(S("A"), 1)

            def to_tokens(ps, src):
                for j in range(4):
                    tr(ps[:, P * j:P * j + P], src[:, META + P * j:META + P * j + P])
                tr(ps[:, 512:512 + P], src[:, PT:T])
                return tr(ps[0:META, 640:640 + P], src[:, 0:META])

            def head_rest(l, h):
                n = l * HG + h
                tv = l * TILES + T_HG + 4 * h + 2
                pe.wait_ge(S(f"evac{tv % 2}"), slot_use(tv))
                pe.wait_ge(S("A_taken"), (n + 1) * LV)
                to_tokens(WA, hv(h)).then_inc(S("v_turned"), 1)
                pe.wait_ge(S("kG"), n + 1)
                to_tokens(WB, hk(h)).then_inc(S("k_turned"), 1)
                pe.wait_ge(S("tok"), 2 * (n + 1))
                for j in range(4):
                    mm(WA[:, P * j:P * j + P], ktok[:, P * j:P * j + P], vtok[:, P * j:P * j + P])
                mm(WA[:, 512:512 + P], ktok[0:META, 640:640 + P], vtok[0:META, 640:640 + P]).then_inc(S("dS"), 1)
                pe.wait_ge(S("v_apart"), n + 1)
                for x in range(2):
                    e = mm(WB[:, 512 * x:512 * x + 512], ktok[:, 512:512 + P],
                           Z[:, :, :].rearrange("p a n -> p (a n)")[:, 512 * x:512 * x + 512])
                e.then_inc(S("dS_sample"), 1)
                pe.wait_ge(S("state"), 5 * (n + 1))
                pe.wait_ge(S("qG"), n + 1)
                pe.wait_ge(S(f"s0_in{h % 2}"), 16 * (2 * l + h // 2 + 1))
                for j in range(4):
                    o = WA[:, P * j:P * j + P]
                    mm(o, vtok[:, P * j:P * j + P], Am[:, P * j:P * j + P], True, False)
                    mm(o, st[:, j, :], hq(h)[:, META + P * j:META + P * j + P], False, True)
                mm(WA[:, 512:512 + META], vtok[0:META, 640:640 + P], Am[0:META, 640:640 + META])
                mm(WA[:, 640:640 + SAMP], vtok[:, 512:512 + P], Am[:, 512:512 + P], True, False)
                for b in range(DB):
                    e = mm(WA[:, 640 + DT * b:640 + DT * b + DT], S0[:, h % 2, P * b:P * b + P],
                           hq(h)[:, PT + DT * b:PT + DT * b + DT], False, b == DB - 1)
                e.then_inc(S("o"), 1)
                pe.wait_ge(S("s0_new"), n + 1)
                norm_sum(l * N_NORM + N_HG + h, WB)

            def prompt_scores(l, u):
                h, j = UNITS[u]
                q0, nq = unit_q(j)
                n = META + P * (j + 1)
                if u >= 2 or l:
                    pe.wait_ge(S("exp"), l * NU + u - 1 if u >= 2 else l * NU)
                ps = (WA, G[0])[u % 2]
                for c in range(0, n, 512):
                    e = mm(ps[0:nq, c:min(n, c + 512)], Y[0:100, h, q0:q0 + nq], KT[0:100, h, c:min(n, c + 512)])
                e.then_inc(S("scores"), 1)

            def prompt_turn(l, u):
                h, j = UNITS[u]
                q0, nq = unit_q(j)
                pe.wait_ge(S("probs"), l * NU + u + 1)
                if u >= 2:
                    pe.wait_ge(S("oa_taken"), l * NU + u - 1)
                ps, pp = (WB, G[1])[u % 2], Pp[:, u % 3, :]
                for c in range(j + 1):
                    tr(ps[:, P * c:P * c + nq], pp[0:nq, META + P * c:META + P * c + P])
                tr(ps[0:META, 512:512 + nq], pp[0:nq, 0:META]).then_inc(S("turned"), 1)

            def prompt_out(l, u):
                h, j = UNITS[u]
                q0, nq = unit_q(j)
                pe.wait_ge(S("Pt"), l * NU + u + 1)
                o = (WB, G[1])[u % 2][0:VH, 640:640 + nq]
                e = mm(o, vt[0:META, 4, VH * h:VH * h + VH], Pt[0:META, u % 2, 512:512 + nq], True, j < 0)
                for c in range(j + 1):
                    e = mm(o, vt[:, c, VH * h:VH * h + VH], Pt[:, u % 2, P * c:P * c + nq], False, c == j)
                e.then_inc(S("oa"), 1)

            def sample_scores(l, b):
                pe.wait_ge(S(f"ck_in{b % 2}"), 32 * (l * DB // 2 + b // 2 + 1))
                if b >= 2:
                    pe.wait_ge(S("s_exp"), l * DB + b - 1)
                ps = (WA, G[0])[b % 2]
                lat, pe_q = ql[:, b, :], qpe[:, P * b:P * b + P]
                for c in range(0, PAST, 512):
                    mm(ps[:, c:c + 512], lat, ckT[:, b % 2, c:c + 512], True, False)
                    mm(ps[:, c:c + 512], pe_q, cpe[64:96, b % 2, c:c + 512], False, True)
                new = WB[:, 512 + DT * (b % 2):512 + DT * (b % 2) + DT]
                cs = slice(PT + DT * b, PT + DT * b + DT)
                if b:
                    pe.wait_ge(S("s_exp"), l * DB + b)
                mm(new, lat, kvn[:, cs], True, False)
                mm(new, pe_q, kpe[64:96, cs], False, True).then_inc(S("s_scores"), 1)

            def sample_turn(l, b):
                pe.wait_ge(S("s_probs"), l * DB + b + 1)
                for x in range(2):
                    if b:
                        pe.wait_ge(S("s_Pt"), 3 * (l * DB + b - 1) + x + 1)
                    for c in range(4):
                        e = tr(G[1][:, 512 * x + P * c:512 * x + P * c + P],
                               Ps[:, b % 2, P * (4 * x + c):P * (4 * x + c) + P])
                    e.then_inc(S("s_turned"), 1)
                if b:
                    pe.wait_ge(S("s_Pt"), 3 * (l * DB + b))
                    pe.wait_ge(S("ol_taken"), l * DB + b)
                tr(WB[0:DT, 0:P], Ps[:, b % 2, PAST:PAST + DT]).then_inc(S("s_turned"), 1)

            def sample_out(l, b):
                pe.wait_ge(S("s_Pt"), 3 * (l * DB + b + 1))
                pe.wait_ge(S(f"ct_in{b % 2}"), 16 * (l * DB // 2 + b // 2 + 1))
                o = WB[:, P:2 * P]
                if b:
                    pe.wait_ge(S("ol_taken"), l * DB + b)
                mm(o, ntok[:, P * b:P * b + P], Pts[0:DT, 8 * P:9 * P], True, False)
                for c in range(PC):
                    e = mm(o, ctok[:, b % 2, P * c:P * c + P], Pts[:, P * c:P * c + P], False, c == PC - 1)
                e.then_inc(S("s_oa"), 1)

            for l in range(DEPTH):
                g0, t0, n0 = l * PIECES, l * TILES, l * N_NORM
                norm_sum(n0 + N_MIXPRE, WA)
                for i in range(T_HG):
                    tile(t0 + i, [(g0 + i, k * P) for k in range(KD)], Hh, Hl,
                         lambda k: pe.wait_ge(S("hl"), l * SPLITS + k + 1))
                norm_sum(n0 + N_CQ, WA)
                norm_sum(n0 + N_CKV, WA)
                for i in range(4):
                    head_tile(l, 0, i)
                pe.wait_ge(S("rstd"), n0 + N_CKV + 1)
                for h in range(HG):
                    for lv in range(LV):
                        level(l, h, lv)
                        if h + 1 < HG and lv in (1, 4):
                            head_tile(l, h + 1, lv // 4)
                    head_rest(l, h)
                    if h + 1 < HG:
                        head_tile(l, h + 1, 2)
                        head_tile(l, h + 1, 3)
                pe.wait_ge(S("hl"), l * SPLITS + KD + 2)
                for h in range(HM):
                    g = g0 + P_UQ + h // 4
                    tile(t0 + T_UQ + h, [(g, 256 * (h % 4) + k * P) for k in range(2)], cqh, cql)
                pe.wait_ge(S("wA_in"), 16 * (l + 1))
                pe.wait_ge(S("kvn"), l + 1)
                for p in range(HM // 2):
                    tt = t0 + T_UK + p
                    tile_free(tt)
                    for x in range(2):
                        e = mm(G[tt % 2][:, 512 * x:512 * x + PT // 2], wA[:, P * p:P * p + P],
                               kvn[:, PT // 2 * x:PT // 2 * x + PT // 2])
                    e.then_inc(S("tile"), 1)
                pe.wait_ge(S("ob"), l * HG + HG)
                for i in range(5):
                    cs = slice(META + P * i, META + P * i + P) if i < 4 else slice(0, META)
                    if i == 4:
                        pe.wait_ge(S("vt"), 5 * l + 1)
                    ps = (WA, WA, WB, WB, WA)[i]
                    c = (0, 512, 0, 512, 0)[i]
                    mm(ps[0:P if i < 4 else META, c:c + 512], kvn[:, cs], wA[:, 512:1024]).then_inc(S("values"), 1)
                pe.wait_ge(S("vt"), 5 * (l + 1))
                pe.wait_ge(S("kt"), l + 1)
                pe.wait_ge(S("maskrows"), 32 * (l + 1))
                for tt in (t0 + T_OUT, t0 + T_OUT + 1):
                    tile_free(tt)
                for u in range(NU + 3):
                    if u < NU:
                        prompt_scores(l, u)
                    if 2 <= u < NU + 2:
                        prompt_turn(l, u - 2)
                    if u >= 3:
                        prompt_out(l, u - 3)
                pe.wait_ge(S("oa_taken"), (l + 1) * NU)
                pe.wait_ge(S("wB_in"), 16 * (l + 1))
                for h in range(HM):
                    e = mm(WA[:, P * h:P * h + P], cpe[0:NOPE, 0, P * h:P * h + P], Y[0:NOPE, h, PT:T])
                e.then_inc(S("ql_ps"), 1)
                for b in range(DB):
                    e = tr(WB[0:DT, P * b:P * b + P], kvn[:, PT + DT * b:PT + DT * b + DT])
                e.then_inc(S("ql_ps"), 1)
                pe.wait_ge(S("ql"), 3 * (l + 1))
                for b in range(DB + 2):
                    if b < DB:
                        sample_scores(l, b)
                    if b >= 2:
                        sample_out(l, b - 2)
                    if 1 <= b < DB + 1:
                        sample_turn(l, b - 1)
                pe.wait_ge(S("ol_taken"), (l + 1) * DB)
                for h in range(HM):
                    e = mm(WA[0:VH, P * h:P * h + P], wA[:, 512 + VH * h:512 + VH * h + VH], OL[:, h, :])
                e.then_inc(S("oas"), 1)
                pe.wait_ge(S("ob_split"), HG * (l + 1))
                pe.wait_ge(S("oas_taken"), l + 1)
                for n in range(KD):
                    tile(t0 + T_OUT + n, [(g0 + P_OUT + n, k * P) for k in range(KD)], Hh, Hl)
                norm_sum(n0 + N_MIXPOST, WA)
                norm_sum(n0 + N_FFNPRE, WA)
                for hf in range(2):
                    for i in range(2 * FH):
                        tile(t0 + T_UP[hf] + i, [(g0 + P_UP[hf] + i, k * P) for k in range(KD)], Hh, Hl,
                             (lambda k: pe.wait_ge(S("hl"), l * SPLITS + KD + 2 + k + 1)) if hf == i == 0 else None)
                    for n in range(KD):
                        tile(t0 + T_DOWN[hf] + n,
                             [(g0 + P_DOWN[hf] + (FH * n + k) // 8, (FH * n + k) % 8 * P) for k in range(FH)], gh, gl,
                             (lambda k: pe.wait_ge(S("gl"), l * KF + hf * FH + k + 1)) if n == 0 else None)
                norm_sum(n0 + N_FFNPOST, WA)
            norm_sum(DEPTH * N_NORM, WA)

        @block.scalar
        def _(act):
            count, last = {}, []

            def did(ins, name, at=None):
                count[name] = at or count.get(name, 0) + 1
                last[:] = [name]
                ins.then_inc(S(name), 1)

            def prev():
                if last:
                    act.wait_ge(S(last[0]), count[last[0]])

            def f(*args, **kw):
                prev()
                return act.activation(*args, **kw)

            def step(ins):
                did(ins, "act")

            for t_, name in ((ones, "ones"), (ident, "ident"), (mask_f, "masks"), (reset, "reset"),
                             (rope, "rope"), (cols, "cols"), (ind, "ind")):
                act.dma_start(t_[:, :] if len(t_.shape) == 2 else t_[:, :, :], a[name]).then_inc(S("const"), 16)
            for k in range(KD):
                act.dma_start(X[:, k, :], a["xT"][k]).then_inc(S("x_in"), 16)
            act.wait_ge(S("lbd"), 1)
            did(f(lbs[:, 1, 0, :], lbs[:, 0, 0, :], ACT.Sigmoid), "lb_sig")
            did(f(lbs[:, 1, 1, :], lbs[:, 0, 0, :], ACT.Sigmoid, scale=-1.0), "lb_sig")

            def exp_table():
                act.preload_act_table_set("natural_log_exp_and_others")

            def square_x(n, k, src):
                c = squares(n) + k
                if c >= 2:
                    act.wait_ge(S("sq_added"), c - 1)
                did(f(sq[:, c % 2, :], src, ACT.Square), "sq")

            def rstd(n, ps, width):
                act.wait_ge(S("ssum"), n + 1)
                if n:
                    act.wait_ge(S("R_used"), n)
                step(f(two(R[:, :]), halves(ps), ACT.Ln, scale=1.0 / width, bias=eps[:, 0:1]))
                did(f(R[:, :], R[:, :], ACT.Exp, scale=-0.5), "rstd")

            def hi_part(n, dst, src):
                act.wait_ge(S("hf"), n + 1)
                did(f(dst, src, ACT.Copy), "hh")

            def take(tt, dst, src=None, func=ACT.Copy, **kw):
                act.wait_ge(S("tile"), tt + 1)
                return f(dst, halves(G[tt % 2]) if src is None else src, func, **kw)

            def evac(tt, ins):
                did(ins, f"evac{tt % 2}", slot_use(tt))

            for l in range(DEPTH):
                t0, n0 = l * TILES, l * N_NORM
                exp_table()
                for k in range(KD):
                    act.wait_ge(S("x_in"), 16 * KD) if not l else act.wait_ge(S("x"), (2 * l - 1) * KD + k + 1)
                    square_x(n0 + N_MIXPRE, k, X[:, k, :])
                rstd(n0 + N_MIXPRE, WA, D)
                act.dma_start(wA[:, :], a["wA"][l]).then_inc(S("wA_in"), 16)
                for i in range(2):
                    act.dma_start(S0[:, i, :], a["s0"][l, i]).then_inc(S(f"s0_in{i}"), 16)
                for k in range(KD):
                    hi_part(l * SPLITS + k, Hh[:, k, :], tmp[:, k % 2, :])
                for i, dst in enumerate((DE[:, 0, :], DE[:, 1, :], kvn[:, :])):
                    did(take(t0 + i, two(dst)), "c_raw")
                    n, k = (n0 + N_CQ, i) if i < 2 else (n0 + N_CKV, 0)
                    c = squares(n) + k
                    act.wait_ge(S("sq_added"), c - 1)
                    evac_sq = f(two(sq[:, c % 2, :]), halves(G[(t0 + i) % 2]), ACT.Square)
                    did(evac_sq, "sq")
                rstd(n0 + N_CQ, WA, QL)
                for k in range(2):
                    hi_part(l * SPLITS + KD + k, cqh[:, k, :], tmp[:, k, :])
                rstd(n0 + N_CKV, WA, KL)
                act.wait_ge(S("kvn"), l + 1)
                act.dma_start(a["o_kv"][l], kvn[:, :]).then_inc(S("out"), 16)
                act.wait_ge(S("kpe"), l + 1)
                act.dma_start(a["o_kpe"][l], kpe[64:96, :]).then_inc(S("out"), 16)
                for h in range(HG):
                    n, th = l * HG + h, t0 + T_HG + 4 * h
                    if h == 0:
                        act.wait_ge(S("hl"), l * SPLITS + KD + 2)
                    else:
                        act.wait_ge(S("ob"), n)
                    did(take(th, two(DE[:, 0, :]), func=ACT.Sigmoid), "act")
                    evac(th, take(th, two(hk(h)), func=ACT.Sigmoid, scale=-1.0))
                    did(take(th + 1, two(hq(h)), func=ACT.Sigmoid), "sig")
                    evac(th + 2, take(th + 2, two(hv(h))))
                    did(take(th + 3, two(gate[:, h % 2, :]), func=ACT.Sigmoid), "sig")
                    exp_table()
                    did(f(DE[:, 0, :], DE[:, 0, :], ACT.Ln, scale=lbs[:, l, 1, h:h + 1], bias=lbs[:, l, 0, h:h + 1]), "gl_")
                    for lv in range(LV - 1):
                        act.wait_ge(S("D"), n * LV + lv + 1)
                        d = span(DE[:, lv % 2, :], LEVELS[lv])
                        did(f(d, d, ACT.Exp), "E")
                    act.wait_ge(S("Z"), n * (LV - 1) + LV - 2)
                    did(f(DE[:, 1, :], hG(h), ACT.Exp), "E")
                    act.wait_ge(S("D"), n * LV + LV)
                    did(f(DE[:, 0, :], DE[:, 0, :], ACT.Exp), "E")
                    for ps, tok, name in ((WA, vtok, "v_turned"), (WB, ktok, "k_turned")):
                        act.wait_ge(S(name), n + 1)
                        did(f(tok[:, 0:640], ps[:, 0:640], ACT.Copy), "act")
                        did(f(tok[0:META, 640:768], ps[0:META, 640:768], ACT.Copy), "tok")
                    act.wait_ge(S("o"), n + 1)
                    act.dma_start(a["o_pst"][l, h], st[:, 4, :]).then_inc(S("pst_out"), 16)
                    c = squares(n0 + N_HG + h)
                    act.wait_ge(S("sq_added"), c - 1)
                    did(f(sq[:, c % 2, META:PT], WA[:, 0:512], ACT.Square), "act")
                    did(f(sq[:, c % 2, 0:META], WA[:, 512:512 + META], ACT.Square), "act")
                    did(f(sq[:, c % 2, PT:T], WA[:, 640:640 + SAMP], ACT.Square), "sq")
                    rstd(n0 + N_HG + h, WB, P)
                    act.wait_ge(S("s0_new"), n + 1)
                    act.dma_start(a["o_sst"][l, h], S0[:, h % 2, :]).then_inc(S(f"sst_out{h % 2}"), 16)
                    if 1 <= h < HG - 1:
                        act.wait_ge(S(f"sst_out{(h - 1) % 2}"), 16 * (2 * l + (h - 1) // 2 + 1))
                        act.dma_start(S0[:, (h - 1) % 2, :], a["s0"][l, h + 1]).then_inc(S(f"s0_in{(h - 1) % 2}"), 16)
                for h in range(HG):
                    act.wait_ge(S("ob"), l * HG + h + 1)
                    did(f(Hh[:, 4 + h, :], ob[:, h, :], ACT.Copy), "obh")
                act.dma_start(Y[96:100, :, :], a["qrows"]).then_inc(S("maskrows"), 16)
                for h in range(HM):
                    tt = t0 + T_UQ + h
                    act.wait_ge(S("tile"), tt + 1)
                    did(f(two(Y[0:64, h, :]), halves(G[tt % 2], p1=64), ACT.Copy), "q_nope")
                act.wait_ge(S("sst_out0"), 16 * 2 * (l + 1))
                act.wait_ge(S("sst_out1"), 16 * 2 * (l + 1))
                act.wait_ge(S("pst_out"), 16 * HG * (l + 1))
                act.dma_start(KT[96:100, :, :], a["krows"]).then_inc(S("maskrows"), 16)
                for p in range(HM // 2):
                    tt = t0 + T_UK + p
                    act.wait_ge(S("tile"), tt + 1)
                    did(f(two(KT[0:64, 2 * p, :], PT // 2), halves(G[tt % 2], PT // 2, 0, 64), ACT.Copy), "act")
                    evac(tt, f(two(KT[0:64, 2 * p + 1, :], PT // 2), halves(G[tt % 2], PT // 2, 64, P), ACT.Copy))
                did(f(KT[64:96, :, :], kpe[64:96, 0:PT].rearrange("p (a n) -> p a n", a=1).broadcast_to([32, HM, PT]),
                  ACT.Copy), "kt")
                for b in range(2):
                    act.dma_start(ckT[:, b, :], a["ckT"][l, b]).then_inc(S(f"ck_in{b}"), 16)
                    act.dma_start(cpe[64:96, b, :], a["cpe"][l, b]).then_inc(S(f"ck_in{b}"), 16)
                act.dma_start(cpe[0:NOPE, 0, :], a["wB"][l]).then_inc(S("wB_in"), 16)
                for u in range(NU + 2):
                    if u < NU:
                        h, j = UNITS[u]
                        nq, n = unit_q(j)[1], META + P * (j + 1)
                        act.wait_ge(S("max"), l * NU + u + 1)
                        if u >= 3:
                            act.wait_ge(S("turned"), l * NU + u - 2)
                        did(f(Pp[0:nq, u % 3, 0:n], (WA, G[0])[u % 2][0:nq, 0:n], ACT.Exp, scale=SCALE,
                          bias=mx[0:nq, u % 3, 1:2], accum_out=mx[0:nq, u % 3, 2:3]), "exp")
                    if u >= 2:
                        v = u - 2
                        h, j = UNITS[v]
                        nq = unit_q(j)[1]
                        act.wait_ge(S("turned"), l * NU + v + 1)
                        if v >= 2:
                            act.wait_ge(S("oa"), l * NU + v - 1)
                        ps = (WB, G[1])[v % 2]
                        if j >= 0:
                            step(f(Pt[:, v % 2, 0:P * (j + 1)], ps[:, 0:P * (j + 1)], ACT.Copy))
                        did(f(Pt[0:META, v % 2, 512:512 + nq], ps[0:META, 512:512 + nq], ACT.Copy), "Pt")
                act.wait_ge(S("oa"), (l + 1) * NU)
                for b in range(2):
                    act.dma_start(ctok[:, b, :], a["ctok"][l, b]).then_inc(S(f"ct_in{b}"), 16)
                act.wait_ge(S("ql_ps"), 2 * l + 1)
                did(f(ql[:, :, :].rearrange("p b (h t) -> p h b t", t=DT),
                  WA[:, :].rearrange("p (h b t) -> p h b t", h=HM, t=DT), ACT.Copy), "ql")
                did(f(qpe.rearrange("p (b h t) -> p h b t", h=HM, t=DT),
                  Y[64:96, :, PT:T].rearrange("p h (b t) -> p h b t", t=DT), ACT.Copy), "ql")
                act.wait_ge(S("ql_ps"), 2 * l + 2)
                act.wait_ge(S("ql"), 3 * l + 2)
                did(f(ntok[:, :], WB[0:DT, :], ACT.Copy), "ql")
                for b in range(DB + 1):
                    if b < DB:
                        sl = b % 2
                        act.wait_ge(S("s_max"), l * DB + b + 1)
                        if b >= 2:
                            act.wait_ge(S("s_turned"), 3 * (l * DB + b - 1))
                        step(f(Ps[:, sl, 0:PAST], (WA, G[0])[sl][:, :], ACT.Exp, scale=SCALE,
                               bias=ms[:, sl, 3:4], accum_out=ms[:, sl, 4:5]))
                        did(f(Ps[:, sl, PAST:PAST + DT], WB[:, 512 + DT * sl:512 + DT * sl + DT], ACT.Exp, scale=SCALE,
                          bias=ms[:, sl, 3:4], accum_out=ms[:, sl, 5:6]), "s_exp")
                        if b + 2 < DB:
                            act.dma_start(ckT[:, sl, :], a["ckT"][l, b + 2]).then_inc(S(f"ck_in{sl}"), 16)
                            act.dma_start(cpe[64:96, sl, :], a["cpe"][l, b + 2]).then_inc(S(f"ck_in{sl}"), 16)
                    if b >= 1:
                        v = b - 1
                        for x in range(2):
                            act.wait_ge(S("s_turned"), 3 * (l * DB + v) + x + 1)
                            if v and not x:
                                act.wait_ge(S("s_oa"), l * DB + v)
                                if v + 1 < DB:
                                    act.dma_start(ctok[:, (v - 1) % 2, :], a["ctok"][l, v + 1])\
                                        .then_inc(S(f"ct_in{(v - 1) % 2}"), 16)
                            did(f(Pts[:, 512 * x:512 * x + 512], G[1][:, 512 * x:512 * x + 512], ACT.Copy), "s_Pt")
                        act.wait_ge(S("s_turned"), 3 * (l * DB + v + 1))
                        act.wait_ge(S("s_Pt"), 3 * (l * DB + v) + 2)
                        did(f(Pts[0:DT, 8 * P:9 * P], WB[0:DT, 0:P], ACT.Copy), "s_Pt")
                act.wait_ge(S("out"), 32 * (l + 1))
                for n in range(KD):
                    tt = t0 + T_OUT + n
                    did(take(tt, two(Y[:, n, :])), "y")
                    c = squares(n0 + N_MIXPOST) + n
                    act.wait_ge(S("sq_added"), c - 1)
                    did(f(two(sq[:, c % 2, :]), halves(G[tt % 2]), ACT.Square), "sq")
                rstd(n0 + N_MIXPOST, WA, D)
                act.wait_ge(S("x"), 2 * l * KD + 1)
                act.dma_start(cst[:, :], a["cst"][l]).then_inc(S("cst_in"), 16)
                for k in range(KD):
                    act.wait_ge(S("x"), 2 * l * KD + k + 1)
                    square_x(n0 + N_FFNPRE, k, X[:, k, :])
                rstd(n0 + N_FFNPRE, WA, D)
                for k in range(KD):
                    hi_part(l * SPLITS + KD + 2 + k, Hh[:, k, :], tmp[:, k % 2, :])
                for hf in range(2):
                    for i in range(FH + 1):
                        ff_ = l * KF + hf * FH + i
                        if i < FH:
                            tt = t0 + T_UP[hf] + 2 * i
                            act.wait_ge(S("tile"), tt + 1)
                            if ff_ >= 2:
                                act.wait_ge(S("conv"), ff_ - 1)
                            s_, ps = ax[:, ff_ % 2, :], G[tt % 2]
                            did(f(s_[:, 2:2 + HALF], ps[:, 0:HALF], ACT.Copy), "act")
                            did(f(s_[:, 2 + HALF:2 + PT], ps[:, 512:512 + PT - HALF], ACT.Copy), "act")
                            evac(tt, f(samples(s_[:, 2 + PT:EXT], DT + 2)[:, :, 2:],
                                       samples(ps[:, 512 + PT - HALF:512 + HALF]), ACT.Copy))
                        if i >= 1:
                            act.wait_ge(S("gv"), ff_)
                            if hf and i == 1:
                                act.wait_ge(S("tile"), t0 + T_DOWN[0] + KD)
                            did(f(gh[:, i - 1, :], tmp[:, (ff_ - 1) % 2, :], ACT.Copy), "gh")
                        if i < FH:
                            act.wait_ge(S("conv"), ff_ + 1)
                            if ff_ >= 2:
                                act.wait_ge(S("gl"), ff_ - 1)
                            d = tmp[:, ff_ % 2, :]
                            did(f(d[:, 0:PT], cc[:, 0:PT], ACT.Silu), "act")
                            did(f(samples(d[:, PT:T]), samples(cc[:, 2 + PT:EXT], DT + 2)[:, :, 0:DT], ACT.Silu), "silu")
                    for n in range(KD):
                        tt = t0 + T_DOWN[hf] + n
                        if hf == 0:
                            evac(tt, take(tt, two(Y[:, n, :])))
                        else:
                            act.wait_ge(S("y2"), l * KD + n + 1)
                            square_x(n0 + N_FFNPOST, n, Y[:, n, :])
                exp_table()
                rstd(n0 + N_FFNPOST, WA, D)
                act.dma_start(a["o_conv"][l], cout[:, :, :]).then_inc(S("conv_out"), 16)
                act.wait_ge(S("conv_out"), 16 * (l + 1))
            for k in range(KD):
                act.wait_ge(S("x"), (2 * DEPTH - 1) * KD + k + 1)
                square_x(DEPTH * N_NORM, k, X[:, k, :])
            rstd(DEPTH * N_NORM, WA, D)
            for k in range(KD):
                act.wait_ge(S("y_out"), k + 1)
                act.dma_start(a["o_y"][k], Y[:, k, :]).then_inc(S("out"), 16)
            act.wait_ge(S("out"), 16 * (2 * DEPTH + KD))

        @block.vector
        def _(dve):
            count, last = {}, []

            def did(ins, name, at=None):
                count[name] = at or count.get(name, 0) + 1
                last[:] = [name]
                ins.then_inc(S(name), 1)

            def prev():
                if last:
                    dve.wait_ge(S(last[0]), count[last[0]])

            def op(kind):
                def go(*args, **kw):
                    prev()
                    return kind(*args, **kw)
                return go

            tt_, ts, stt, cp = (op(k) for k in (dve.tensor_tensor, dve.tensor_scalar, dve.scalar_tensor_tensor,
                                                dve.tensor_copy))
            scan, fill, keep, rmax, recip, mark = (op(k) for k in (
                dve.tensor_tensor_scan, dve.memset, dve.copy_predicated, dve.reduce_max, dve.reciprocal, dve.engine_nop))

            def step(ins):
                did(ins, "dve")

            def evac(tt, ins):
                did(ins, f"evac{tt % 2}", slot_use(tt))

            step(fill(eps[:, :], EPS))
            step(fill(Am[:, :], 0.0))
            dve.wait_ge(S("const"), 16 * N_CONST)
            step(cp(masks[:, :, :].rearrange("p (a b) t -> p a (b t)", a=2), mask_f))
            did(tt_(lbs[:, 0, 0, :], cols[:, 0, C_LB1:C_LB1 + HG], cols[:, 0, C_LB0:C_LB0 + HG], ALU.subtract), "lbd")
            dve.wait_ge(S("lb_sig"), 2)
            step(fill(lbs[:, 0, 0, :], 0.0))
            step(fill(lbs[:, 0, 1, :], 1.0))

            def add_square(n, k, first):
                c = squares(n) + k
                dve.wait_ge(S("sq"), c + 1)
                if first:
                    if n:
                        dve.wait_ge(S("ssum"), n)
                    did(cp(acc[:, :], sq[:, c % 2, :]), "sq_added")
                else:
                    dve.wait_ge(S("sq_added"), c)
                    did(tt_(acc[:, :], acc[:, :], sq[:, c % 2, :], ALU.add), "sq_added")

            def col(l, c):
                return cols[:, l, c:c + 1]

            def split(n, src, dsts, w, last):
                for k in range(len(src) + 1):
                    if k < len(src):
                        did(stt(tmp[:, k % 2, :], src[k], w[k], R[:, :], ALU.mult, ALU.mult), "hf")
                    if k:
                        dve.wait_ge(S("hh"), n + k)
                        hh_, hl_ = dsts[k - 1]
                        did(tt_(hl_, tmp[:, (k - 1) % 2, :], hh_, ALU.subtract), "hl")
                        if k < len(src):
                            dve.wait_ge(S("hl"), n + k)

            def rotate(tt, dst, rows):
                ps = G[tt % 2]
                step(tt_(two(tmp[64:96, 0, :]), halves(ps, HALF, 96, P), two(rope[96:P, :]), ALU.mult))
                evac(tt, tt_(two(dst), halves(ps, HALF, 64, 96), two(rope[64:96, :]), ALU.mult))
                dve.wait_ge(S(f"evac{tt % 2}"), slot_use(tt))
                return tt_(dst, dst, tmp[64:96, 0, :], ALU.add)

            def residual(l, n, c_w, x0):
                dve.wait_ge(S("rstd"), n + 1)
                for k in range(KD):
                    if k < KD - 1:
                        step(stt(tmp[:, k % 2, :], Y[:, k, :], col(l, c_w + k), R[:, :], ALU.mult, ALU.mult))
                    else:
                        did(stt(tmp[:, k % 2, :], Y[:, k, :], col(l, c_w + k), R[:, :], ALU.mult, ALU.mult), "R_used")
                        dve.wait_ge(S("R_used"), n + 1)
                    did(tt_(X[:, k, :], X[:, k, :], tmp[:, k % 2, :], ALU.add), "x")

            def hg_diff(l, h, lv):
                n, m, G_, d = l * HG + h, LEVELS[lv], hG(h), DE[:, lv % 2, :]
                g1, g2, ref = sub_halves(G_, m)
                d1, d2, _ = sub_halves(d, m)
                step(tt_(d1, ref, g1, ALU.subtract))
                did(tt_(d2, g2, ref, ALU.subtract), "D")

            def hg_decayed(l, h, lv):
                n, m = l * HG + h, LEVELS[lv]
                dve.wait_ge(S("E"), n * (LV + 1) + lv + 1)
                e1, e2, _ = sub_halves(DE[:, lv % 2, :], m)
                z1, z2, _ = sub_halves(Z[:, lv % 2, :], m)
                k1, _, _ = sub_halves(hk(h), m)
                _, q2, _ = sub_halves(hq(h), m)
                step(tt_(z1, k1, e1, ALU.mult))
                did(tt_(z2, q2, e2, ALU.mult), "Z")

            def hg_take(l, h, lv):
                n, m, bank = (l * HG + h) * LV + lv, LEVELS[lv], 512 * (lv % 2)
                dve.wait_ge(S("A"), n + 1)
                mk = masks[:, lv, :]
                if m <= 8:
                    step(keep(Am[:, 512:640], mk, WB[:, bank:bank + P]))
                    step(keep(Am[0:META, 640:640 + META], mk[0:META, 0:META],
                                             WB[0:META, bank + P:bank + P + META]))
                did(keep(Am[:, 0:512].rearrange("p (j t) -> p j t", j=4),
                                    mk.rearrange("p (a t) -> p a t", a=1).broadcast_to([P, 4, P]),
                                    WA[:, bank:bank + 512].rearrange("p (j t) -> p j t", j=4)), "A_taken")

            for l in range(DEPTH):
                t0, n0 = l * TILES, l * N_NORM
                for k in range(KD):
                    add_square(n0 + N_MIXPRE, k, k == 0)
                dve.wait_ge(S("rstd"), n0 + N_MIXPRE + 1)
                if l == 0:
                    dve.wait_ge(S("x_in"), 16 * KD)
                split(l * SPLITS, [X[:, k, :] for k in range(KD)], [(Hh[:, k, :], Hl[:, k, :]) for k in range(KD)],
                      [col(l, C_MIXPRE + k) for k in range(KD)], None)
                dve.wait_ge(S("hl"), l * SPLITS + KD)
                did(mark(), "R_used")
                for i in range(3):
                    tt = t0 + i
                    n, k = (n0 + N_CQ, i) if i < 2 else (n0 + N_CKV, 0)
                    if i == 2:
                        dve.wait_ge(S("ssum"), n0 + N_CQ + 1)
                    add_square(n, k, k == 0)
                    evac(tt, mark())
                dve.wait_ge(S("rstd"), n0 + N_CQ + 1)
                split(l * SPLITS + KD, [DE[:, k, :] for k in range(2)], [(cqh[:, k, :], cql[:, k, :]) for k in range(2)],
                      [col(l, C_QN + k) for k in range(2)], None)
                dve.wait_ge(S("hl"), l * SPLITS + KD + 2)
                did(mark(), "R_used")
                dve.wait_ge(S("rstd"), n0 + N_CKV + 1)
                did(stt(kvn[:, :], kvn[:, :], col(l, C_KVN), R[:, :], ALU.mult, ALU.mult), "kvn")
                dve.wait_ge(S("kvn"), l + 1)
                did(mark(), "R_used")
                dve.wait_ge(S("tile"), t0 + 4)
                did(rotate(t0 + 3, kpe[64:96, :], None), "kpe")
                for h in range(HG):
                    n, th = l * HG + h, t0 + T_HG + 4 * h
                    dve.wait_ge(S(f"evac{th % 2}"), slot_use(th))
                    step(ts(hk(h), hk(h), lbs[:, l, 1, h:h + 1], None, ALU.mult))
                    for i, dst in ((1, hq(h)), (3, gate[:, h % 2, :])):
                        dve.wait_ge(S("sig"), 2 * n + (i + 1) // 2)
                        evac(th + i, tt_(two(dst), halves(G[(th + i) % 2]), two(dst), ALU.mult))
                    dve.wait_ge(S(f"evac{(th + 3) % 2}"), slot_use(th + 3))
                    dve.wait_ge(S("gl_"), n + 1)
                    step(scan(hG(h), reset[:, :], DE[:, 0, :], 0.0, ALU.mult, ALU.add))
                    for i in range(LV + 2):
                        if i < LV - 1:
                            hg_diff(l, h, i)
                        if 1 <= i < LV:
                            hg_decayed(l, h, i - 1)
                        if i >= 2:
                            hg_take(l, h, i - 2)
                    G_, d = hG(h), DE[:, 0, :]
                    step(tt_(d[:, 0:META], G_[:, META - 1:META].broadcast_to([P, META]), G_[:, 0:META], ALU.subtract))
                    for lo, hi_, w in ((META, PT, P), (PT, T, DT)):
                        g3 = G_[:, lo:hi_].rearrange("p (b t) -> p b t", t=w)
                        e = tt_(d[:, lo:hi_].rearrange("p (b t) -> p b t", t=w),
                                g3[:, :, w - 1:w].broadcast_to([P, (hi_ - lo) // w, w]), g3, ALU.subtract)
                        if lo == META:
                            step(e)
                    did(e, "D")
                    dve.wait_ge(S("E"), n * (LV + 1) + LV)
                    dve.wait_ge(S("A_taken"), (n + 1) * LV)
                    did(tt_(hq(h), hq(h), DE[:, 1, :], ALU.mult), "qG")
                    dve.wait_ge(S("E"), n * (LV + 1) + LV + 1)
                    did(tt_(hk(h), hk(h), DE[:, 0, :], ALU.mult), "kG")
                    dve.wait_ge(S("tok"), 2 * n + 1)
                    did(tt_(Z[:, :, :].rearrange("p a n -> p (a n)")[:, 0:DB * P].rearrange("p (b v) -> p b v", b=DB),
                        vtok[:, 512:640].rearrange("p (a v) -> p a v", a=1).broadcast_to([P, DB, P]),
                        ind[:, :].rearrange("p (b a) -> p b a", a=1).broadcast_to([P, DB, P]), ALU.mult), "v_apart")
                    dve.wait_ge(S("dS"), n + 1)
                    if n:
                        dve.wait_ge(S("pst_out"), 16 * n)
                    did(cp(st[:, 0, :], WA[:, 512:640]), "state")
                    for j in range(4):
                        dve.wait_ge(S("state"), 5 * n + j + 1)
                        e_ = META + P * (j + 1) - 1
                        did(stt(st[:, j + 1, :], st[:, j, :], DE[:, 1, e_:e_ + 1], WA[:, P * j:P * j + P], ALU.mult, ALU.add), "state")
                    c = squares(n0 + N_HG + h)
                    dve.wait_ge(S("o"), n + 1)
                    dve.wait_ge(S("sq"), c + 1)
                    gt = gate[:, h % 2, :]
                    s3 = S0[:, h % 2, :].rearrange("p (b v) -> p b v", b=DB)
                    for (p0, p1), (a0, a1) in (((0, 512), (META, PT)), ((512, 512 + META), (0, META))):
                        step(stt(ob[:, h, a0:a1], WA[:, p0:p1], col(l, C_HGN), gt[:, a0:a1], ALU.mult, ALU.mult))
                    step(stt(ob[:, h, PT:T], WA[:, 640:640 + SAMP], col(l, C_HGN), gt[:, PT:T], ALU.mult, ALU.mult))
                    step(tt_(s3, s3, DE[:, 1, PT:T].rearrange("p (b t) -> p b t", t=DT)[:, :, DT - 1:DT]
                             .broadcast_to([P, DB, P]), ALU.mult))
                    dve.wait_ge(S("dS_sample"), n + 1)
                    did(tt_(S0[:, h % 2, :], S0[:, h % 2, :], WB[:, :], ALU.add), "s0_new")
                    c = squares(n0 + N_HG + h)
                    dve.wait_ge(S("sq"), c + 1)
                    dve.wait_ge(S("ssum"), n0 + N_HG + h)
                    did(mark(), "o_taken")
                    did(cp(acc[:, :], sq[:, c % 2, :]), "sq_added")
                    dve.wait_ge(S("rstd"), n0 + N_HG + h + 1)
                    did(tt_(ob[:, h, :], ob[:, h, :], R[:, :], ALU.mult), "ob")
                    dve.wait_ge(S("ob"), n + 1)
                    did(mark(), "R_used")
                for h in range(HG):
                    dve.wait_ge(S("obh"), l * HG + h + 1)
                    did(tt_(Hl[:, 4 + h, :], ob[:, h, :], Hh[:, 4 + h, :], ALU.subtract), "ob_split")
                for h in range(HM):
                    tt = t0 + T_UQ + h
                    dve.wait_ge(S("q_nope"), l * HM + h + 1)
                    step(rotate(tt, Y[64:96, h, :], None))
                for i in range(5):
                    dve.wait_ge(S("values"), 5 * l + i + 1)
                    ps = (WA, WA, WB, WB, WA)[i]
                    c = (0, 512, 0, 512, 0)[i]
                    np_ = P if i < 4 else META
                    did(cp(vt[0:np_, i, :], ps[0:np_, c:c + 512]), "vt")
                for u in range(NU + 3):
                    if u < NU:
                        h, j = UNITS[u]
                        nq, n = unit_q(j)[1], META + P * (j + 1)
                        m = mx[0:nq, u % 3, :]
                        dve.wait_ge(S("scores"), l * NU + u + 1)
                        step(rmax(m[:, 0:1], (WA, G[0])[u % 2][0:nq, 0:n], AX_X))
                        did(ts(m[:, 1:2], m[:, 0:1], -SCALE, None, ALU.mult), "max")
                    if 1 <= u < NU + 1:
                        v = u - 1
                        h, j = UNITS[v]
                        nq, n = unit_q(j)[1], META + P * (j + 1)
                        m = mx[0:nq, v % 3, :]
                        dve.wait_ge(S("exp"), l * NU + v + 1)
                        step(recip(m[:, 3:4], m[:, 2:3]))
                        pp = Pp[0:nq, v % 3, 0:n]
                        did(ts(pp, pp, m[:, 3:4], None, ALU.mult), "probs")
                    if u >= 3:
                        v = u - 3
                        h, j = UNITS[v]
                        q0, nq = unit_q(j)
                        dve.wait_ge(S("oa"), l * NU + v + 1)
                        rows = slice(64 * (h % 2), 64 * (h % 2) + 64)
                        o = (WB, G[1])[v % 2][0:VH, 640:640 + nq]
                        step(cp(Hh[rows, h // 2, q0:q0 + nq], o))
                        did(tt_(Hl[rows, h // 2, q0:q0 + nq], o, Hh[rows, h // 2, q0:q0 + nq], ALU.subtract), "oa_taken")
                for b in range(DB + 2):
                    if b < DB:
                        sl = b % 2
                        m = ms[:, sl, :]
                        dve.wait_ge(S("s_scores"), l * DB + b + 1)
                        step(rmax(m[:, 0:1], (WA, G[0])[sl][:, :], AX_X))
                        step(rmax(m[:, 1:2], WB[:, 512 + DT * sl:512 + DT * sl + DT], AX_X))
                        step(tt_(m[:, 2:3], m[:, 0:1], m[:, 1:2], ALU.max))
                        did(ts(m[:, 3:4], m[:, 2:3], -SCALE, None, ALU.mult), "s_max")
                        dve.wait_ge(S("s_exp"), l * DB + b + 1)
                        step(tt_(m[:, 6:7], m[:, 4:5], m[:, 5:6], ALU.add))
                        step(recip(m[:, 7:8], m[:, 6:7]))
                        did(ts(Ps[:, sl, :], Ps[:, sl, :], m[:, 7:8], None, ALU.mult), "s_probs")
                    if b >= 2:
                        v = b - 2
                        dve.wait_ge(S("s_oa"), l * DB + v + 1)
                        did(cp(OL[:, :, DT * v:DT * v + DT], WB[:, P:2 * P].rearrange("p (h t) -> p h t", h=HM)), "ol_taken")
                dve.wait_ge(S("oas"), l + 1)
                for par in range(2):
                    rows = slice(64 * par, 64 * par + 64)
                    o = WA[0:VH, :].rearrange("p (g a t) -> p a g t", g=4, a=2)[:, par, :, :]
                    step(cp(Hh[rows, 0:4, PT:T], o))
                    e = tt_(Hl[rows, 0:4, PT:T], o, Hh[rows, 0:4, PT:T], ALU.subtract)
                    if par == 0:
                        step(e)
                did(e, "oas_taken")
                for n in range(KD):
                    tt = t0 + T_OUT + n
                    add_square(n0 + N_MIXPOST, n, n == 0)
                    evac(tt, mark())
                dve.wait_ge(S("y"), (l + 1) * KD)
                residual(l, n0 + N_MIXPOST, C_MIXPOST, 2 * l * KD)
                for k in range(KD):
                    add_square(n0 + N_FFNPRE, k, k == 0)
                dve.wait_ge(S("rstd"), n0 + N_FFNPRE + 1)
                split(l * SPLITS + KD + 2, [X[:, k, :] for k in range(KD)],
                      [(Hh[:, k, :], Hl[:, k, :]) for k in range(KD)], [col(l, C_FFNPRE + k) for k in range(KD)], None)
                dve.wait_ge(S("hl"), l * SPLITS + 2 * KD + 2)
                did(mark(), "R_used")
                step(fill(ax[:, :, 0:2], 0.0))
                dve.wait_ge(S("cst_in"), 16 * (l + 1))
                for hf in range(2):
                    for i in range(FH + 1):
                        ff_ = l * KF + hf * FH + i
                        fc = hf * FH + i
                        if i < FH:
                            tt = t0 + T_UP[hf] + 2 * i
                            s_ = ax[:, ff_ % 2, :]
                            sv = samples(s_[:, 2 + PT:EXT], DT + 2)
                            step(cp(sv[:, :, 0:2], cst[:, 16 * fc:16 * fc + 16].rearrange("p (b t) -> p b t", t=2)))
                            dve.wait_ge(S(f"evac{tt % 2}"), slot_use(tt))
                            step(cp(cout[:, fc, 0:2], s_[:, PT:PT + 2]))
                            step(cp(cout[:, fc, 2:18].rearrange("p (b t) -> p b t", t=2), sv[:, :, DT:DT + 2]))
                            if ff_:
                                dve.wait_ge(S("silu"), ff_)
                            n_ = EXT - 2
                            step(ts(cc[:, 0:n_], s_[:, 0:n_], col(l, C_CW + fc), col(l, C_CB + fc), ALU.mult, ALU.add))
                            step(stt(cc[:, 0:n_], s_[:, 1:1 + n_], col(l, C_CW + KF + fc), cc[:, 0:n_], ALU.mult, ALU.add))
                            did(stt(cc[:, 0:n_], s_[:, 2:2 + n_], col(l, C_CW + 2 * KF + fc), cc[:, 0:n_], ALU.mult, ALU.add), "conv")
                        if i >= 1:
                            dve.wait_ge(S("gh"), ff_)
                            did(tt_(gl[:, i - 1, :], tmp[:, (ff_ - 1) % 2, :], gh[:, i - 1, :], ALU.subtract), "gl")
                        if i < FH:
                            tt = t0 + T_UP[hf] + 2 * i + 1
                            dve.wait_ge(S("tile"), tt + 1)
                            dve.wait_ge(S("silu"), ff_ + 1)
                            d = two(tmp[:, ff_ % 2, :])
                            step(tt_(d, halves(G[tt % 2]), d, ALU.mult))
                            did(mark(), "gv")
                            evac(tt, mark())
                    for n in range(KD):
                        tt = t0 + T_DOWN[hf] + n
                        if hf:
                            dve.wait_ge(S("tile"), tt + 1)
                            step(tt_(two(Y[:, n, :]), two(Y[:, n, :]), halves(G[tt % 2]), ALU.add))
                            did(mark(), "y2")
                            evac(tt, mark())
                            add_square(n0 + N_FFNPOST, n, n == 0)
                residual(l, n0 + N_FFNPOST, C_FFNPOST, (2 * l + 1) * KD)
                step(fill(Am[:, :], 0.0)) if l + 1 < DEPTH else None
            for k in range(KD):
                add_square(DEPTH * N_NORM, k, k == 0)
            dve.wait_ge(S("rstd"), DEPTH * N_NORM + 1)
            for k in range(KD):
                did(stt(Y[:, k, :], X[:, k, :], col(0, C_FIN + k), R[:, :], ALU.mult, ALU.mult), "y_out")


def layouts(x):
    f = np.float32
    ins = {}
    tokens = np.concatenate([x["meta_tokens"], x["x_prompt"][0], x["x_sample"].reshape(SAMP, D)], 0)
    ins["xT"] = tokens.T.reshape(KD, P, T)

    def blocks(w):
        k, n = w.shape
        return w.reshape(k // P, P, n // P, P).transpose(2, 1, 0, 3).reshape(n // P, P, k)

    in_cols = [np.arange(i * P, i * P + P) for i in range(3)]
    pe = QL + KL + np.arange(ROPE)
    swap = np.concatenate([pe[ROPE // 2:], pe[:ROPE // 2]])
    in_cols.append(np.concatenate([pe, pe, pe, swap]))
    base = QL + KL + ROPE
    for h in range(HG):
        for part in (1, 0, 2, 3):
            in_cols.append(base + part * HG * P + h * P + np.arange(P))
    in_cols = np.concatenate(in_cols)
    uq_cols = np.concatenate([h * (NOPE + ROPE) + np.concatenate(
        [np.arange(NOPE), NOPE + np.arange(ROPE), NOPE + ROPE // 2 + np.arange(ROPE // 2), NOPE + np.arange(ROPE // 2)])
        for h in range(HM)])
    stream = []
    for l in range(DEPTH):
        up = x["w_ffn_up"][l]
        av = np.stack([up[:, :FF].reshape(D, KF, P), up[:, FF:].reshape(D, KF, P)], 2).reshape(D, 2 * FF)
        uq = blocks(x["w_uq"][l][:, uq_cols])
        parts = [blocks(x["w_in"][l][:, in_cols]),
                 uq.reshape(2, 4, P, 256).transpose(0, 2, 1, 3).reshape(2, P, W_PIECE),
                 blocks(x["w_out"][l])]
        for hf in range(2):
            parts.append(blocks(av[:, hf * 2 * FH * P:(hf + 1) * 2 * FH * P]))
            dn = x["w_ffn_down"][l][hf * FH * P:(hf + 1) * FH * P].reshape(FH, P, KD, P)
            parts.append(dn.transpose(2, 0, 1, 3).reshape(FH, 8, P, P).transpose(0, 2, 1, 3).reshape(FH, P, W_PIECE))
        stream.append(np.concatenate(parts, 0))
    ins["wstream"] = np.stack(stream)
    ins["wA"] = np.concatenate([x["w_uk"].reshape(DEPTH, KL, 512), x["w_uv"].reshape(DEPTH, KL, 512)], 2)
    ins["wB"] = x["w_uk"].transpose(0, 3, 2, 1).reshape(DEPTH, NOPE, 1024)
    ins["ckT"] = x["cache_kv_latent"].transpose(0, 1, 3, 2)
    ins["cpe"] = x["cache_k_rope"].transpose(0, 1, 3, 2)
    ins["ctok"] = x["cache_kv_latent"].reshape(DEPTH, DB, PC, P, KL).transpose(0, 1, 3, 2, 4).reshape(DEPTH, DB, P, PAST)
    ins["s0"] = x["state_hgrn"].transpose(0, 2, 3, 1, 4).reshape(DEPTH, HG, P, DB * P)
    ins["cst"] = x["state_ffn_conv"].transpose(0, 3, 1, 2).reshape(DEPTH, KF, P, DB * 2).transpose(0, 2, 1, 3)\
        .reshape(DEPTH, P, KF * DB * 2)

    def col(v):
        return v.reshape(v.shape[0], -1, P)

    both = lambda v: np.stack([v, v])
    pack = np.concatenate([
        col(x["norm_mix_pre"]), col(x["norm_mix_post"]), col(x["norm_ffn_pre"]), col(x["norm_ffn_post"]),
        col(x["q_norm"]), col(x["kv_norm"]), col(x["hg_out_norm"]),
        both(x["hg_lower_bounds"][0].reshape(HG, P)), both(x["hg_lower_bounds"][1].reshape(HG, P)),
        both(x["final_norm"].reshape(KD, P)), col(x["ffn_conv_b"]), x["ffn_conv_w"].reshape(DEPTH, CONV * KF, P)], 1)
    ins["cols"] = pack.transpose(2, 0, 1)
    pos = np.concatenate([np.arange(PT) - META, PAST + np.tile(np.arange(DT), DB)]).astype(f)
    inv = f(10000.0) ** (-np.arange(ROPE // 2, dtype=f) / f(ROPE // 2))
    ang = (inv[:, None] * pos[None]).astype(f)
    tab = np.zeros((P, T), f)
    tab[64:80] = tab[80:96] = np.cos(ang)
    tab[96:112], tab[112:128] = -np.sin(ang), np.sin(ang)
    ins["rope"] = tab
    rs = np.ones((P, T), f)
    rs[:, [0] + [META + P * j for j in range(4)] + [PT + DT * b for b in range(DB)]] = 0
    ins["reset"] = rs
    s, t = np.arange(P)[:, None], np.arange(P)[None]
    ins["masks"] = np.stack([(s // (2 * m) == t // (2 * m)) & (s % (2 * m) < m) & (t % (2 * m) >= m) if m else s == t
                             for m in LEVELS], 1).astype(f).reshape(P, 2, -1)
    ins["ones"], ins["ident"] = np.ones((P, P), f), np.eye(P, dtype=f)
    ins["ind"] = (np.arange(P)[:, None] // DT == np.arange(DB)[None]).astype(f)
    q, k = np.zeros((4, T), f), np.zeros((4, PT), f)
    for j in range(4):
        q[j, META + P * j:META + P * j + CH] = 1
        k[j, META + P * j + CH:META + P * (j + 1)] = -BIG
    ins["qrows"] = np.repeat(q[:, None], HM, 1)
    ins["krows"] = np.repeat(k[:, None], HM, 1)
    return {n: np.ascontiguousarray(v) for n, v in ins.items()}


CONV = 3
OUTS = {
    "o_y": (KD, P, T), "o_kv": (DEPTH, P, T), "o_kpe": (DEPTH, ROPE, T), "o_pst": (DEPTH, HG, P, P),
    "o_sst": (DEPTH, HG, P, DB * P), "o_conv": (DEPTH, P, KF, 2 + DB * 2),
}


def kernel(**inputs):
    import concourse.bacc as bacc
    from concourse.bass_utils import run_bass_kernel_spmd

    arrays = {"in_" + n: v for n, v in layouts({k: np.asarray(v) for k, v in inputs.items()}).items()}
    nc = bacc.Bacc("TRN2", target_bir_lowering=False, num_devices=1)
    aps = {n[3:]: nc.dram_tensor(n, v.shape, mybir.dt.from_np(v.dtype), kind="ExternalInput").ap() for n, v in arrays.items()}
    for n, shape in OUTS.items():
        aps[n] = nc.dram_tensor(n, shape, F32, kind="ExternalOutput").ap()
    build(nc, aps)
    r = run_bass_kernel_spmd(nc, [arrays], core_ids=[0]).results[0]
    y = r["o_y"].reshape(D, T)
    kv, kpe, conv = r["o_kv"], r["o_kpe"], r["o_conv"]
    conv = conv.transpose(0, 2, 1, 3).reshape(DEPTH, FF, 2 + DB * 2)
    sst = r["o_sst"].reshape(DEPTH, HG, P, DB, P).transpose(0, 3, 1, 2, 4)

    def rows(v):
        v = v.transpose(0, 2, 1)
        return v[:, None, :PT], v[:, PT:].reshape(DEPTH, DB, DT, -1)

    (pkv, skv), (ppe, spe) = rows(kv), rows(kpe)
    out = (y[:, META:PT].T[None], y[:, PT:].T.reshape(DB, DT, D), pkv, ppe, r["o_pst"][:, None],
           conv[:, :, :2].transpose(0, 2, 1)[:, None], skv, spe, sst,
           conv[:, :, 2:].reshape(DEPTH, FF, DB, 2).transpose(0, 2, 3, 1))
    return tuple(np.ascontiguousarray(o) for o in out)
```

```python
from contextlib import ExitStack

import numpy as np

import concourse.bass as bass
from concourse import mybir

F32 = mybir.dt.float32
F32R = mybir.dt.float32r
U8 = mybir.dt.uint8
BF16 = mybir.dt.bfloat16
ALU = mybir.AluOpType
ACT = mybir.ActivationFunctionType
AX_X = mybir.AxisListType.X

P = 128
D = 1024
KD = D // P
DEPTH = 2
META = 16
SEQ = 512
DB, DT = 8, 16
SAMP = DB * DT
PT = META + SEQ
T = PT + SAMP
HALF = T // 2
PAST = 1024
PC = PAST // P
CH = 64
HM, NOPE, ROPE, VH = 8, 64, 32, 64
QL, KL = 256, 128
HG = 4
FF = 2816
KF = FF // P
FH = KF // 2
EPS = 1e-6
SCALE = float(NOPE + ROPE) ** -0.5
BIG = float(2.0 ** 100)
EXT = PT + 2 + DB * (DT + 2)
LEVELS = [64, 32, 16, 8, 4, 2, 1, 0]

W_PIECE = 1024
N_IN, N_UQ, N_OUT, N_UP, N_DOWN = 20, 2, KD, 2 * FH, FH
PIECES = N_IN + N_UQ + N_OUT + 2 * (N_UP + N_DOWN)
P_UQ = N_IN
P_OUT = P_UQ + N_UQ
P_UP = [P_OUT + N_OUT, P_OUT + N_OUT + N_UP + N_DOWN]
P_DOWN = [p + N_UP for p in P_UP]
RAW, SPL = 2, 3

T_HG = 4
T_UQ = T_HG + 4 * HG
T_UK = T_UQ + HM
T_OUT = T_UK + HM // 2
T_UP = [T_OUT + KD, T_OUT + KD + 2 * FH + KD]
T_DOWN = [t + 2 * FH for t in T_UP]
TILES = T_DOWN[1] + KD

C_MIXPRE, C_MIXPOST, C_FFNPRE, C_FFNPOST = 0, 8, 16, 24
C_QN, C_KVN, C_HGN, C_LB0, C_LB1, C_FIN, C_CB, C_CW = 32, 34, 35, 36, 40, 44, 52, 74
NCOL = C_CW + 3 * KF



def build(nc, a):
    ctx = ExitStack()
    sems = {}

    def sb(stack, name, shape, dt=F32):
        return stack.enter_context(nc.sbuf_tensor(name, shape, dt))

    with ctx:
        def S(name):
            if name not in sems:
                sems[name] = ctx.enter_context(nc.semaphore(name))
            return sems[name]

        X = sb(ctx, "X", [P, KD, T])
        Y = sb(ctx, "Y", [P, KD, T])
        Hh = sb(ctx, "Hh", [P, KD, T], F32R)
        Hl = sb(ctx, "Hl", [P, KD, T], F32R)
        wraw = sb(ctx, "wraw", [P, RAW, W_PIECE])
        whi = sb(ctx, "whi", [P, SPL, W_PIECE], F32R)
        wlo = sb(ctx, "wlo", [P, SPL, W_PIECE], F32R)
        ones = sb(ctx, "ones", [P, P])
        ident = sb(ctx, "ident", [P, P])
        masks = sb(ctx, "masks", [P, len(LEVELS), P], U8)
        reset = sb(ctx, "reset", [P, T], BF16)
        rope = sb(ctx, "rope", [P, T])
        cols = sb(ctx, "cols", [P, DEPTH, NCOL])
        ind = sb(ctx, "ind", [P, DB])
        lbs = sb(ctx, "lbs", [P, DEPTH, 2, HG])
        zero = sb(ctx, "zero", [P, 1])
        eps = sb(ctx, "eps", [P, 1])
        mask_f = Y[:, 0:2, 0:P * len(LEVELS) // 2]
        reset_f = Y[:, 2, :]
        acc = sb(ctx, "acc", [P, T])
        sq = sb(ctx, "sq", [P, 2, T])
        R = sb(ctx, "R", [P, T])
        R2 = sb(ctx, "R2", [P, T])
        tmp = sb(ctx, "tmp", [P, 2, T])

        mix = ExitStack()
        kvn = sb(mix, "kvn", [P, T])
        kpe = sb(mix, "kpe", [P, T])
        ob = sb(mix, "ob", [P, HG, T])
        wA = sb(mix, "wA", [P, 1024])
        hg = ExitStack()
        cqh = sb(hg, "cqh", [P, 2, T], F32R)
        cql = sb(hg, "cql", [P, 2, T], F32R)
        gate = sb(hg, "gate", [P, 2, T])
        DE = sb(hg, "DE", [P, 2, T])
        Z = sb(hg, "Z", [P, 2, T])
        Am = sb(hg, "Am", [P, 6 * P])
        vtok = sb(hg, "vtok", [P, 6 * P])
        ktok = sb(hg, "ktok", [P, 6 * P])
        st = sb(hg, "st", [P, 5, P])
        S0 = sb(hg, "S0", [P, 2, DB * P])
        hg.close()
        att = ExitStack()
        ckT = sb(att, "ckT", [P, 2, PAST])
        cpe = sb(att, "cpe", [P, 2, PAST])
        pr = ExitStack()
        KT = sb(pr, "KT", [P, HM, PT])
        vt = sb(pr, "vt", [P, 5, HM * VH])
        Pp_ = sb(pr, "Pp", [P, 3, PT])
        Pt = sq
        mx = sb(pr, "mx", [P, 4, 4])
        mxm = sb(pr, "mxm", [META, 3, HM])
        pr.close()
        sa = ExitStack()
        ctok = sb(sa, "ctok", [P, 2, PAST])
        Ps = sb(sa, "Ps", [P, 2, PAST + DT])
        Pts = sb(sa, "Pts", [P, 9 * P])
        ntok = sb(sa, "ntok", [DT, DB * P])
        ql = sb(sa, "ql", [P, DB, HM * DT])
        OL = sb(sa, "OL", [P, HM, SAMP])
        ms = sb(sa, "ms", [P, 2, 8])
        qpe = tmp[64:96, :, :].rearrange("p a n -> p (a n)")[:, 0:DB * HM * DT]
        sa.close()
        att.close()
        mix.close()
        ff = ExitStack()
        gh = sb(ff, "gh", [P, FH, T], F32R)
        gl = sb(ff, "gl", [P, FH, T], F32R)
        ax = sb(ff, "ax", [P, 2, EXT])
        cc = sb(ff, "cc", [P, EXT])
        cst = sb(ff, "cst", [P, KF * DB * 2])
        cout = sb(ff, "cout", [P, KF, 2 + DB * 2])
        ff.close()

        def pb(name):
            return ctx.enter_context(nc.psum_tensor(name, [P, 1024], F32))

        G = [pb("G0"), pb("G1")]
        WA, WB = pb("WA"), pb("WB")

        def halves(ps, n=HALF, p0=0, p1=P):
            return ps[p0:p1, :].rearrange("p (a n) -> p a n", a=2)[:, :, 0:n]

        def two(ap, n=HALF):
            return ap.rearrange("p (a n) -> p a n", n=n)

        def samples(ap, w=DT):
            return ap.rearrange("p (b t) -> p b t", t=w)

        NORM_SQ = [KD, 2, 1, 1, 1, 1, 1, KD, KD, KD]
        N_NORM = len(NORM_SQ)
        N_MIXPRE, N_CQ, N_CKV, N_HG, N_MIXPOST, N_FFNPRE, N_FFNPOST = 0, 1, 2, 3, 7, 8, 9

        def squares(n):
            l, i = divmod(n, N_NORM)
            return l * sum(NORM_SQ) + sum(NORM_SQ[:i])

        LV = len(LEVELS)
        SPLITS = 2 * KD + 2

        def slot_use(tt):
            return tt // 2 + 1

        def piece_end(g):
            l, p = divmod(g, PIECES)
            if p < N_IN:
                return "tile", l * TILES + p + 1
            if p < P_OUT:
                return "tile", l * TILES + T_UQ + 4 * (p - P_UQ) + 4
            if p < P_UP[0]:
                return "tile", l * TILES + T_OUT + p - P_OUT + 1
            for hf in range(2):
                if P_UP[hf] <= p < P_DOWN[hf]:
                    return "tile", l * TILES + T_UP[hf] + p - P_UP[hf] + 1
                if P_DOWN[hf] <= p < P_DOWN[hf] + N_DOWN:
                    i = p - P_DOWN[hf]
                    if i == N_DOWN - 1:
                        return "tile", l * TILES + T_DOWN[hf] + KD
                    return "w_mid", (2 * l + hf) * (N_DOWN - 1) + i + 1

        UNITS = [(0, -1)] + [(h, j) for h in range(HM) for j in range(4)]
        NU = len(UNITS)

        def Pp(u):
            return R2[:, 0:PT] if u % 4 == 3 else Pp_[:, u % 4, :]

        def unit_keys(j):
            return META + P * (j + 1)

        def sub_halves(t, m):
            v = t[:, 0:T] if m <= 8 else t[:, META:PT]
            v = v.rearrange("p (b m) -> p b m", m=2 * m)
            nb = v.shape[1]
            return v[:, :, 0:m], v[:, :, m:2 * m], v[:, :, m - 1:m].broadcast_to([P, nb, m])

        def span(t, m):
            return t[:, 0:T] if m <= 8 else t[:, META:PT]

        def hq(h): return Y[:, 4 * (h % 2) + 0, :]
        def hk(h): return Y[:, 4 * (h % 2) + 1, :]
        def hG(h): return Y[:, 4 * (h % 2) + 2, :]
        def hv(h): return Y[:, 4 * (h % 2) + 3, :]

        N_CONST = 6

        def outer(n):
            l, i = divmod(n, N_NORM)
            return 4 * l + (0 if i == 0 else i - N_MIXPOST + 1)

        def inner(n):
            l, i = divmod(n, N_NORM)
            return (N_MIXPOST - 1) * l + i - 1
        block = ctx.enter_context(nc.Block())

        @block.sync
        def _(sp):
            for g in range(DEPTH * PIECES):
                if g >= RAW:
                    sp.wait_ge(S("w_split"), g - RAW + 1)
                sp.dma_start(wraw[:, g % RAW, :], a["wstream"][g // PIECES, g % PIECES])\
                    .then_inc(S(f"w_in{g % RAW}"), 16)

        @block.gpsimd
        def _(pool):
            pool.memset(zero[:, :], 0.0).then_inc(S("zero"), 1)
            pool.wait_ge(S("zero"), 1)
            zb = zero[:, 0:1].broadcast_to([P, W_PIECE])

            def residual(r):
                for k in range(KD):
                    pool.wait_ge(S("dx"), r * KD + k + 1)
                    pool.tensor_tensor(X[:, k, :], X[:, k, :], tmp[:, k % 2, :], ALU.add).then_inc(S("x"), 1)

            def normalize(l):
                for u in range(1, NU):
                    n = unit_keys(UNITS[u][1])
                    pool.wait_ge(S("inv_sum"), l * (NU - 1) + u)
                    pp = Pp(u)[:, 0:n]
                    pool.tensor_tensor(pp, pp, mx[:, u % 4, 2:3].broadcast_to([P, n]), ALU.mult).then_inc(S("probs"), 1)

            for g in range(DEPTH * PIECES):
                l, i = divmod(g, PIECES)
                if i == P_OUT + 3:
                    normalize(l)
                if i == P_UP[0] + 2:
                    residual(2 * l)
                if l and i == 2:
                    residual(2 * l - 1)
                pool.wait_ge(S(f"w_in{g % RAW}"), 16 * (g // RAW + 1))
                if g >= SPL:
                    pool.wait_ge(S(piece_end(g - SPL)[0]), piece_end(g - SPL)[1])
                raw, hi, lo = wraw[:, g % RAW, :], whi[:, g % SPL, :], wlo[:, g % SPL, :]
                pool.tensor_tensor(hi, raw, zb, ALU.add).then_inc(S("w_hi"), 1)
                pool.wait_ge(S("w_hi"), g + 1)
                pool.tensor_tensor(lo, raw, hi, ALU.subtract).then_inc(S("w_split"), 1)
            residual(2 * DEPTH - 1)

        @block.tensor
        def _(pe):
            pe.wait_ge(S("const"), 16 * N_CONST)

            def mm(out, lhsT, rhs, start=True, stop=True):
                return pe.matmul(out, lhsT, rhs, start=start, stop=stop, skip_group_check=True)

            def tr(out, in_):
                n = in_.shape[0]
                return pe.transpose(out, in_, ident[0:n, 0:n])

            def norm_sum(n, ps):
                pe.wait_ge(S("sq_added"), squares(n + 1))
                if n:
                    pe.wait_ge(S("rstd"), n)
                for x in range(2):
                    m = mm(ps[:, 512 * x:512 * x + HALF], ones[:, :], acc[:, HALF * x:HALF * x + HALF])
                m.then_inc(S("ssum"), 1)

            def tile_free(tt):
                if tt >= 2:
                    pe.wait_ge(S(f"evac{tt % 2}"), slot_use(tt) - 1)

            def tile(tt, chunks, rh, rl, ready=None):
                tile_free(tt)
                for i, (g, c) in enumerate(chunks):
                    pe.wait_ge(S("w_split"), g + 1)
                    if ready is not None:
                        ready(i)
                    wh, wl = whi[:, g % SPL, c:c + P], wlo[:, g % SPL, c:c + P]
                    last = i == len(chunks) - 1
                    for x in range(2):
                        o = G[tt % 2][:, 512 * x:512 * x + HALF]
                        cs = slice(HALF * x, HALF * x + HALF)
                        mm(o, wl, rh[:, i, cs], i == 0, False)
                        mm(o, wh, rh[:, i, cs], False, False)
                        m = mm(o, wh, rl[:, i, cs], False, last)
                    if c + P == W_PIECE and not last:
                        m.then_inc(S("w_mid"), 1)
                m.then_inc(S("tile"), 1)

            def head_tile(l, h, i):
                g = l * PIECES + T_HG + 4 * h + i
                tile(l * TILES + T_HG + 4 * h + i, [(g, k * P) for k in range(KD)], Hh, Hl)

            def level(l, h, lv):
                n = (l * HG + h) * LV + lv
                m = LEVELS[lv]
                if m:
                    pe.wait_ge(S("Z"), (l * HG + h) * (LV - 1) + lv + 1)
                    zk = zq = Z[:, lv % 2, :]
                else:
                    zk, zq = hk(h), hq(h)
                if n >= 2:
                    pe.wait_ge(S("A_taken"), n - 1)
                if lv < 2 and (l or h):
                    pe.wait_ge(S("o_taken"), l * HG + h)
                bank = 512 * (lv % 2)
                for j in range(4):
                    cs = slice(META + P * j, META + P * j + P)
                    e = mm(WA[:, bank + P * j:bank + P * j + P], zk[:, cs], zq[:, cs])
                if m <= 8:
                    mm(WB[:, bank:bank + P], zk[:, PT:T], zq[:, PT:T])
                    e = mm(WB[0:META, bank + P:bank + P + META], zk[:, 0:META], zq[:, 0:META])
                e.then_inc(S("A"), 1)

            def to_tokens(ps, src):
                for j in range(4):
                    tr(ps[:, P * j:P * j + P], src[:, META + P * j:META + P * j + P])
                tr(ps[:, 512:512 + P], src[:, PT:T])
                return tr(ps[0:META, 640:640 + P], src[:, 0:META])

            def turns(l, h):
                n = l * HG + h
                tv = l * TILES + T_HG + 4 * h
                pe.wait_ge(S(f"evac{tv % 2}"), slot_use(tv))
                pe.wait_ge(S("A_taken"), (n + 1) * LV)
                to_tokens(WA, hv(h)).then_inc(S("v_turned"), 1)
                pe.wait_ge(S("kG"), n + 1)
                to_tokens(WB, hk(h)).then_inc(S("k_turned"), 1)

            def state_sums(l, h):
                n = l * HG + h
                pe.wait_ge(S("tok"), 2 * (n + 1))
                for j in range(4):
                    mm(WA[:, P * j:P * j + P], ktok[:, P * j:P * j + P], vtok[:, P * j:P * j + P])
                mm(WA[:, 512:512 + P], ktok[0:META, 640:640 + P], vtok[0:META, 640:640 + P]).then_inc(S("dS"), 1)
                pe.wait_ge(S("v_apart"), n + 1)
                for x in range(2):
                    e = mm(WB[:, 512 * x:512 * x + 512], ktok[:, 512:512 + P],
                           Z[:, :, :].rearrange("p a n -> p (a n)")[:, 512 * x:512 * x + 512])
                e.then_inc(S("dS_sample"), 1)

            def head_out(l, h):
                n = l * HG + h
                pe.wait_ge(S("state"), 5 * (n + 1))
                pe.wait_ge(S("qG"), n + 1)
                pe.wait_ge(S(f"s0_in{h % 2}"), 16 * (2 * l + h // 2 + 1))
                for j in range(4):
                    o = WA[:, P * j:P * j + P]
                    mm(o, vtok[:, P * j:P * j + P], Am[:, P * j:P * j + P], True, False)
                    mm(o, st[:, j, :], hq(h)[:, META + P * j:META + P * j + P], False, True)
                mm(WA[:, 512:512 + META], vtok[0:META, 640:640 + P], Am[0:META, 640:640 + META])
                mm(WA[:, 640:640 + SAMP], vtok[:, 512:512 + P], Am[:, 512:512 + P], True, False)
                for b in range(DB):
                    e = mm(WA[:, 640 + DT * b:640 + DT * b + DT], S0[:, h % 2, P * b:P * b + P],
                           hq(h)[:, PT + DT * b:PT + DT * b + DT], False, b == DB - 1)
                e.then_inc(S("o"), 1)

            def prompt_scores(l, u):
                h, j = UNITS[u]
                n = unit_keys(j)
                if u >= 2 or l:
                    pe.wait_ge(S("exp"), l * NU + u - 1 if u >= 2 else l * NU)
                ps = (WA, G[0])[u % 2]
                if j < 0:
                    for h in range(HM):
                        e = mm(ps[0:META, META * h:META * h + META], Y[0:100, h, 0:META], KT[0:100, h, 0:META])
                else:
                    for c in range(0, n, 512):
                        e = mm(ps[:, c:min(n, c + 512)], Y[0:100, h, META + P * j:META + P * j + P],
                               KT[0:100, h, c:min(n, c + 512)])
                e.then_inc(S("scores"), 1)

            def prompt_turn(l, u):
                h, j = UNITS[u]
                ps, pp = (WB, G[1])[u % 2], Pp(u)
                if j < 0:
                    pe.wait_ge(S("probs_meta"), l + 1)
                else:
                    pe.wait_ge(S("probs"), l * (NU - 1) + u)
                if u >= 2:
                    pe.wait_ge(S("oa_taken"), l * NU + u - 1)
                if j < 0:
                    for h in range(HM):
                        e = tr(ps[0:META, META * h:META * h + META], pp[0:META, META * h:META * h + META])
                else:
                    for c in range(j + 1):
                        tr(ps[:, P * c:P * c + P], pp[:, META + P * c:META + P * c + P])
                    e = tr(ps[0:META, P * (j + 1):P * (j + 2)], pp[:, 0:META])
                e.then_inc(S("turned"), 1)

            def prompt_out(l, u):
                h, j = UNITS[u]
                pe.wait_ge(S("Pt"), l * NU + u + 1)
                o, pt = (WB, G[1])[u % 2][0:VH, 640:640 + P], Pt[:, u % 2, :]
                if j < 0:
                    for h in range(HM):
                        e = mm(o[:, META * h:META * h + META], vt[0:META, 4, VH * h:VH * h + VH],
                               pt[0:META, META * h:META * h + META])
                else:
                    mm(o, vt[0:META, 4, VH * h:VH * h + VH], pt[0:META, P * (j + 1):P * (j + 2)], True, False)
                    for c in range(j + 1):
                        e = mm(o, vt[:, c, VH * h:VH * h + VH], pt[:, P * c:P * c + P], False, c == j)
                e.then_inc(S("oa"), 1)

            def sample_scores(l, b):
                pe.wait_ge(S(f"ck_in{b % 2}"), 32 * (l * DB // 2 + b // 2 + 1))
                if b >= 2:
                    pe.wait_ge(S("s_exp"), l * DB + b - 1)
                ps = (WA, G[0])[b % 2]
                lat, pe_q = ql[:, b, :], qpe[:, P * b:P * b + P]
                for c in range(0, PAST, 512):
                    mm(ps[:, c:c + 512], lat, ckT[:, b % 2, c:c + 512], True, False)
                    mm(ps[:, c:c + 512], pe_q, cpe[64:96, b % 2, c:c + 512], False, True)
                new = WB[:, 512 + DT * (b % 2):512 + DT * (b % 2) + DT]
                cs = slice(PT + DT * b, PT + DT * b + DT)
                if b:
                    pe.wait_ge(S("s_exp"), l * DB + b)
                mm(new, lat, kvn[:, cs], True, False)
                mm(new, pe_q, kpe[64:96, cs], False, True).then_inc(S("s_scores"), 1)

            def sample_turn(l, b):
                pe.wait_ge(S("s_probs"), l * DB + b + 1)
                for x in range(2):
                    if b:
                        pe.wait_ge(S("s_Pt"), 3 * (l * DB + b - 1) + x + 1)
                    for c in range(4):
                        e = tr(G[1][:, 512 * x + P * c:512 * x + P * c + P],
                               Ps[:, b % 2, P * (4 * x + c):P * (4 * x + c) + P])
                    e.then_inc(S("s_turned"), 1)
                if b:
                    pe.wait_ge(S("s_Pt"), 3 * (l * DB + b))
                    pe.wait_ge(S("ol_taken"), l * DB + b)
                tr(WB[0:DT, 0:P], Ps[:, b % 2, PAST:PAST + DT]).then_inc(S("s_turned"), 1)

            def sample_out(l, b):
                pe.wait_ge(S("s_Pt"), 3 * (l * DB + b + 1))
                pe.wait_ge(S(f"ct_in{b % 2}"), 16 * (l * DB // 2 + b // 2 + 1))
                o = WB[:, P:2 * P]
                if b:
                    pe.wait_ge(S("ol_taken"), l * DB + b)
                mm(o, ntok[:, P * b:P * b + P], Pts[0:DT, 8 * P:9 * P], True, False)
                for c in range(PC):
                    e = mm(o, ctok[:, b % 2, P * c:P * c + P], Pts[:, P * c:P * c + P], False, c == PC - 1)
                e.then_inc(S("s_oa"), 1)

            for l in range(DEPTH):
                g0, t0, n0 = l * PIECES, l * TILES, l * N_NORM
                for i in range(T_HG):
                    tile(t0 + i, [(g0 + i, k * P) for k in range(KD)], Hh, Hl,
                         (lambda k: pe.wait_ge(S("hl"), l * SPLITS + k + 1)) if i == 0 else None)
                    if i == 1:
                        norm_sum(n0 + N_MIXPRE, WA)
                head_tile(l, 0, 0)
                norm_sum(n0 + N_CQ, WA)
                head_tile(l, 0, 1)
                head_tile(l, 0, 2)
                norm_sum(n0 + N_CKV, WA)
                head_tile(l, 0, 3)
                head_tile(l, 1, 0)
                head_tile(l, 1, 1)
                pe.wait_ge(S("rstd"), n0 + N_CKV + 1)

                def queries(h):
                    g = g0 + P_UQ + h // 4
                    tile(t0 + T_UQ + h, [(g, 256 * (h % 4) + k * P) for k in range(2)], cqh, cql,
                         lambda k: pe.wait_ge(S("hl"), l * SPLITS + KD + 2))

                for h in range(HG):
                    for lv in range(LV):
                        level(l, h, lv)
                        if lv in (2, 5) and h + 1 < HG:
                            head_tile(l, h + 1, 2 + lv // 5)
                        if lv == 2 and h + 1 == HG:
                            queries(2)
                            queries(3)
                    turns(l, h)
                    state_sums(l, h)
                    head_out(l, h)
                    if h + 2 < HG:
                        head_tile(l, h + 2, 0)
                    elif h + 2 == HG:
                        queries(0)
                        queries(1)
                    pe.wait_ge(S("s0_new"), l * HG + h + 1)
                    norm_sum(n0 + N_HG + h, WB)
                    if h + 2 < HG:
                        head_tile(l, h + 2, 1)
                for h in range(HG, HM):
                    queries(h)
                pe.wait_ge(S("wA_in"), 16 * (l + 1))
                pe.wait_ge(S("kvn"), l + 1)
                for p in range(HM // 2):
                    tt = t0 + T_UK + p
                    tile_free(tt)
                    for x in range(2):
                        e = mm(G[tt % 2][:, 512 * x:512 * x + PT // 2], wA[:, P * p:P * p + P],
                               kvn[:, PT // 2 * x:PT // 2 * x + PT // 2])
                    e.then_inc(S("tile"), 1)
                pe.wait_ge(S("ob"), l * HG + HG)
                for i in range(5):
                    cs = slice(META + P * i, META + P * i + P) if i < 4 else slice(0, META)
                    if i == 4:
                        pe.wait_ge(S("vt"), 5 * l + 1)
                    ps = (WA, WA, WB, WB, WA)[i]
                    c = (0, 512, 0, 512, 0)[i]
                    mm(ps[0:P if i < 4 else META, c:c + 512], kvn[:, cs], wA[:, 512:1024]).then_inc(S("values"), 1)
                pe.wait_ge(S("vt"), 5 * (l + 1))
                pe.wait_ge(S("kt"), l + 1)
                pe.wait_ge(S("maskrows"), 32 * (l + 1))
                for tt in (t0 + T_OUT, t0 + T_OUT + 1):
                    tile_free(tt)
                for u in range(NU + 4):
                    if u < NU:
                        prompt_scores(l, u)
                    if u >= 4:
                        prompt_out(l, u - 4)
                    if 3 <= u < NU + 3:
                        prompt_turn(l, u - 3)
                pe.wait_ge(S("oa_taken"), (l + 1) * NU)
                pe.wait_ge(S("wB_in"), 16 * (l + 1))
                for h in range(HM):
                    e = mm(WA[:, P * h:P * h + P], cpe[0:NOPE, 0, P * h:P * h + P], Y[0:NOPE, h, PT:T])
                e.then_inc(S("ql_ps"), 1)
                for b in range(DB):
                    e = tr(WB[0:DT, P * b:P * b + P], kvn[:, PT + DT * b:PT + DT * b + DT])
                e.then_inc(S("ql_ps"), 1)
                pe.wait_ge(S("ql"), 3 * (l + 1))
                for b in range(DB + 2):
                    if b < DB:
                        sample_scores(l, b)
                    if b >= 2:
                        sample_out(l, b - 2)
                    if 1 <= b < DB + 1:
                        sample_turn(l, b - 1)
                pe.wait_ge(S("ol_taken"), (l + 1) * DB)
                for h in range(HM):
                    e = mm(WA[0:VH, P * h:P * h + P], wA[:, 512 + VH * h:512 + VH * h + VH], OL[:, h, :])
                e.then_inc(S("oas"), 1)
                pe.wait_ge(S("ob_split"), HG * (l + 1))
                pe.wait_ge(S("oas_taken"), l + 1)
                for n in range(KD):
                    tile(t0 + T_OUT + n, [(g0 + P_OUT + n, k * P) for k in range(KD)], Hh, Hl)
                norm_sum(n0 + N_MIXPOST, WA)
                for hf in range(2):
                    for i in range(2 * FH):
                        tile(t0 + T_UP[hf] + i, [(g0 + P_UP[hf] + i, k * P) for k in range(KD)], Hh, Hl,
                             (lambda k: pe.wait_ge(S("hl"), l * SPLITS + KD + 2 + k + 1)) if hf == i == 0 else None)
                        if hf == 0 and i == 1:
                            norm_sum(n0 + N_FFNPRE, WA)
                    for n in range(KD):
                        tile(t0 + T_DOWN[hf] + n,
                             [(g0 + P_DOWN[hf] + (FH * n + k) // 8, (FH * n + k) % 8 * P) for k in range(FH)], gh, gl,
                             (lambda k: pe.wait_ge(S("gl"), l * KF + hf * FH + k + 1)) if n == 0 else None)
                norm_sum(n0 + N_FFNPOST, WA)
            norm_sum(DEPTH * N_NORM, WA)

        @block.scalar
        def _(act):
            count, last = {}, []

            def did(ins, name, at=None):
                count[name] = at or count.get(name, 0) + 1
                last[:] = [name]
                ins.then_inc(S(name), 1)

            def prev():
                if last:
                    act.wait_ge(S(last[0]), count[last[0]])

            def f(*args, **kw):
                prev()
                return act.activation(*args, **kw)

            def step(ins):
                did(ins, "act")

            act.dma_start(cols[:, :, :], a["cols"]).then_inc(S("cols_in"), 16)
            for k in range(KD):
                act.dma_start(X[:, k, :], a["xT"][k]).then_inc(S(f"x_in{k}"), 16)
            for t_, name in ((ones, "ones"), (ident, "ident"), (mask_f, "masks"), (reset_f, "reset"),
                             (rope, "rope"), (ind, "ind")):
                act.dma_start(t_[:, :] if len(t_.shape) == 2 else t_[:, :, :], a[name]).then_inc(S("const"), 16)
            act.wait_ge(S("cols_in"), 16)
            def exp_table():
                act.preload_act_table_set("natural_log_exp_and_others")

            def square_x(n, k, src):
                c = squares(n) + k
                if c >= 2:
                    act.wait_ge(S("sq_added"), c - 1)
                did(f(sq[:, c % 2, :], src, ACT.Square), "sq")

            def rstd(n, ps, width, dst):
                act.wait_ge(S("ssum"), n + 1)
                used, before = ("R_used", outer(n)) if dst is R else ("R2_used", inner(n))
                if before:
                    act.wait_ge(S(used), before)
                step(f(two(dst[:, :]), halves(ps), ACT.Ln, scale=1.0 / width, bias=eps[:, 0:1]))
                did(f(dst[:, :], dst[:, :], ACT.Exp, scale=-0.5), "rstd")

            def split_x(l, n, c_w, ready):
                for k in range(KD):
                    ready(k)
                    did(f(Hh[:, k, :], X[:, k, :], ACT.Copy, scale=cols[:, l, c_w + k:c_w + k + 1]), "hh")
                for k in range(KD):
                    square_x(n, k, X[:, k, :])

            def hi_part(n, dst, src):
                act.wait_ge(S("hf"), n + 1)
                did(f(dst, src, ACT.Copy), "hh")

            def take(tt, dst, src=None, func=ACT.Copy, **kw):
                act.wait_ge(S("tile"), tt + 1)
                return f(dst, halves(G[tt % 2]) if src is None else src, func, **kw)

            def evac(tt, ins):
                did(ins, f"evac{tt % 2}", slot_use(tt))

            for l in range(DEPTH):
                t0, n0 = l * TILES, l * N_NORM
                if l == 0:
                    split_x(l, n0 + N_MIXPRE, C_MIXPRE, lambda k: act.wait_ge(S(f"x_in{k}"), 16))
                    act.wait_ge(S("lbd"), 1)
                    did(f(lbs[:, 1, 0, :], lbs[:, 0, 0, :], ACT.Sigmoid), "lb_sig")
                    did(f(lbs[:, 1, 1, :], lbs[:, 0, 0, :], ACT.Sigmoid, scale=-1.0), "lb_sig")
                else:
                    split_x(l, n0 + N_MIXPRE, C_MIXPRE, lambda k: act.wait_ge(S("x"), (2 * l - 1) * KD + k + 1))
                exp_table()
                rstd(n0 + N_MIXPRE, WA, D, R)
                act.dma_start(wA[:, :], a["wA"][l]).then_inc(S("wA_in"), 16)
                for i in range(2):
                    act.dma_start(S0[:, i, :], a["s0"][l, i]).then_inc(S(f"s0_in{i}"), 16)
                for i, src in enumerate((DE[:, 0, :], DE[:, 1, :], kvn[:, :])):
                    n, k = (n0 + N_CQ, i) if i < 2 else (n0 + N_CKV, 0)
                    act.wait_ge(S(f"evac{(t0 + i) % 2}"), slot_use(t0 + i))
                    square_x(n, k, src)
                rstd(n0 + N_CQ, WA, QL, R2)
                for k in range(2):
                    hi_part(2 * l + k, cqh[:, k, :], tmp[:, k, :])
                rstd(n0 + N_CKV, WA, KL, R2)
                act.wait_ge(S("kvn"), l + 1)
                act.dma_start(a["o_kv"][l], kvn[:, :]).then_inc(S("out"), 16)
                act.wait_ge(S("kpe"), l + 1)
                act.dma_start(a["o_kpe"][l], kpe[64:96, :]).then_inc(S("out"), 16)

                def gates(h):
                    n, th = l * HG + h, t0 + T_HG + 4 * h
                    act.wait_ge(S(f"evac{(th + 2) % 2}"), slot_use(th + 2))
                    act.wait_ge(S(f"evac{(th + 3) % 2}"), slot_use(th + 3))
                    if n:
                        act.wait_ge(S("gated"), 2 * n)
                    act.wait_ge(S("hl"), l * SPLITS + KD + 2)
                    did(f(hG(h), hk(h), ACT.Sigmoid), "act")
                    did(f(hk(h), hk(h), ACT.Sigmoid, scale=-1.0), "sig")
                    did(f(tmp[:, 0, :], hq(h), ACT.Sigmoid), "sig")
                    did(f(tmp[:, 1, :], gate[:, h % 2, :], ACT.Sigmoid), "sig")
                    exp_table()
                    did(f(hG(h), hG(h), ACT.Ln, scale=lbs[:, l, 1, h:h + 1], bias=lbs[:, l, 0, h:h + 1]), "gl_")

                def q_nope(h):
                    tt = t0 + T_UQ + h
                    act.wait_ge(S("tile"), tt + 1)
                    did(f(two(Y[0:64, h, :]), halves(G[tt % 2], p1=64), ACT.Copy, scale=SCALE), "q_nope")

                gates(0)
                for h in range(HG):
                    n = l * HG + h
                    for lv in range(LV - 1):
                        act.wait_ge(S("D"), n * LV + lv + 1)
                        d = span(DE[:, lv % 2, :], LEVELS[lv])
                        did(f(d, d, ACT.Exp), "E")
                        if h == HG - 1 and lv in (0, 2, 4):
                            q_nope(lv // 2)
                            if lv == 4:
                                q_nope(3)
                    act.wait_ge(S("Z"), n * (LV - 1) + LV - 2)
                    did(f(DE[:, 1, :], hG(h), ACT.Exp), "E")
                    act.wait_ge(S("D"), n * LV + LV)
                    did(f(DE[:, 0, :], DE[:, 0, :], ACT.Exp), "E")
                    for ps, tok, name in ((WA, vtok, "v_turned"), (WB, ktok, "k_turned")):
                        act.wait_ge(S(name), n + 1)
                        did(f(tok[:, 0:640], ps[:, 0:640], ACT.Copy), "act")
                        did(f(tok[0:META, 640:768], ps[0:META, 640:768], ACT.Copy), "tok")
                    if h + 1 < HG:
                        gates(h + 1)
                    act.wait_ge(S("o"), n + 1)
                    act.dma_start(a["o_pst"][l, h], st[:, 4, :]).then_inc(S("pst_out"), 16)
                    c = squares(n0 + N_HG + h)
                    act.wait_ge(S("sq_added"), c - 1)
                    did(f(sq[:, c % 2, META:PT], WA[:, 0:512], ACT.Square), "act")
                    did(f(sq[:, c % 2, 0:META], WA[:, 512:512 + META], ACT.Square), "act")
                    did(f(sq[:, c % 2, PT:T], WA[:, 640:640 + SAMP], ACT.Square), "sq")
                    rstd(n0 + N_HG + h, WB, P, R2)
                    act.wait_ge(S("s0_new"), n + 1)
                    act.dma_start(a["o_sst"][l, h], S0[:, h % 2, :]).then_inc(S(f"sst_out{h % 2}"), 16)
                    if 1 <= h < HG - 1:
                        act.wait_ge(S(f"sst_out{(h - 1) % 2}"), 16 * (2 * l + (h - 1) // 2 + 1))
                        act.dma_start(S0[:, (h - 1) % 2, :], a["s0"][l, h + 1]).then_inc(S(f"s0_in{(h - 1) % 2}"), 16)
                for h in range(HG):
                    act.wait_ge(S("ob"), l * HG + h + 1)
                    did(f(Hh[:, 4 + h, :], ob[:, h, :], ACT.Copy), "obh")
                act.dma_start(Y[96:100, :, :], a["qrows"]).then_inc(S("maskrows"), 16)
                for h in range(HG, HM):
                    q_nope(h)
                act.wait_ge(S("sst_out0"), 16 * 2 * (l + 1))
                act.wait_ge(S("sst_out1"), 16 * 2 * (l + 1))
                act.wait_ge(S("pst_out"), 16 * HG * (l + 1))
                act.dma_start(KT[96:100, :, :], a["krows"]).then_inc(S("maskrows"), 16)
                for p in range(HM // 2):
                    tt = t0 + T_UK + p
                    act.wait_ge(S("tile"), tt + 1)
                    did(f(two(KT[0:64, 2 * p, :], PT // 2), halves(G[tt % 2], PT // 2, 0, 64), ACT.Copy), "act")
                    evac(tt, f(two(KT[0:64, 2 * p + 1, :], PT // 2), halves(G[tt % 2], PT // 2, 64, P), ACT.Copy))
                did(f(KT[64:96, :, :], kpe[64:96, 0:PT].rearrange("p (a n) -> p a n", a=1).broadcast_to([32, HM, PT]),
                  ACT.Copy), "kt")
                for b in range(2):
                    act.dma_start(ckT[:, b, :], a["ckT"][l, b]).then_inc(S(f"ck_in{b}"), 16)
                    act.dma_start(cpe[64:96, b, :], a["cpe"][l, b]).then_inc(S(f"ck_in{b}"), 16)
                act.dma_start(cpe[0:NOPE, 0, :], a["wB"][l]).then_inc(S("wB_in"), 16)
                for u in range(NU + 3):
                    if u < NU:
                        j = UNITS[u][1]
                        n = unit_keys(j)
                        act.wait_ge(S("max"), l * NU + u + 1)
                        if u >= 4:
                            act.wait_ge(S("turned"), l * NU + u - 3)
                        if j < 0:
                            did(f(Pp(0)[0:META, 0:P], Pp(0)[0:META, 0:P], ACT.Exp), "exp")
                        else:
                            did(f(Pp(u)[:, 0:n], (WA, G[0])[u % 2][:, 0:n], ACT.Exp,
                                  bias=mx[:, u % 4, 0:1], accum_out=mx[:, u % 4, 1:2]), "exp")
                    if u >= 3:
                        v = u - 3
                        j = UNITS[v][1]
                        act.wait_ge(S("turned"), l * NU + v + 1)
                        if v >= 2:
                            act.wait_ge(S("oa"), l * NU + v - 1)
                        w, rows = (META, P * (j + 2)) if j < 0 else (P, P * (j + 2))
                        did(f(Pt[0:w, v % 2, 0:rows], (WB, G[1])[v % 2][0:w, 0:rows], ACT.Copy), "Pt")
                act.wait_ge(S("oa"), (l + 1) * NU)
                for b in range(2):
                    act.dma_start(ctok[:, b, :], a["ctok"][l, b]).then_inc(S(f"ct_in{b}"), 16)
                act.wait_ge(S("ql_ps"), 2 * l + 1)
                did(f(ql[:, :, :].rearrange("p b (h t) -> p h b t", t=DT),
                  WA[:, :].rearrange("p (h b t) -> p h b t", h=HM, t=DT), ACT.Copy), "ql")
                did(f(qpe.rearrange("p (b h t) -> p h b t", h=HM, t=DT),
                  Y[64:96, :, PT:T].rearrange("p h (b t) -> p h b t", t=DT), ACT.Copy), "ql")
                act.wait_ge(S("ql_ps"), 2 * l + 2)
                act.wait_ge(S("ql"), 3 * l + 2)
                did(f(ntok[:, :], WB[0:DT, :], ACT.Copy), "ql")
                for b in range(DB + 1):
                    if b < DB:
                        sl = b % 2
                        act.wait_ge(S("s_max"), l * DB + b + 1)
                        if b >= 2:
                            act.wait_ge(S("s_turned"), 3 * (l * DB + b - 1))
                        step(f(Ps[:, sl, 0:PAST], (WA, G[0])[sl][:, :], ACT.Exp,
                               bias=ms[:, sl, 3:4], accum_out=ms[:, sl, 4:5]))
                        did(f(Ps[:, sl, PAST:PAST + DT], WB[:, 512 + DT * sl:512 + DT * sl + DT], ACT.Exp,
                          bias=ms[:, sl, 3:4], accum_out=ms[:, sl, 5:6]), "s_exp")
                        if b + 2 < DB:
                            act.dma_start(ckT[:, sl, :], a["ckT"][l, b + 2]).then_inc(S(f"ck_in{sl}"), 16)
                            act.dma_start(cpe[64:96, sl, :], a["cpe"][l, b + 2]).then_inc(S(f"ck_in{sl}"), 16)
                    if b >= 1:
                        v = b - 1
                        for x in range(2):
                            act.wait_ge(S("s_turned"), 3 * (l * DB + v) + x + 1)
                            if v and not x:
                                act.wait_ge(S("s_oa"), l * DB + v)
                                if v + 1 < DB:
                                    act.dma_start(ctok[:, (v - 1) % 2, :], a["ctok"][l, v + 1])\
                                        .then_inc(S(f"ct_in{(v - 1) % 2}"), 16)
                            did(f(Pts[:, 512 * x:512 * x + 512], G[1][:, 512 * x:512 * x + 512], ACT.Copy), "s_Pt")
                        act.wait_ge(S("s_turned"), 3 * (l * DB + v + 1))
                        act.wait_ge(S("s_Pt"), 3 * (l * DB + v) + 2)
                        did(f(Pts[0:DT, 8 * P:9 * P], WB[0:DT, 0:P], ACT.Copy), "s_Pt")
                act.wait_ge(S("out"), 32 * (l + 1))
                for n in range(KD):
                    tt = t0 + T_OUT + n
                    c = squares(n0 + N_MIXPOST) + n
                    act.wait_ge(S("sq_added"), c - 1)
                    did(take(tt, two(sq[:, c % 2, :]), func=ACT.Square), "sq")
                    evac(tt, f(two(Y[:, n, :]), halves(G[tt % 2]), ACT.Copy))
                rstd(n0 + N_MIXPOST, WA, D, R)
                split_x(l, n0 + N_FFNPRE, C_FFNPRE, lambda k: act.wait_ge(S("x"), 2 * l * KD + k + 1))
                act.dma_start(cst[:, :], a["cst"][l]).then_inc(S("cst_in"), 16)
                rstd(n0 + N_FFNPRE, WA, D, R)
                for hf in range(2):
                    for i in range(FH + 1):
                        ff_ = l * KF + hf * FH + i
                        if i >= 1:
                            act.wait_ge(S("gv"), ff_)
                            if hf and i == 1:
                                act.wait_ge(S("tile"), t0 + T_DOWN[0] + KD)
                            did(f(gh[:, i - 1, :], tmp[:, (ff_ - 1) % 2, :], ACT.Copy), "gh")
                        if i < FH:
                            act.wait_ge(S("conv"), ff_ + 1)
                            if ff_ >= 2:
                                act.wait_ge(S("gl"), ff_ - 1)
                            d = tmp[:, ff_ % 2, :]
                            did(f(d[:, 0:PT], cc[:, 0:PT], ACT.Silu), "act")
                            did(f(samples(d[:, PT:T]), samples(cc[:, 2 + PT:EXT], DT + 2)[:, :, 0:DT], ACT.Silu), "silu")
                    for n in range(KD):
                        tt = t0 + T_DOWN[hf] + n
                        if hf == 0:
                            evac(tt, take(tt, two(Y[:, n, :])))
                        else:
                            act.wait_ge(S("y2"), l * KD + n + 1)
                            square_x(n0 + N_FFNPOST, n, Y[:, n, :])
                exp_table()
                rstd(n0 + N_FFNPOST, WA, D, R)
                act.dma_start(a["o_conv"][l], cout[:, :, :]).then_inc(S("conv_out"), 16)
                act.wait_ge(S("conv_out"), 16 * (l + 1))
            for k in range(KD):
                act.wait_ge(S("x"), (2 * DEPTH - 1) * KD + k + 1)
                square_x(DEPTH * N_NORM, k, X[:, k, :])
            rstd(DEPTH * N_NORM, WA, D, R)
            for k in range(KD):
                act.wait_ge(S("y_out"), k + 1)
                act.dma_start(a["o_y"][k], Y[:, k, :]).then_inc(S("out"), 16)
            act.wait_ge(S("out"), 16 * (2 * DEPTH + KD))

        @block.vector
        def _(dve):
            count, last = {}, []

            def did(ins, name, at=None):
                count[name] = at or count.get(name, 0) + 1
                last[:] = [name]
                ins.then_inc(S(name), 1)

            def prev():
                if last:
                    dve.wait_ge(S(last[0]), count[last[0]])

            def op(kind):
                def go(*args, **kw):
                    prev()
                    return kind(*args, **kw)
                return go

            tt_, ts, stt, cp = (op(k) for k in (dve.tensor_tensor, dve.tensor_scalar, dve.scalar_tensor_tensor,
                                                dve.tensor_copy))
            scan, fill, keep, rmax, rsum, recip, mark = (op(k) for k in (
                dve.tensor_tensor_scan, dve.memset, dve.copy_predicated, dve.reduce_max, dve.reduce_sum,
                dve.reciprocal, dve.engine_nop))

            def step(ins):
                did(ins, "dve")

            def evac(tt, ins):
                did(ins, f"evac{tt % 2}", slot_use(tt))

            step(fill(eps[:, :], EPS))
            step(fill(Am[:, :], 0.0))
            step(fill(G[1][:, 256:512], 0.0))
            dve.wait_ge(S("cols_in"), 16)
            did(tt_(lbs[:, 0, 0, :], cols[:, 0, C_LB1:C_LB1 + HG], cols[:, 0, C_LB0:C_LB0 + HG], ALU.subtract), "lbd")

            def add_square(n, k, first):
                c = squares(n) + k
                dve.wait_ge(S("sq"), c + 1)
                if first:
                    if n:
                        dve.wait_ge(S("ssum"), n)
                    did(cp(acc[:, :], sq[:, c % 2, :]), "sq_added")
                else:
                    dve.wait_ge(S("sq_added"), c)
                    did(tt_(acc[:, :], acc[:, :], sq[:, c % 2, :], ALU.add), "sq_added")

            def col(l, c):
                return cols[:, l, c:c + 1]

            def split_cq(l):
                for k in range(2):
                    did(stt(tmp[:, k, :], DE[:, k, :], col(l, C_QN + k), R2[:, :], ALU.mult, ALU.mult), "hf")
                for k in range(2):
                    dve.wait_ge(S("hh"), l * SPLITS + KD + k + 1)
                    did(tt_(cql[:, k, :], tmp[:, k, :], cqh[:, k, :], ALU.subtract), "hl")

            def rest_of_x(l, base, c_w, k):
                dve.wait_ge(S("hh"), base + k + 1)
                did(stt(Hl[:, k, :], X[:, k, :], col(l, c_w + k), Hh[:, k, :], ALU.mult, ALU.subtract), "hl")

            def rotate(tt, dst, scale=1.0):
                ps = G[tt % 2]
                step(stt(two(tmp[64:96, 0, :]), halves(ps, HALF, 96, P), scale, two(rope[96:P, :]), ALU.mult, ALU.mult))
                evac(tt, stt(two(dst), halves(ps, HALF, 64, 96), scale, two(rope[64:96, :]), ALU.mult, ALU.mult))
                dve.wait_ge(S(f"evac{tt % 2}"), slot_use(tt))
                return tt_(dst, dst, tmp[64:96, 0, :], ALU.add)

            def residual(l, n, c_w, r, then):
                dve.wait_ge(S("rstd"), n + 1)
                for k in range(KD + 1):
                    if k < KD:
                        if k >= 2:
                            dve.wait_ge(S("x"), r * KD + k - 1)
                        did(stt(tmp[:, k % 2, :], Y[:, k, :], col(l, c_w + k), R[:, :], ALU.mult, ALU.mult), "dx")
                    if k >= 1:
                        then(k - 1)
                did(mark(), "R_used")

            def scaled(tt, dst):
                dve.wait_ge(S("tile"), tt + 1)
                evac(tt, tt_(two(dst), halves(G[tt % 2]), two(R[:, :]), ALU.mult))

            def hg_diff(l, h, lv):
                n, m, G_, d = l * HG + h, LEVELS[lv], hG(h), DE[:, lv % 2, :]
                g1, g2, ref = sub_halves(G_, m)
                d1, d2, _ = sub_halves(d, m)
                step(tt_(d1, ref, g1, ALU.subtract))
                did(tt_(d2, g2, ref, ALU.subtract), "D")

            def hg_decayed(l, h, lv):
                n, m = l * HG + h, LEVELS[lv]
                dve.wait_ge(S("E"), n * (LV + 1) + lv + 1)
                e1, e2, _ = sub_halves(DE[:, lv % 2, :], m)
                z1, z2, _ = sub_halves(Z[:, lv % 2, :], m)
                k1, _, _ = sub_halves(hk(h), m)
                _, q2, _ = sub_halves(hq(h), m)
                step(tt_(z1, k1, e1, ALU.mult))
                did(tt_(z2, q2, e2, ALU.mult), "Z")

            def hg_take(l, h, lv):
                n, m, bank = (l * HG + h) * LV + lv, LEVELS[lv], 512 * (lv % 2)
                dve.wait_ge(S("A"), n + 1)
                mk = masks[:, lv, :]
                if m <= 8:
                    step(keep(Am[:, 512:640], mk, WB[:, bank:bank + P]))
                    step(keep(Am[0:META, 640:640 + META], mk[0:META, 0:META],
                                             WB[0:META, bank + P:bank + P + META]))
                did(keep(Am[:, 0:512].rearrange("p (j t) -> p j t", j=4),
                                    mk.rearrange("p (a t) -> p a t", a=1).broadcast_to([P, 4, P]),
                                    WA[:, bank:bank + 512].rearrange("p (j t) -> p j t", j=4)), "A_taken")

            for l in range(DEPTH):
                t0, n0 = l * TILES, l * N_NORM
                if l == 0:
                    for k in range(KD):
                        rest_of_x(l, 0, C_MIXPRE, k)
                for k in range(KD):
                    add_square(n0 + N_MIXPRE, k, k == 0)
                if l == 0:
                    dve.wait_ge(S("const"), 16 * N_CONST)
                    step(cp(reset[:, :], reset_f))
                    step(cp(masks[:, :, :].rearrange("p (a b) t -> p a (b t)", a=2), mask_f))
                    dve.wait_ge(S("lb_sig"), 2)
                    step(fill(lbs[:, 0, 0, :], 0.0))
                    step(fill(lbs[:, 0, 1, :], 1.0))
                step(fill(Am[:, :], 0.0))
                dve.wait_ge(S("rstd"), n0 + N_MIXPRE + 1)
                for i, dst in enumerate((DE[:, 0, :], DE[:, 1, :], kvn[:, :])):
                    scaled(t0 + i, dst)
                add_square(n0 + N_CQ, 0, True)
                add_square(n0 + N_CQ, 1, False)
                dve.wait_ge(S("tile"), t0 + 4)
                step(rotate(t0 + 3, kpe[64:96, :]))
                did(tt_(kpe[64:96, :], kpe[64:96, :], R[64:96, :], ALU.mult), "kpe")
                scaled(t0 + T_HG, hv(0))
                dve.wait_ge(S("rstd"), n0 + N_CQ + 1)
                split_cq(l)
                did(mark(), "R2_used")
                add_square(n0 + N_CKV, 0, True)
                scaled(t0 + T_HG + 1, hk(0))
                scaled(t0 + T_HG + 2, hq(0))
                dve.wait_ge(S("rstd"), n0 + N_CKV + 1)
                did(stt(kvn[:, :], kvn[:, :], col(l, C_KVN), R2[:, :], ALU.mult, ALU.mult), "kvn")
                did(mark(), "R2_used")
                scaled(t0 + T_HG + 3, gate[:, 0, :])

                def gated(h):
                    n = l * HG + h
                    dve.wait_ge(S("sig"), 3 * (n + 1))
                    step(ts(hk(h), hk(h), lbs[:, l, 1, h:h + 1], None, ALU.mult))
                    did(tt_(hq(h), hq(h), tmp[:, 0, :], ALU.mult), "gated")
                    did(tt_(gate[:, h % 2, :], gate[:, h % 2, :], tmp[:, 1, :], ALU.mult), "gated")
                    dve.wait_ge(S("gl_"), n + 1)
                    step(scan(hG(h), reset[:, :], hG(h), 0.0, ALU.mult, ALU.add))

                def queries(h):
                    dve.wait_ge(S("q_nope"), l * HM + h + 1)
                    step(rotate(t0 + T_UQ + h, Y[64:96, h, :], SCALE))

                def finish(h):
                    dve.wait_ge(S("rstd"), n0 + N_HG + h + 1)
                    did(tt_(ob[:, h, :], ob[:, h, :], R2[:, :], ALU.mult), "ob")
                    did(mark(), "R2_used")

                gated(0)
                for h in range(HG):
                    n, th = l * HG + h, t0 + T_HG + 4 * (h + 1)
                    for i in range(LV + 2):
                        if i < LV - 1:
                            hg_diff(l, h, i)
                        if 1 <= i < LV:
                            hg_decayed(l, h, i - 1)
                        if i == LV - 1:
                            G_, d = hG(h), DE[:, 0, :]
                            step(tt_(d[:, 0:META], G_[:, META - 1:META].broadcast_to([P, META]), G_[:, 0:META],
                                     ALU.subtract))
                            for lo, hi_, w in ((META, PT, P), (PT, T, DT)):
                                g3 = G_[:, lo:hi_].rearrange("p (b t) -> p b t", t=w)
                                e = tt_(d[:, lo:hi_].rearrange("p (b t) -> p b t", t=w),
                                        g3[:, :, w - 1:w].broadcast_to([P, (hi_ - lo) // w, w]), g3, ALU.subtract)
                                did(e, "dve" if lo == META else "D")
                        if i in (1, 3, 5, 8) and h + 1 < HG:
                            x = (1, 3, 5, 8).index(i)
                            scaled(th + x, (hv(h + 1), hk(h + 1), hq(h + 1), gate[:, (h + 1) % 2, :])[x])
                        elif i in (1, 3, 5):
                            queries(i // 2)
                            if i == 5:
                                queries(3)
                        if i == 3 and h:
                            finish(h - 1)
                        if i >= 2:
                            hg_take(l, h, i - 2)
                    dve.wait_ge(S("E"), n * (LV + 1) + LV + 1)
                    did(tt_(hk(h), hk(h), DE[:, 0, :], ALU.mult), "kG")
                    did(tt_(hq(h), hq(h), DE[:, 1, :], ALU.mult), "qG")
                    dve.wait_ge(S("tok"), 2 * n + 1)
                    did(tt_(Z[:, :, :].rearrange("p a n -> p (a n)")[:, 0:DB * P].rearrange("p (b v) -> p b v", b=DB),
                            vtok[:, 512:640].rearrange("p (a v) -> p a v", a=1).broadcast_to([P, DB, P]),
                            ind[:, :].rearrange("p (b a) -> p b a", a=1).broadcast_to([P, DB, P]), ALU.mult), "v_apart")
                    if h + 2 == HG:
                        did(mark(), "R_used")
                    dve.wait_ge(S("dS"), n + 1)
                    if n:
                        dve.wait_ge(S("pst_out"), 16 * n)
                    did(cp(st[:, 0, :], WA[:, 512:640]), "state")
                    for j in range(4):
                        dve.wait_ge(S("state"), 5 * n + j + 1)
                        e_ = META + P * (j + 1) - 1
                        did(stt(st[:, j + 1, :], st[:, j, :], DE[:, 1, e_:e_ + 1], WA[:, P * j:P * j + P], ALU.mult, ALU.add), "state")
                    if h + 1 < HG:
                        gated(h + 1)
                    c = squares(n0 + N_HG + h)
                    dve.wait_ge(S("o"), n + 1)
                    dve.wait_ge(S("sq"), c + 1)
                    gt = gate[:, h % 2, :]
                    s3 = S0[:, h % 2, :].rearrange("p (b v) -> p b v", b=DB)
                    for (p0, p1), (a0, a1) in (((0, 512), (META, PT)), ((512, 512 + META), (0, META))):
                        step(stt(ob[:, h, a0:a1], WA[:, p0:p1], col(l, C_HGN), gt[:, a0:a1], ALU.mult, ALU.mult))
                    step(stt(ob[:, h, PT:T], WA[:, 640:640 + SAMP], col(l, C_HGN), gt[:, PT:T], ALU.mult, ALU.mult))
                    step(tt_(s3, s3, DE[:, 1, PT:T].rearrange("p (b t) -> p b t", t=DT)[:, :, DT - 1:DT]
                             .broadcast_to([P, DB, P]), ALU.mult))
                    dve.wait_ge(S("dS_sample"), n + 1)
                    did(tt_(S0[:, h % 2, :], S0[:, h % 2, :], WB[:, :], ALU.add), "s0_new")
                    c = squares(n0 + N_HG + h)
                    dve.wait_ge(S("sq"), c + 1)
                    dve.wait_ge(S("ssum"), n0 + N_HG + h)
                    did(mark(), "o_taken")
                    did(cp(acc[:, :], sq[:, c % 2, :]), "sq_added")
                finish(HG - 1)
                for h in range(HG):
                    dve.wait_ge(S("obh"), l * HG + h + 1)
                    did(tt_(Hl[:, 4 + h, :], ob[:, h, :], Hh[:, 4 + h, :], ALU.subtract), "ob_split")
                for h in range(HG, HM):
                    queries(h)
                for i in range(5):
                    dve.wait_ge(S("values"), 5 * l + i + 1)
                    ps = (WA, WA, WB, WB, WA)[i]
                    c = (0, 512, 0, 512, 0)[i]
                    np_ = P if i < 4 else META
                    did(cp(vt[0:np_, i, :], ps[0:np_, c:c + 512]), "vt")
                for u in range(NU + 4):
                    if u < NU:
                        j = UNITS[u][1]
                        ps = (WA, G[0])[u % 2]
                        dve.wait_ge(S("scores"), l * NU + u + 1)
                        if j < 0:
                            s3 = ps[0:META, 0:P].rearrange("p (h k) -> p h k", h=HM)
                            p3 = Pp(0)[0:META, 0:P].rearrange("p (h k) -> p h k", h=HM)
                            step(rmax(mxm[:, 0, :], s3, AX_X))
                            did(tt_(p3, s3, mxm[:, 0, :].rearrange("p (h a) -> p h a", a=1)
                                    .broadcast_to([META, HM, META]), ALU.subtract), "max")
                        else:
                            did(rmax(mx[:, u % 4, 0:1], ps[:, 0:unit_keys(j)], AX_X, negate=True), "max")
                    if 1 <= u < NU + 1:
                        v = u - 1
                        dve.wait_ge(S("exp"), l * NU + v + 1)
                        if v == 0:
                            step(rsum(mxm[:, 1, :], p3, AX_X))
                            step(recip(mxm[:, 2, :], mxm[:, 1, :]))
                            did(tt_(p3, p3, mxm[:, 2, :].rearrange("p (h a) -> p h a", a=1)
                                    .broadcast_to([META, HM, META]), ALU.mult), "probs_meta")
                        else:
                            did(recip(mx[:, v % 4, 2:3], mx[:, v % 4, 1:2]), "inv_sum")
                    if u >= 4:
                        v = u - 4
                        h, j = UNITS[v]
                        dve.wait_ge(S("oa"), l * NU + v + 1)
                        o = (WB, G[1])[v % 2][0:VH, 640:640 + P]
                        if j < 0:
                            for par in range(2):
                                rows = slice(64 * par, 64 * par + 64)
                                o4 = o.rearrange("p (g a t) -> p a g t", g=4, a=2)[:, par, :, :]
                                step(cp(Hh[rows, 0:4, 0:META], o4))
                                did(tt_(Hl[rows, 0:4, 0:META], o4, Hh[rows, 0:4, 0:META], ALU.subtract),
                                    "oa_taken" if par else "dve")
                        else:
                            rows, q0 = slice(64 * (h % 2), 64 * (h % 2) + 64), META + P * j
                            step(cp(Hh[rows, h // 2, q0:q0 + P], o))
                            did(tt_(Hl[rows, h // 2, q0:q0 + P], o, Hh[rows, h // 2, q0:q0 + P], ALU.subtract), "oa_taken")
                for b in range(DB + 2):
                    if b < DB:
                        sl = b % 2
                        m = ms[:, sl, :]
                        dve.wait_ge(S("s_scores"), l * DB + b + 1)
                        step(rmax(m[:, 1:2], WB[:, 512 + DT * sl:512 + DT * sl + DT], AX_X, negate=True))
                        step(rmax(m[:, 0:1], (WA, G[0])[sl][:, :], AX_X, negate=True))
                        did(tt_(m[:, 3:4], m[:, 0:1], m[:, 1:2], ALU.min), "s_max")
                        dve.wait_ge(S("s_exp"), l * DB + b + 1)
                        step(tt_(m[:, 6:7], m[:, 4:5], m[:, 5:6], ALU.add))
                        step(recip(m[:, 7:8], m[:, 6:7]))
                        did(ts(Ps[:, sl, :], Ps[:, sl, :], m[:, 7:8], None, ALU.mult), "s_probs")
                    if b >= 2:
                        v = b - 2
                        dve.wait_ge(S("s_oa"), l * DB + v + 1)
                        did(cp(OL[:, :, DT * v:DT * v + DT], WB[:, P:2 * P].rearrange("p (h t) -> p h t", h=HM)), "ol_taken")
                dve.wait_ge(S("oas"), l + 1)
                for par in range(2):
                    rows = slice(64 * par, 64 * par + 64)
                    o = WA[0:VH, :].rearrange("p (g a t) -> p a g t", g=4, a=2)[:, par, :, :]
                    step(cp(Hh[rows, 0:4, PT:T], o))
                    e = tt_(Hl[rows, 0:4, PT:T], o, Hh[rows, 0:4, PT:T], ALU.subtract)
                    if par == 0:
                        step(e)
                did(e, "oas_taken")
                for n in range(KD):
                    add_square(n0 + N_MIXPOST, n, n == 0)
                dve.wait_ge(S(f"evac{(t0 + T_OUT + KD - 1) % 2}"), slot_use(t0 + T_OUT + KD - 1))
                residual(l, n0 + N_MIXPOST, C_MIXPOST, 2 * l,
                         lambda k: rest_of_x(l, l * SPLITS + KD + 2, C_FFNPRE, k))
                for k in range(KD):
                    add_square(n0 + N_FFNPRE, k, k == 0)
                dve.wait_ge(S("rstd"), n0 + N_FFNPRE + 1)
                step(fill(ax[:, :, 0:2], 0.0))
                dve.wait_ge(S("cst_in"), 16 * (l + 1))
                for hf in range(2):
                    for i in range(FH + 1):
                        ff_ = l * KF + hf * FH + i
                        fc = hf * FH + i
                        if i < FH:
                            tt = t0 + T_UP[hf] + 2 * i
                            s_ = ax[:, ff_ % 2, :]
                            sv = samples(s_[:, 2 + PT:EXT], DT + 2)
                            step(cp(sv[:, :, 0:2], cst[:, 16 * fc:16 * fc + 16].rearrange("p (b t) -> p b t", t=2)))
                            dve.wait_ge(S("tile"), tt + 1)
                            ps = G[tt % 2]
                            step(tt_(s_[:, 2:2 + HALF], ps[:, 0:HALF], R[:, 0:HALF], ALU.mult))
                            step(tt_(s_[:, 2 + HALF:2 + PT], ps[:, 512:512 + PT - HALF], R[:, HALF:PT], ALU.mult))
                            evac(tt, tt_(sv[:, :, 2:], samples(ps[:, 512 + PT - HALF:512 + HALF]), samples(R[:, PT:T]),
                                         ALU.mult))
                            step(cp(cout[:, fc, 0:2], s_[:, PT:PT + 2]))
                            step(cp(cout[:, fc, 2:18].rearrange("p (b t) -> p b t", t=2), sv[:, :, DT:DT + 2]))
                            if ff_:
                                dve.wait_ge(S("silu"), ff_)
                            n_ = EXT - 2
                            step(ts(cc[:, 0:n_], s_[:, 0:n_], col(l, C_CW + fc), col(l, C_CB + fc), ALU.mult, ALU.add))
                            step(stt(cc[:, 0:n_], s_[:, 1:1 + n_], col(l, C_CW + KF + fc), cc[:, 0:n_], ALU.mult, ALU.add))
                            did(stt(cc[:, 0:n_], s_[:, 2:2 + n_], col(l, C_CW + 2 * KF + fc), cc[:, 0:n_], ALU.mult, ALU.add), "conv")
                        if i >= 1:
                            dve.wait_ge(S("gh"), ff_)
                            did(tt_(gl[:, i - 1, :], tmp[:, (ff_ - 1) % 2, :], gh[:, i - 1, :], ALU.subtract), "gl")
                        if i < FH:
                            tt = t0 + T_UP[hf] + 2 * i + 1
                            dve.wait_ge(S("silu"), ff_ + 1)
                            step(tt_(tmp[:, ff_ % 2, :], tmp[:, ff_ % 2, :], R[:, :], ALU.mult))
                            dve.wait_ge(S("tile"), tt + 1)
                            d = two(tmp[:, ff_ % 2, :])
                            step(tt_(d, halves(G[tt % 2]), d, ALU.mult))
                            did(mark(), "gv")
                            evac(tt, mark())
                    if hf:
                        did(mark(), "R_used")
                    for n in range(KD):
                        tt = t0 + T_DOWN[hf] + n
                        if hf:
                            dve.wait_ge(S("tile"), tt + 1)
                            step(tt_(two(Y[:, n, :]), two(Y[:, n, :]), halves(G[tt % 2]), ALU.add))
                            did(mark(), "y2")
                            evac(tt, mark())
                            add_square(n0 + N_FFNPOST, n, n == 0)
                if l + 1 < DEPTH:
                    residual(l, n0 + N_FFNPOST, C_FFNPOST, 2 * l + 1,
                             lambda k: rest_of_x(l + 1, (l + 1) * SPLITS, C_MIXPRE, k))
                else:
                    residual(l, n0 + N_FFNPOST, C_FFNPOST, 2 * l + 1,
                             lambda k: add_square(DEPTH * N_NORM, k, k == 0))
            dve.wait_ge(S("rstd"), DEPTH * N_NORM + 1)
            for k in range(KD):
                did(stt(Y[:, k, :], X[:, k, :], col(0, C_FIN + k), R[:, :], ALU.mult, ALU.mult), "y_out")


def layouts(x):
    f = np.float32
    ins = {}
    tokens = np.concatenate([x["meta_tokens"], x["x_prompt"][0], x["x_sample"].reshape(SAMP, D)], 0)
    ins["xT"] = tokens.T.reshape(KD, P, T)

    def blocks(w):
        k, n = w.shape
        return w.reshape(k // P, P, n // P, P).transpose(2, 1, 0, 3).reshape(n // P, P, k)

    in_cols = [np.arange(i * P, i * P + P) for i in range(3)]
    pe = QL + KL + np.arange(ROPE)
    swap = np.concatenate([pe[ROPE // 2:], pe[:ROPE // 2]])
    in_cols.append(np.concatenate([pe, pe, pe, swap]))
    base = QL + KL + ROPE
    for h in range(HG):
        for part in (2, 1, 0, 3):
            in_cols.append(base + part * HG * P + h * P + np.arange(P))
    in_cols = np.concatenate(in_cols)
    uq_cols = np.concatenate([h * (NOPE + ROPE) + np.concatenate(
        [np.arange(NOPE), NOPE + np.arange(ROPE), NOPE + ROPE // 2 + np.arange(ROPE // 2), NOPE + np.arange(ROPE // 2)])
        for h in range(HM)])
    stream = []
    for l in range(DEPTH):
        up = x["w_ffn_up"][l]
        av = np.stack([up[:, :FF].reshape(D, KF, P), up[:, FF:].reshape(D, KF, P)], 2).reshape(D, 2 * FF)
        uq = blocks(x["w_uq"][l][:, uq_cols])
        parts = [blocks(x["w_in"][l][:, in_cols]),
                 uq.reshape(2, 4, P, 256).transpose(0, 2, 1, 3).reshape(2, P, W_PIECE),
                 blocks(x["w_out"][l])]
        for hf in range(2):
            parts.append(blocks(av[:, hf * 2 * FH * P:(hf + 1) * 2 * FH * P]))
            dn = x["w_ffn_down"][l][hf * FH * P:(hf + 1) * FH * P].reshape(FH, P, KD, P)
            parts.append(dn.transpose(2, 0, 1, 3).reshape(FH, 8, P, P).transpose(0, 2, 1, 3).reshape(FH, P, W_PIECE))
        stream.append(np.concatenate(parts, 0))
    ins["wstream"] = np.stack(stream)
    ins["wA"] = np.concatenate([x["w_uk"].reshape(DEPTH, KL, 512), x["w_uv"].reshape(DEPTH, KL, 512)], 2)
    ins["wB"] = x["w_uk"].transpose(0, 3, 2, 1).reshape(DEPTH, NOPE, 1024)
    ins["ckT"] = x["cache_kv_latent"].transpose(0, 1, 3, 2)
    ins["cpe"] = x["cache_k_rope"].transpose(0, 1, 3, 2)
    ins["ctok"] = x["cache_kv_latent"].reshape(DEPTH, DB, PC, P, KL).transpose(0, 1, 3, 2, 4).reshape(DEPTH, DB, P, PAST)
    ins["s0"] = x["state_hgrn"].transpose(0, 2, 3, 1, 4).reshape(DEPTH, HG, P, DB * P)
    ins["cst"] = x["state_ffn_conv"].transpose(0, 3, 1, 2).reshape(DEPTH, KF, P, DB * 2).transpose(0, 2, 1, 3)\
        .reshape(DEPTH, P, KF * DB * 2)

    def col(v):
        return v.reshape(v.shape[0], -1, P)

    both = lambda v: np.stack([v, v])
    pack = np.concatenate([
        col(x["norm_mix_pre"]), col(x["norm_mix_post"]), col(x["norm_ffn_pre"]), col(x["norm_ffn_post"]),
        col(x["q_norm"]), col(x["kv_norm"]), col(x["hg_out_norm"]),
        both(x["hg_lower_bounds"][0].reshape(HG, P)), both(x["hg_lower_bounds"][1].reshape(HG, P)),
        both(x["final_norm"].reshape(KD, P)), col(x["ffn_conv_b"]), x["ffn_conv_w"].reshape(DEPTH, CONV * KF, P)], 1)
    ins["cols"] = pack.transpose(2, 0, 1)
    pos = np.concatenate([np.arange(PT) - META, PAST + np.tile(np.arange(DT), DB)]).astype(f)
    inv = f(10000.0) ** (-np.arange(ROPE // 2, dtype=f) / f(ROPE // 2))
    ang = (inv[:, None] * pos[None]).astype(f)
    tab = np.zeros((P, T), f)
    tab[64:80] = tab[80:96] = np.cos(ang)
    tab[96:112], tab[112:128] = -np.sin(ang), np.sin(ang)
    ins["rope"] = tab
    rs = np.ones((P, T), f)
    rs[:, [0] + [META + P * j for j in range(4)] + [PT + DT * b for b in range(DB)]] = 0
    ins["reset"] = rs
    s, t = np.arange(P)[:, None], np.arange(P)[None]
    ins["masks"] = np.stack([(s // (2 * m) == t // (2 * m)) & (s % (2 * m) < m) & (t % (2 * m) >= m) if m else s == t
                             for m in LEVELS], 1).astype(f).reshape(P, 2, -1)
    ins["ones"], ins["ident"] = np.ones((P, P), f), np.eye(P, dtype=f)
    ins["ind"] = (np.arange(P)[:, None] // DT == np.arange(DB)[None]).astype(f)
    q, k = np.zeros((4, T), f), np.zeros((4, PT), f)
    for j in range(4):
        q[j, META + P * j:META + P * j + CH] = 1
        k[j, META + P * j + CH:META + P * (j + 1)] = -BIG
    ins["qrows"] = np.repeat(q[:, None], HM, 1)
    ins["krows"] = np.repeat(k[:, None], HM, 1)
    return {n: np.ascontiguousarray(v) for n, v in ins.items()}


CONV = 3
OUTS = {
    "o_y": (KD, P, T), "o_kv": (DEPTH, P, T), "o_kpe": (DEPTH, ROPE, T), "o_pst": (DEPTH, HG, P, P),
    "o_sst": (DEPTH, HG, P, DB * P), "o_conv": (DEPTH, P, KF, 2 + DB * 2),
}


def kernel(**inputs):
    import concourse.bacc as bacc
    from concourse.bass_utils import run_bass_kernel_spmd

    arrays = {"in_" + n: v for n, v in layouts({k: np.asarray(v) for k, v in inputs.items()}).items()}
    nc = bacc.Bacc("TRN2", target_bir_lowering=False, num_devices=1)
    aps = {n[3:]: nc.dram_tensor(n, v.shape, mybir.dt.from_np(v.dtype), kind="ExternalInput").ap() for n, v in arrays.items()}
    for n, shape in OUTS.items():
        aps[n] = nc.dram_tensor(n, shape, F32, kind="ExternalOutput").ap()
    build(nc, aps)
    r = run_bass_kernel_spmd(nc, [arrays], core_ids=[0]).results[0]
    y = r["o_y"].reshape(D, T)
    kv, kpe, conv = r["o_kv"], r["o_kpe"], r["o_conv"]
    conv = conv.transpose(0, 2, 1, 3).reshape(DEPTH, FF, 2 + DB * 2)
    sst = r["o_sst"].reshape(DEPTH, HG, P, DB, P).transpose(0, 3, 1, 2, 4)

    def rows(v):
        v = v.transpose(0, 2, 1)
        return v[:, None, :PT], v[:, PT:].reshape(DEPTH, DB, DT, -1)

    (pkv, skv), (ppe, spe) = rows(kv), rows(kpe)
    out = (y[:, META:PT].T[None], y[:, PT:].T.reshape(DB, DT, D), pkv, ppe, r["o_pst"][:, None],
           conv[:, :, :2].transpose(0, 2, 1)[:, None], skv, spe, sst,
           conv[:, :, 2:].reshape(DEPTH, FF, DB, 2).transpose(0, 2, 3, 1))
    return tuple(np.ascontiguousarray(o) for o in out)
```

```python
from contextlib import ExitStack

import numpy as np

import concourse.bass as bass
from concourse import mybir

F32 = mybir.dt.float32
F32R = mybir.dt.float32r
U8 = mybir.dt.uint8
BF16 = mybir.dt.bfloat16
ALU = mybir.AluOpType
ACT = mybir.ActivationFunctionType
AX_X = mybir.AxisListType.X

P = 128
D = 1024
KD = D // P
DEPTH = 2
META = 16
SEQ = 512
DB, DT = 8, 16
SAMP = DB * DT
PT = META + SEQ
T = PT + SAMP
HALF = T // 2
PAST = 1024
PC = PAST // P
CH = 64
HM, NOPE, ROPE, VH = 8, 64, 32, 64
QL, KL = 256, 128
HG = 4
FF = 2816
KF = FF // P
FH = KF // 2
EPS = 1e-6
SCALE = float(NOPE + ROPE) ** -0.5
BIG = float(2.0 ** 100)
EXT = PT + 2 + DB * (DT + 2)
LEVELS = [64, 32, 16, 8, 4, 2, 1, 0]

W_PIECE = 1024
N_IN, N_UQ, N_OUT, N_UP, N_DOWN = 20, 2, KD, 2 * FH, FH
PIECES = N_IN + N_UQ + N_OUT + 2 * (N_UP + N_DOWN)
P_UQ = N_IN
P_OUT = P_UQ + N_UQ
P_UP = [P_OUT + N_OUT, P_OUT + N_OUT + N_UP + N_DOWN]
P_DOWN = [p + N_UP for p in P_UP]
RAW, SPL = 2, 3

T_HG = 4
T_UQ = T_HG + 4 * HG
T_UK = T_UQ + HM
T_OUT = T_UK + HM // 2
T_UP = [T_OUT + KD, T_OUT + KD + 2 * FH + KD]
T_DOWN = [t + 2 * FH for t in T_UP]
TILES = T_DOWN[1] + KD

C_MIXPRE, C_MIXPOST, C_FFNPRE, C_FFNPOST = 0, 8, 16, 24
C_QN, C_KVN, C_HGN, C_LB0, C_LB1, C_FIN, C_CB, C_CW = 32, 34, 35, 36, 40, 44, 52, 74
NCOL = C_CW + 3 * KF


def build(nc, a):
    ctx = ExitStack()
    sems = {}

    def sb(stack, name, shape, dt=F32):
        return stack.enter_context(nc.sbuf_tensor(name, shape, dt))

    with ctx:
        def S(name):
            if name not in sems:
                sems[name] = ctx.enter_context(nc.semaphore(name))
            return sems[name]

        X = sb(ctx, "X", [P, KD, T])
        Y = sb(ctx, "Y", [P, KD, T])
        Hh = sb(ctx, "Hh", [P, KD, T], F32R)
        Hl = sb(ctx, "Hl", [P, KD, T], F32R)
        wraw = sb(ctx, "wraw", [P, RAW, W_PIECE])
        whi = sb(ctx, "whi", [P, SPL, W_PIECE], F32R)
        wlo = sb(ctx, "wlo", [P, SPL, W_PIECE], F32R)
        ones = sb(ctx, "ones", [P, P])
        ident = sb(ctx, "ident", [P, P])
        masks = sb(ctx, "masks", [P, len(LEVELS), P], U8)
        reset = sb(ctx, "reset", [P, T], BF16)
        rope = sb(ctx, "rope", [P, T])
        cols = sb(ctx, "cols", [P, DEPTH, NCOL])
        ind = sb(ctx, "ind", [P, DB])
        lbs = sb(ctx, "lbs", [P, DEPTH, 2, HG])
        zero = sb(ctx, "zero", [P, 1])
        eps = sb(ctx, "eps", [P, 1])
        mask_f = Y[:, 0:2, 0:P * len(LEVELS) // 2]
        reset_f = Y[:, 2, :]
        acc = sb(ctx, "acc", [P, T])
        sq = sb(ctx, "sq", [P, 2, T])
        R = sb(ctx, "R", [P, T])
        R2 = sb(ctx, "R2", [P, T])
        tmp = sb(ctx, "tmp", [P, 2, T])

        mix = ExitStack()
        kvn = sb(mix, "kvn", [P, T])
        kpe = sb(mix, "kpe", [P, T])
        ob = sb(mix, "ob", [P, HG, T])
        wA = sb(mix, "wA", [P, 1024])
        hg = ExitStack()
        cqh = sb(hg, "cqh", [P, 2, T], F32R)
        cql = sb(hg, "cql", [P, 2, T], F32R)
        gate = sb(hg, "gate", [P, 2, T])
        DE = sb(hg, "DE", [P, 2, T])
        Z = sb(hg, "Z", [P, 2, T])
        Am = sb(hg, "Am", [P, 6 * P])
        vtok = sb(hg, "vtok", [P, 6 * P])
        ktok = sb(hg, "ktok", [P, 6 * P])
        st = sb(hg, "st", [P, 5, P])
        S0 = sb(hg, "S0", [P, 2, DB * P])
        dec = sb(hg, "dec", [P, DB])
        hg.close()
        att = ExitStack()
        ckT = sb(att, "ckT", [P, 2, PAST])
        cpe = sb(att, "cpe", [P, 2, PAST])
        pr = ExitStack()
        KT = sb(pr, "KT", [P, HM, PT])
        vt = sb(pr, "vt", [P, 5, HM * VH])
        Pp_ = sb(pr, "Pp", [P, 3, PT])
        Pt = sq
        mx = sb(pr, "mx", [P, 4, 4])
        mxm = sb(pr, "mxm", [META, 3, HM])
        pr.close()
        sa = ExitStack()
        ctok = sb(sa, "ctok", [P, 2, PAST])
        Ps = sb(sa, "Ps", [P, 2, PAST + DT])
        Pts = sb(sa, "Pts", [P, 9 * P])
        OL = sb(sa, "OL", [P, HM, SAMP])
        ms = sb(sa, "ms", [P, 2, 8])
        ql = tmp[:, :, :].rearrange("p a n -> p (a n)")[:, 0:DB * HM * DT]
        ntok = cpe[0:DT, 1, :]

        def qpe(b):
            return (acc, R)[b // 4][64:96, P * (b % 4):P * (b % 4) + P]

        sa.close()
        att.close()
        mix.close()
        ff = ExitStack()
        gh = sb(ff, "gh", [P, FH, T], F32R)
        gl = sb(ff, "gl", [P, FH, T], F32R)
        ax = sb(ff, "ax", [P, 2, EXT])
        cc = sb(ff, "cc", [P, EXT])
        cst = sb(ff, "cst", [P, KF * DB * 2])
        cout = sb(ff, "cout", [P, KF, 2 + DB * 2])
        ff.close()

        def pb(name):
            return ctx.enter_context(nc.psum_tensor(name, [P, 1024], F32))

        G = [pb("G0"), pb("G1")]
        WA, WB = pb("WA"), pb("WB")

        def halves(ps, n=HALF, p0=0, p1=P):
            return ps[p0:p1, :].rearrange("p (a n) -> p a n", a=2)[:, :, 0:n]

        def two(ap, n=HALF):
            return ap.rearrange("p (a n) -> p a n", n=n)

        def samples(ap, w=DT):
            return ap.rearrange("p (b t) -> p b t", t=w)

        NORM_SQ = [KD, 2, 1, 1, 1, 1, 1, KD, KD, KD]
        N_NORM = len(NORM_SQ)
        N_MIXPRE, N_CQ, N_CKV, N_HG, N_MIXPOST, N_FFNPRE, N_FFNPOST = 0, 1, 2, 3, 7, 8, 9

        def squares(n):
            l, i = divmod(n, N_NORM)
            return l * sum(NORM_SQ) + sum(NORM_SQ[:i])

        def by_pe(n):
            return n % N_NORM in (N_MIXPRE, N_FFNPRE)

        adder = []
        for n in range(DEPTH * N_NORM + 1):
            for _ in range(NORM_SQ[n % N_NORM]):
                name = "sq_summed" if by_pe(n) else "sq_added"
                adder.append((name, sum(x[0] == name for x in adder) + 1))

        def sums(n):
            return sum(not by_pe(i) for i in range(n))

        def sq_free(c):
            return adder[c - 2]

        LV = len(LEVELS)
        SPLITS = 2 * KD + 2

        def slot_use(tt):
            return tt // 2 + 1

        def piece_end(g):
            l, p = divmod(g, PIECES)
            if p < N_IN:
                return "tile", l * TILES + p + 1
            if p < P_OUT:
                return "tile", l * TILES + T_UQ + 4 * (p - P_UQ) + 4
            if p < P_UP[0]:
                return "tile", l * TILES + T_OUT + p - P_OUT + 1
            for hf in range(2):
                if P_UP[hf] <= p < P_DOWN[hf]:
                    return "tile", l * TILES + T_UP[hf] + p - P_UP[hf] + 1
                if P_DOWN[hf] <= p < P_DOWN[hf] + N_DOWN:
                    i = p - P_DOWN[hf]
                    if i == N_DOWN - 1:
                        return "tile", l * TILES + T_DOWN[hf] + KD
                    return "w_mid", (2 * l + hf) * (N_DOWN - 1) + i + 1

        UNITS = [(0, -1)] + [(h, j) for h in range(HM) for j in range(4)]
        NU = len(UNITS)

        def Pp(u):
            return R2[:, 0:PT] if u % 4 == 3 else Pp_[:, u % 4, :]

        def unit_keys(j):
            return META + P * (j + 1)

        def sub_halves(t, m):
            v = t[:, 0:T] if m <= 8 else t[:, META:PT]
            v = v.rearrange("p (b m) -> p b m", m=2 * m)
            nb = v.shape[1]
            return v[:, :, 0:m], v[:, :, m:2 * m], v[:, :, m - 1:m].broadcast_to([P, nb, m])

        def span(t, m):
            return t[:, 0:T] if m <= 8 else t[:, META:PT]

        def hq(h): return Y[:, 4 * (h % 2) + 0, :]
        def hk(h): return Y[:, 4 * (h % 2) + 1, :]
        def hG(h): return Y[:, 4 * (h % 2) + 2, :]
        def hv(h): return Y[:, 4 * (h % 2) + 3, :]

        N_CONST = 6

        def outer(n):
            l, i = divmod(n, N_NORM)
            return 4 * l + (0 if i == 0 else i - N_MIXPOST + 1)

        def inner(n):
            l, i = divmod(n, N_NORM)
            return (N_MIXPOST - 1) * l + i - 1

        block = ctx.enter_context(nc.Block())

        @block.sync
        def _(sp):
            def latents(l, b):
                sp.wait_ge(S("s_exp"), l * DB + b - 1)
                sp.dma_start(ckT[:, b % 2, :], a["ckT"][l, b]).then_inc(S(f"ck_in{b % 2}"), 16)
                sp.dma_start(cpe[64:96, b % 2, :], a["cpe"][l, b]).then_inc(S(f"ck_in{b % 2}"), 16)

            for g in range(DEPTH * PIECES):
                if g % PIECES == P_OUT + 5:
                    l = g // PIECES
                    latents(l, 2)
                    for b in range(2, DB):
                        if b + 1 < DB:
                            latents(l, b + 1)
                        sp.wait_ge(S("s_oa"), l * DB + b - 1)
                        sp.dma_start(ctok[:, b % 2, :], a["ctok"][l, b]).then_inc(S(f"ct_in{b % 2}"), 16)
                if g >= RAW:
                    sp.wait_ge(S("w_split"), g - RAW + 1)
                sp.dma_start(wraw[:, g % RAW, :], a["wstream"][g // PIECES, g % PIECES])\
                    .then_inc(S(f"w_in{g % RAW}"), 16)
                if g == 0:
                    for k in range(1, KD, 2):
                        sp.dma_start(X[:, k, :], a["xT"][k]).then_inc(S(f"x_in{k}"), 16)
                if g == 1:
                    for t_, name in ((ones, "ones"), (ident, "ident"), (mask_f, "masks"), (reset_f, "reset"),
                                     (rope, "rope"), (ind, "ind")):
                        sp.dma_start(t_[:, :] if len(t_.shape) == 2 else t_[:, :, :], a[name]).then_inc(S("const"), 16)

        @block.gpsimd
        def _(pool):
            pool.memset(zero[:, :], 0.0).then_inc(S("zero"), 1)
            pool.wait_ge(S("zero"), 1)
            zb = zero[:, 0:1].broadcast_to([P, W_PIECE])

            def residual(r):
                for k in range(KD):
                    pool.wait_ge(S("dx"), r * KD + k + 1)
                    pool.tensor_tensor(X[:, k, :], X[:, k, :], tmp[:, k % 2, :], ALU.add).then_inc(S("x"), 1)

            def decay_state(l, h):
                n = l * HG + h
                pool.wait_ge(S("dec"), n + 1)
                pool.wait_ge(S("o"), n + 1)
                s3 = S0[:, h % 2, :].rearrange("p (b v) -> p b v", b=DB)
                pool.tensor_tensor(s3, s3, dec[:, :].rearrange("p (b a) -> p b a", a=1).broadcast_to([P, DB, P]),
                                   ALU.mult).then_inc(S("s0_decayed"), 1)

            def add_rotated(l, heads, g):
                pool.wait_ge(S("w_split"), g)
                if heads[0]:
                    pool.wait_ge(S("s0_decayed"), (l + 1) * HG)
                    if heads[0] > HG:
                        pool.wait_ge(S("ob_split"), (l + 1) * HG)
                else:
                    pool.wait_ge(S("s0_decayed"), (l + 1) * HG - 1)
                for h in heads:
                    tt = l * TILES + T_UQ + h
                    pool.wait_ge(S(f"evac{tt % 2}"), slot_use(tt))
                    pool.tensor_tensor(Y[64:96, h, :], Y[64:96, h, :], tmp[64:96, h % 2, :], ALU.add)\
                        .then_inc(S("rotated"), 1)
                    pool.wait_ge(S("rotated"), l * HM + h + 1)

            def split_out(l, heads):
                pool.wait_ge(S("tile"), l * TILES + T_UQ)
                for h in heads:
                    n = l * HG + h
                    pool.wait_ge(S("ob"), n + 1)
                    pool.tensor_tensor(Hh[:, 4 + h, :], ob[:, h, :], zero[:, 0:1].broadcast_to([P, T]), ALU.add)\
                        .then_inc(S("ob_hi"), 1)
                    pool.wait_ge(S("ob_hi"), n + 1)
                    pool.tensor_tensor(Hl[:, 4 + h, :], ob[:, h, :], Hh[:, 4 + h, :], ALU.subtract).then_inc(S("ob_split"), 1)

            def normalize(l):
                for u in range(1, NU):
                    n = unit_keys(UNITS[u][1])
                    pool.wait_ge(S("inv_sum"), l * (NU - 1) + u)
                    pp = Pp(u)[:, 0:n]
                    pool.tensor_tensor(pp, pp, mx[:, u % 4, 2:3].broadcast_to([P, n]), ALU.mult).then_inc(S("probs"), 1)

            for g in range(DEPTH * PIECES):
                l, i = divmod(g, PIECES)
                for h in range(HG):
                    if i == (T_HG + 11, T_HG + 15, P_UQ + 1, P_OUT + 2)[h]:
                        decay_state(l, h)
                if i == P_OUT:
                    add_rotated(l, range(HG), g)
                if i == P_OUT + 1:
                    split_out(l, range(HG - 1))
                if i == P_OUT + 2:
                    add_rotated(l, (HG, HG + 1), g)
                    split_out(l, [HG - 1])
                    add_rotated(l, (HG + 2, HG + 3), g)
                if i == P_OUT + 3:
                    pool.wait_ge(S("vt"), 5 * l + 1)
                    pool.wait_ge(S("w_split"), g)
                    for x in range(2):
                        if l or x:
                            pool.wait_ge(S("qpe"), 2 * l + x)
                        pool.tensor_copy((acc, R)[x][64:96, 0:512].rearrange("p (b h t) -> p h b t", h=HM, t=DT),
                                               Y[64:96, :, PT + 64 * x:PT + 64 * x + 64].rearrange("p h (b t) -> p h b t", t=DT))\
                            .then_inc(S("qpe"), 1)
                    pool.wait_ge(S("qpe"), 2 * l + 2)
                    normalize(l)
                if i == P_UP[0] + 2:
                    residual(2 * l)
                if l and i == 2:
                    residual(2 * l - 1)
                pool.wait_ge(S(f"w_in{g % RAW}"), 16 * (g // RAW + 1))
                if g >= SPL:
                    pool.wait_ge(S(piece_end(g - SPL)[0]), piece_end(g - SPL)[1])
                raw, hi, lo = wraw[:, g % RAW, :], whi[:, g % SPL, :], wlo[:, g % SPL, :]
                pool.tensor_tensor(hi, raw, zb, ALU.add).then_inc(S("w_hi"), 1)
                pool.wait_ge(S("w_hi"), g + 1)
                pool.tensor_tensor(lo, raw, hi, ALU.subtract).then_inc(S("w_split"), 1)
            residual(2 * DEPTH - 1)

        @block.tensor
        def _(pe):
            def mm(out, lhsT, rhs, start=True, stop=True):
                return pe.matmul(out, lhsT, rhs, start=start, stop=stop, skip_group_check=True)

            def tr(out, in_):
                n = in_.shape[0]
                return pe.transpose(out, in_, ident[0:n, 0:n])

            def norm_sum(n, ps):
                sem, c = adder[squares(n + 1) - 1]
                pe.wait_ge(S(sem), c)
                pe.wait_ge(S("rstd"), n)
                for x in range(2):
                    m = mm(ps[:, 512 * x:512 * x + HALF], ones[:, :], acc[:, HALF * x:HALF * x + HALF])
                m.then_inc(S("ssum"), 1)

            def square_sum(n, k):
                c = squares(n) + k
                if k == 0 and n == 0:
                    pe.wait_ge(S("const"), 16 * N_CONST)
                elif k == 0:
                    pe.wait_ge(S("rstd"), n)
                pe.wait_ge(S("sq"), c + 1)
                for x in range(2):
                    m = mm(WA[:, 512 * x:512 * x + HALF], ones[:, :], sq[:, c % 2, HALF * x:HALF * x + HALF],
                           k == 0, k == KD - 1)
                m.then_inc(S("sq_summed"), 1)

            def tile_free(tt):
                if tt >= 2:
                    pe.wait_ge(S(f"evac{tt % 2}"), slot_use(tt) - 1)

            def tile(tt, chunks, rh, rl, ready=None, part=None, after=None):
                lo, hi = part or (0, len(chunks))
                if lo == 0:
                    tile_free(tt)
                for i in range(lo, hi):
                    g, c, k = chunks[i]
                    pe.wait_ge(S("w_split"), g + 1)
                    if ready is not None:
                        ready(k)
                    wh, wl = whi[:, g % SPL, c:c + P], wlo[:, g % SPL, c:c + P]
                    last = i == len(chunks) - 1
                    for x in range(2):
                        o = G[tt % 2][:, 512 * x:512 * x + HALF]
                        cs = slice(HALF * x, HALF * x + HALF)
                        mm(o, wl, rh[:, k, cs], i == 0, False)
                        mm(o, wh, rh[:, k, cs], False, False)
                        m = mm(o, wh, rl[:, k, cs], False, last)
                    if last:
                        m.then_inc(S("tile"), 1)
                    if c + P == W_PIECE and len(chunks) == FH and not last:
                        m.then_inc(S("w_mid"), 1)
                    if after is not None:
                        after(k)

            def head_tile(l, h, i):
                g = l * PIECES + T_HG + 4 * h + i
                tile(l * TILES + T_HG + 4 * h + i, [(g, k * P, k) for k in range(KD)], Hh, Hl)

            def level(l, h, lv):
                n = (l * HG + h) * LV + lv
                m = LEVELS[lv]
                if m:
                    pe.wait_ge(S("Z"), (l * HG + h) * (LV - 1) + lv + 1)
                    zk = zq = Z[:, lv % 2, :]
                else:
                    zk, zq = hk(h), hq(h)
                if n >= 2:
                    pe.wait_ge(S("A_taken"), n - 1)
                if lv < 2 and (l or h):
                    pe.wait_ge(S("o_taken"), l * HG + h)
                bank = 512 * (lv % 2)
                for j in range(4):
                    cs = slice(META + P * j, META + P * j + P)
                    e = mm(WA[:, bank + P * j:bank + P * j + P], zk[:, cs], zq[:, cs])
                if m <= 8:
                    mm(WB[:, bank:bank + P], zk[:, PT:T], zq[:, PT:T])
                    e = mm(WB[0:META, bank + P:bank + P + META], zk[:, 0:META], zq[:, 0:META])
                e.then_inc(S("A"), 1)

            def to_tokens(ps, src):
                for j in range(4):
                    tr(ps[:, P * j:P * j + P], src[:, META + P * j:META + P * j + P])
                tr(ps[:, 512:512 + P], src[:, PT:T])
                return tr(ps[0:META, 640:640 + P], src[:, 0:META])

            def turns(l, h):
                n = l * HG + h
                tv = l * TILES + T_HG + 4 * h
                pe.wait_ge(S(f"evac{tv % 2}"), slot_use(tv))
                pe.wait_ge(S("A_taken"), (n + 1) * LV)
                to_tokens(WA, hv(h)).then_inc(S("v_turned"), 1)
                pe.wait_ge(S("kG"), n + 1)
                to_tokens(WB, hk(h)).then_inc(S("k_turned"), 1)

            def state_sums(l, h):
                n = l * HG + h
                pe.wait_ge(S("tok"), 2 * (n + 1))
                for j in range(4):
                    mm(WA[:, P * j:P * j + P], ktok[:, P * j:P * j + P], vtok[:, P * j:P * j + P])
                mm(WA[:, 512:512 + P], ktok[0:META, 640:640 + P], vtok[0:META, 640:640 + P]).then_inc(S("dS"), 1)
                pe.wait_ge(S("v_apart"), n + 1)
                for x in range(2):
                    e = mm(WB[:, 512 * x:512 * x + 512], ktok[:, 512:512 + P],
                           Z[:, :, :].rearrange("p a n -> p (a n)")[:, 512 * x:512 * x + 512])
                e.then_inc(S("dS_sample"), 1)

            def head_out(l, h):
                n = l * HG + h
                pe.wait_ge(S("state"), 5 * (n + 1))
                pe.wait_ge(S("qG"), n + 1)
                pe.wait_ge(S(f"s0_in{h % 2}"), 16 * (2 * l + h // 2 + 1))
                for j in range(4):
                    o = WA[:, P * j:P * j + P]
                    mm(o, vtok[:, P * j:P * j + P], Am[:, P * j:P * j + P], True, False)
                    mm(o, st[:, j, :], hq(h)[:, META + P * j:META + P * j + P], False, True)
                mm(WA[:, 512:512 + META], vtok[0:META, 640:640 + P], Am[0:META, 640:640 + META])
                mm(WA[:, 640:640 + SAMP], vtok[:, 512:512 + P], Am[:, 512:512 + P], True, False)
                for b in range(DB):
                    e = mm(WA[:, 640 + DT * b:640 + DT * b + DT], S0[:, h % 2, P * b:P * b + P],
                           hq(h)[:, PT + DT * b:PT + DT * b + DT], False, b == DB - 1)
                e.then_inc(S("o"), 1)

            def prompt_scores(l, u):
                h, j = UNITS[u]
                n = unit_keys(j)
                if u >= 2 or l:
                    pe.wait_ge(S("exp"), l * NU + u - 1 if u >= 2 else l * NU)
                ps = (WA, G[0])[u % 2]
                if j < 0:
                    for h in range(HM):
                        e = mm(ps[0:META, META * h:META * h + META], Y[0:100, h, 0:META], KT[0:100, h, 0:META])
                else:
                    for c in range(0, n, 512):
                        e = mm(ps[:, c:min(n, c + 512)], Y[0:100, h, META + P * j:META + P * j + P],
                               KT[0:100, h, c:min(n, c + 512)])
                e.then_inc(S("scores"), 1)

            def prompt_turn(l, u):
                h, j = UNITS[u]
                ps, pp = (WB, G[1])[u % 2], Pp(u)
                if j < 0:
                    pe.wait_ge(S("probs_meta"), l + 1)
                else:
                    pe.wait_ge(S("probs"), l * (NU - 1) + u)
                if u >= 2:
                    pe.wait_ge(S("oa_taken"), l * NU + u - 1)
                if j < 0:
                    for h in range(HM):
                        e = tr(ps[0:META, META * h:META * h + META], pp[0:META, META * h:META * h + META])
                else:
                    for c in range(j + 1):
                        tr(ps[:, P * c:P * c + P], pp[:, META + P * c:META + P * c + P])
                    e = tr(ps[0:META, P * (j + 1):P * (j + 2)], pp[:, 0:META])
                e.then_inc(S("turned"), 1)

            def prompt_out(l, u):
                h, j = UNITS[u]
                pe.wait_ge(S("Pt"), l * NU + u + 1)
                o, pt = (WB, G[1])[u % 2][0:VH, 640:640 + P], Pt[:, u % 2, :]
                if j < 0:
                    for h in range(HM):
                        e = mm(o[:, META * h:META * h + META], vt[0:META, 4, VH * h:VH * h + VH],
                               pt[0:META, META * h:META * h + META])
                else:
                    mm(o, vt[0:META, 4, VH * h:VH * h + VH], pt[0:META, P * (j + 1):P * (j + 2)], True, False)
                    for c in range(j + 1):
                        e = mm(o, vt[:, c, VH * h:VH * h + VH], pt[:, P * c:P * c + P], False, c == j)
                e.then_inc(S("oa"), 1)

            def sample_scores(l, b):
                pe.wait_ge(S(f"ck_in{b % 2}"), 32 * (l * DB // 2 + b // 2 + 1))
                if b >= 2:
                    pe.wait_ge(S("s_exp"), l * DB + b - 1)
                else:
                    pe.wait_ge(S("exp"), (l + 1) * NU - 1 + b)
                ps = (G[0], WA)[b % 2]
                for c in range(0, PAST, 512):
                    mm(ps[:, c:c + 512], ql[:, P * b:P * b + P], ckT[:, b % 2, c:c + 512], True, False)
                    e = mm(ps[:, c:c + 512], qpe(b), cpe[64:96, b % 2, c:c + 512], False, True)
                if b >= 2 and b % 2:
                    e.then_inc(S("s_scores"), 1)

            def new_scores(l, b):
                if b:
                    pe.wait_ge(S("s_exp"), l * DB + b)
                else:
                    pe.wait_ge(S("oa_taken"), (l + 1) * NU)
                for v in (b, b + 1):
                    cs = slice(PT + DT * v, PT + DT * v + DT)
                    new = WB[:, 512 + DT * (v % 2):512 + DT * (v % 2) + DT]
                    mm(new, ql[:, P * v:P * v + P], kvn[:, cs], True, False)
                    e = mm(new, qpe(v), kpe[64:96, cs], False, True)
                e.then_inc(S("s_scores"), 1)

            def sample_turn(l, b):
                pe.wait_ge(S("s_probs"), l * DB + b + 1)
                for x in range(2):
                    if b:
                        pe.wait_ge(S("s_Pt"), 3 * (l * DB + b - 1) + x + 1)
                    for c in range(4):
                        e = tr(G[1][:, 512 * x + P * c:512 * x + P * c + P],
                               Ps[:, b % 2, P * (4 * x + c):P * (4 * x + c) + P])
                    e.then_inc(S("s_turned"), 1)
                if b:
                    pe.wait_ge(S("s_Pt"), 3 * (l * DB + b))
                    pe.wait_ge(S("ol_taken"), l * DB + b)
                tr(WB[0:DT, 0:P], Ps[:, b % 2, PAST:PAST + DT]).then_inc(S("s_turned"), 1)

            def sample_out(l, b):
                pe.wait_ge(S("s_Pt"), 3 * (l * DB + b + 1))
                pe.wait_ge(S(f"ct_in{b % 2}"), 16 * (l * DB // 2 + b // 2 + 1))
                o = WB[:, P:2 * P]
                if b:
                    pe.wait_ge(S("ol_taken"), l * DB + b)
                mm(o, ntok[:, P * b:P * b + P], Pts[0:DT, 8 * P:9 * P], True, False)
                for c in range(PC):
                    e = mm(o, ctok[:, b % 2, P * c:P * c + P], Pts[:, P * c:P * c + P], False, c == PC - 1)
                e.then_inc(S("s_oa"), 1)

            for l in range(DEPTH):
                g0, t0, n0 = l * PIECES, l * TILES, l * N_NORM
                for i in range(T_HG):
                    tile(t0 + i, [(g0 + i, k * P, k) for k in range(KD)], Hh, Hl,
                         (lambda k: pe.wait_ge(S("hl"), l * SPLITS + k + 1)) if i == 0 else None,
                         after=(lambda k: square_sum(n0 + N_MIXPRE, k)) if i == 0 else None)
                head_tile(l, 0, 0)
                norm_sum(n0 + N_CQ, WA)
                head_tile(l, 0, 1)
                head_tile(l, 0, 2)
                norm_sum(n0 + N_CKV, WA)
                head_tile(l, 0, 3)
                head_tile(l, 1, 0)
                head_tile(l, 1, 1)
                pe.wait_ge(S("rstd"), n0 + N_CKV + 1)

                def queries(h):
                    g = g0 + P_UQ + h // 4
                    tile(t0 + T_UQ + h, [(g, 256 * (h % 4) + k * P, k) for k in range(2)], cqh, cql,
                         lambda k: pe.wait_ge(S("hl"), l * SPLITS + KD + 2))

                for h in range(HG):
                    for lv in range(LV):
                        level(l, h, lv)
                        if lv in (2, 5) and h + 1 < HG:
                            head_tile(l, h + 1, 2 + lv // 5)
                        if lv == 2 and h + 1 == HG:
                            queries(2)
                            queries(3)
                    turns(l, h)
                    state_sums(l, h)
                    head_out(l, h)
                    if h + 2 < HG:
                        head_tile(l, h + 2, 0)
                    else:
                        q = 0 if h + 2 == HG else HG
                        queries(q)
                        queries(q + 1)
                    pe.wait_ge(S("s0_new"), l * HG + h + 1)
                    norm_sum(n0 + N_HG + h, WB)
                    if h + 2 < HG:
                        head_tile(l, h + 2, 1)
                for h in range(HG + 2, HM):
                    queries(h)
                pe.wait_ge(S("wA_in"), 16 * (l + 1))
                pe.wait_ge(S("kvn"), l + 1)
                for p in range(HM // 2):
                    tt = t0 + T_UK + p
                    tile_free(tt)
                    for x in range(2):
                        e = mm(G[tt % 2][:, 512 * x:512 * x + PT // 2], wA[:, P * p:P * p + P],
                               kvn[:, PT // 2 * x:PT // 2 * x + PT // 2])
                    e.then_inc(S("tile"), 1)
                pe.wait_ge(S("ob"), l * HG + HG)
                for i in range(5):
                    cs = slice(META + P * i, META + P * i + P) if i < 4 else slice(0, META)
                    if i == 4:
                        pe.wait_ge(S("vt"), 5 * l + 1)
                    ps = (WA, WA, WB, WB, WA)[i]
                    c = (0, 512, 0, 512, 0)[i]
                    mm(ps[0:P if i < 4 else META, c:c + 512], kvn[:, cs], wA[:, 512:1024]).then_inc(S("values"), 1)
                pe.wait_ge(S("wB_in"), 16 * (l + 1))
                pe.wait_ge(S("q_nope"), HM * (l + 1))
                tile_free(t0 + T_OUT + 1)
                for h in range(HM):
                    e = mm(G[1][:, P * h:P * h + P], cpe[0:NOPE, 0, P * h:P * h + P], Y[0:NOPE, h, PT:T])
                e.then_inc(S("ql_ps"), 1)
                pe.wait_ge(S("vt"), 5 * (l + 1))
                for b in range(DB):
                    e = tr(WB[0:DT, P * b:P * b + P], kvn[:, PT + DT * b:PT + DT * b + DT])
                e.then_inc(S("ql_ps"), 1)

                def out_tile(n, part=None):
                    tile(t0 + T_OUT + n, [(g0 + P_OUT + n, k * P, k) for k in (4, 5, 6, 7, 0, 1, 2, 3)], Hh, Hl,
                         lambda k: pe.wait_ge(S("oas_taken"), l + 1) if k < 4 else pe.wait_ge(S("ob_split"), HG * (l + 1)),
                         part)

                pe.wait_ge(S("vt"), 5 * (l + 1))
                pe.wait_ge(S("maskrows"), 32 * (l + 1))
                tile_free(t0 + T_OUT)
                pe.wait_ge(S("ql"), l + 1)
                pe.wait_ge(S("ntok"), l + 1)
                pe.wait_ge(S("rotated"), HM * (l + 1))
                pe.wait_ge(S("qpe"), 2 * (l + 1))
                for u in range(NU + 4):
                    if u < NU:
                        prompt_scores(l, u)
                    if u >= 4:
                        prompt_out(l, u - 4)
                    if 3 <= u < NU + 3:
                        prompt_turn(l, u - 3)
                    if u in (NU, NU + 1):
                        sample_scores(l, u - NU)
                for b in range(DB + 2):
                    if b < DB:
                        if b >= 2:
                            sample_scores(l, b)
                        if b % 2 == 0:
                            new_scores(l, b)
                    if b >= 2:
                        sample_out(l, b - 2)
                    if 1 <= b < DB + 1:
                        sample_turn(l, b - 1)
                    if b == DB:
                        out_tile(0, (0, 4))
                pe.wait_ge(S("ol_taken"), (l + 1) * DB)
                for h in range(HM):
                    e = mm(WA[0:VH, P * h:P * h + P], wA[:, 512 + VH * h:512 + VH * h + VH], OL[:, h, :])
                e.then_inc(S("oas"), 1)
                out_tile(1, (0, 4))
                for n in range(2):
                    out_tile(n, (4, KD))
                for n in range(2, KD):
                    out_tile(n)
                norm_sum(n0 + N_MIXPOST, WA)
                for hf in range(2):
                    for i in range(2 * FH):
                        tile(t0 + T_UP[hf] + i, [(g0 + P_UP[hf] + i, k * P, k) for k in range(KD)], Hh, Hl,
                             (lambda k: pe.wait_ge(S("hl"), l * SPLITS + KD + 2 + k + 1)) if hf == i == 0 else None,
                             after=(lambda k: square_sum(n0 + N_FFNPRE, k)) if hf == i == 0 else None)
                    for n in range(KD):
                        tile(t0 + T_DOWN[hf] + n,
                             [(g0 + P_DOWN[hf] + (FH * n + k) // 8, (FH * n + k) % 8 * P, k) for k in range(FH)], gh, gl,
                             (lambda k: pe.wait_ge(S("gl"), l * KF + hf * FH + k + 1)) if n == 0 else None)
                norm_sum(n0 + N_FFNPOST, WA)
            for k in range(KD):
                square_sum(DEPTH * N_NORM, k)

        @block.scalar
        def _(act):
            count, last = {}, []

            def did(ins, name, at=None):
                count[name] = at or count.get(name, 0) + 1
                last[:] = [name]
                ins.then_inc(S(name), 1)

            def prev():
                if last:
                    act.wait_ge(S(last[0]), count[last[0]])

            def f(*args, **kw):
                prev()
                return act.activation(*args, **kw)

            def step(ins):
                did(ins, "act")

            act.dma_start(cols[:, :, :], a["cols"]).then_inc(S("cols_in"), 16)
            for k in range(0, KD, 2):
                act.dma_start(X[:, k, :], a["xT"][k]).then_inc(S(f"x_in{k}"), 16)
            act.wait_ge(S("cols_in"), 16)

            def exp_table():
                act.preload_act_table_set("natural_log_exp_and_others")

            def square_x(n, k, src):
                c = squares(n) + k
                if c >= 2:
                    act.wait_ge(S(sq_free(c)[0]), sq_free(c)[1])
                did(f(sq[:, c % 2, :], src, ACT.Square), "sq")

            def rstd(n, ps, width, dst):
                if by_pe(n):
                    act.wait_ge(S("sq_summed"), adder[squares(n + 1) - 1][1])
                else:
                    act.wait_ge(S("ssum"), sums(n) + 1)
                used, before = ("R_used", outer(n)) if dst is R else ("R2_used", inner(n))
                if before:
                    act.wait_ge(S(used), before)
                step(f(two(dst[:, :]), halves(ps), ACT.Ln, scale=1.0 / width, bias=eps[:, 0:1]))
                did(f(dst[:, :], dst[:, :], ACT.Exp, scale=-0.5), "rstd")

            def split_x(l, n, c_w, ready):
                for k in range(KD):
                    ready(k)
                    did(f(Hh[:, k, :], X[:, k, :], ACT.Copy, scale=cols[:, l, c_w + k:c_w + k + 1]), "hh")
                    square_x(n, k, X[:, k, :])

            def hi_part(n, dst, src):
                act.wait_ge(S("hf"), n + 1)
                did(f(dst, src, ACT.Copy), "hh")

            def take(tt, dst, src=None, func=ACT.Copy, **kw):
                act.wait_ge(S("tile"), tt + 1)
                return f(dst, halves(G[tt % 2]) if src is None else src, func, **kw)

            def evac(tt, ins):
                did(ins, f"evac{tt % 2}", slot_use(tt))

            for l in range(DEPTH):
                t0, n0 = l * TILES, l * N_NORM
                if l == 0:
                    split_x(l, n0 + N_MIXPRE, C_MIXPRE, lambda k: act.wait_ge(S(f"x_in{k}"), 16))
                    act.wait_ge(S("lbd"), 1)
                    did(f(lbs[:, 1, 0, :], lbs[:, 0, 0, :], ACT.Sigmoid), "lb_sig")
                    did(f(lbs[:, 1, 1, :], lbs[:, 0, 0, :], ACT.Sigmoid, scale=-1.0), "lb_sig")
                else:
                    split_x(l, n0 + N_MIXPRE, C_MIXPRE, lambda k: act.wait_ge(S("x"), (2 * l - 1) * KD + k + 1))
                exp_table()
                rstd(n0 + N_MIXPRE, WA, D, R)
                act.dma_start(wA[:, :], a["wA"][l]).then_inc(S("wA_in"), 16)
                for i in range(2):
                    act.dma_start(S0[:, i, :], a["s0"][l, i]).then_inc(S(f"s0_in{i}"), 16)
                for i, src in enumerate((DE[:, 0, :], DE[:, 1, :], kvn[:, :])):
                    n, k = (n0 + N_CQ, i) if i < 2 else (n0 + N_CKV, 0)
                    act.wait_ge(S(f"evac{(t0 + i) % 2}"), slot_use(t0 + i))
                    square_x(n, k, src)
                rstd(n0 + N_CQ, WA, QL, R2)
                for k in range(2):
                    hi_part(2 * l + k, cqh[:, k, :], tmp[:, k, :])
                rstd(n0 + N_CKV, WA, KL, R2)
                act.wait_ge(S("kvn"), l + 1)
                act.dma_start(a["o_kv"][l], kvn[:, :]).then_inc(S("out"), 16)
                act.wait_ge(S("kpe"), l + 1)
                act.dma_start(a["o_kpe"][l], kpe[64:96, :]).then_inc(S("out"), 16)

                def gates(h):
                    n, th = l * HG + h, t0 + T_HG + 4 * h
                    act.wait_ge(S(f"evac{(th + 2) % 2}"), slot_use(th + 2))
                    act.wait_ge(S(f"evac{(th + 3) % 2}"), slot_use(th + 3))
                    if n:
                        act.wait_ge(S("gated"), 2 * n)
                    act.wait_ge(S("hl"), l * SPLITS + KD + 2)
                    did(f(hG(h), hk(h), ACT.Sigmoid), "act")
                    did(f(hk(h), hk(h), ACT.Sigmoid, scale=-1.0), "sig")
                    did(f(tmp[:, 0, :], hq(h), ACT.Sigmoid), "sig")
                    did(f(tmp[:, 1, :], gate[:, h % 2, :], ACT.Sigmoid), "sig")
                    exp_table()
                    did(f(hG(h), hG(h), ACT.Ln, scale=lbs[:, l, 1, h:h + 1], bias=lbs[:, l, 0, h:h + 1]), "gl_")

                def q_nope(h):
                    tt = t0 + T_UQ + h
                    act.wait_ge(S("tile"), tt + 1)
                    did(f(two(Y[0:64, h, :]), halves(G[tt % 2], p1=64), ACT.Copy, scale=SCALE), "q_nope")

                gates(0)
                for h in range(HG):
                    n = l * HG + h
                    for lv in range(LV - 1):
                        act.wait_ge(S("D"), n * LV + lv + 1)
                        d = span(DE[:, lv % 2, :], LEVELS[lv])
                        did(f(d, d, ACT.Exp), "E")
                        if h == HG - 1 and lv in (0, 2, 4):
                            q_nope(lv // 2)
                            if lv == 4:
                                q_nope(3)
                    act.wait_ge(S("Z"), n * (LV - 1) + LV - 2)
                    did(f(DE[:, 1, :], hG(h), ACT.Exp), "E")
                    act.wait_ge(S("D"), n * LV + LV)
                    did(f(DE[:, 0, :], DE[:, 0, :], ACT.Exp), "E")
                    for ps, tok, name in ((WA, vtok, "v_turned"), (WB, ktok, "k_turned")):
                        act.wait_ge(S(name), n + 1)
                        did(f(tok[:, 0:640], ps[:, 0:640], ACT.Copy), "act")
                        did(f(tok[0:META, 640:768], ps[0:META, 640:768], ACT.Copy), "tok")
                    if h + 1 < HG:
                        gates(h + 1)
                    act.wait_ge(S("o"), n + 1)
                    act.dma_start(a["o_pst"][l, h], st[:, 4, :]).then_inc(S("pst_out"), 16)
                    c = squares(n0 + N_HG + h)
                    act.wait_ge(S(sq_free(c)[0]), sq_free(c)[1])
                    did(f(sq[:, c % 2, META:PT], WA[:, 0:512], ACT.Square), "act")
                    did(f(sq[:, c % 2, 0:META], WA[:, 512:512 + META], ACT.Square), "act")
                    did(f(sq[:, c % 2, PT:T], WA[:, 640:640 + SAMP], ACT.Square), "sq")
                    if h + 1 == HG:
                        q_nope(HG)
                        q_nope(HG + 1)
                    rstd(n0 + N_HG + h, WB, P, R2)
                    act.wait_ge(S("s0_new"), n + 1)
                    act.dma_start(a["o_sst"][l, h], S0[:, h % 2, :]).then_inc(S(f"sst_out{h % 2}"), 16)
                    if 1 <= h < HG - 1:
                        act.wait_ge(S(f"sst_out{(h - 1) % 2}"), 16 * (2 * l + (h - 1) // 2 + 1))
                        act.dma_start(S0[:, (h - 1) % 2, :], a["s0"][l, h + 1]).then_inc(S(f"s0_in{(h - 1) % 2}"), 16)
                act.dma_start(Y[96:100, :, :], a["qrows"]).then_inc(S("maskrows"), 16)
                for h in range(HG + 2, HM):
                    q_nope(h)
                act.wait_ge(S("sst_out0"), 16 * 2 * (l + 1))
                act.wait_ge(S("sst_out1"), 16 * 2 * (l + 1))
                act.wait_ge(S("pst_out"), 16 * HG * (l + 1))
                act.dma_start(KT[96:100, :, :], a["krows"]).then_inc(S("maskrows"), 16)
                act.wait_ge(S("ob"), l * HG + HG)
                for b in range(2):
                    act.dma_start(ckT[:, b, :], a["ckT"][l, b]).then_inc(S(f"ck_in{b}"), 16)
                    act.dma_start(cpe[64:96, b, :], a["cpe"][l, b]).then_inc(S(f"ck_in{b}"), 16)
                act.dma_start(cpe[0:NOPE, 0, :], a["wB"][l]).then_inc(S("wB_in"), 16)
                for p in range(HM // 2):
                    tt = t0 + T_UK + p
                    act.wait_ge(S("tile"), tt + 1)
                    did(f(two(KT[0:64, 2 * p, :], PT // 2), halves(G[tt % 2], PT // 2, 0, 64), ACT.Copy), "act")
                    evac(tt, f(two(KT[0:64, 2 * p + 1, :], PT // 2), halves(G[tt % 2], PT // 2, 64, P), ACT.Copy))
                act.wait_ge(S("ql_ps"), 2 * l + 2)
                did(f(ntok, WB[0:DT, :], ACT.Copy), "ntok")
                for u in range(NU + 3):
                    if u < NU:
                        j = UNITS[u][1]
                        n = unit_keys(j)
                        act.wait_ge(S("max"), l * NU + u + 1)
                        if u >= 4:
                            act.wait_ge(S("turned"), l * NU + u - 3)
                        if j < 0:
                            did(f(Pp(0)[0:META, 0:P], Pp(0)[0:META, 0:P], ACT.Exp), "exp")
                        else:
                            did(f(Pp(u)[:, 0:n], (WA, G[0])[u % 2][:, 0:n], ACT.Exp,
                                  bias=mx[:, u % 4, 0:1], accum_out=mx[:, u % 4, 1:2]), "exp")
                    if u == NU:
                        act.wait_ge(S("scores"), (l + 1) * NU)
                        for b in range(2):
                            act.dma_start(ctok[:, b, :], a["ctok"][l, b]).then_inc(S(f"ct_in{b}"), 16)
                    if u >= 3:
                        v = u - 3
                        j = UNITS[v][1]
                        act.wait_ge(S("turned"), l * NU + v + 1)
                        if v >= 2:
                            act.wait_ge(S("oa"), l * NU + v - 1)
                        w, rows = (META, P * (j + 2)) if j < 0 else (P, P * (j + 2))
                        did(f(Pt[0:w, v % 2, 0:rows], (WB, G[1])[v % 2][0:w, 0:rows], ACT.Copy), "Pt")
                for b in range(DB + 1):
                    if b < DB:
                        sl = b % 2
                        act.wait_ge(S("s_max"), l * DB + b + 1)
                        if b >= 2:
                            act.wait_ge(S("s_turned"), 3 * (l * DB + b - 1))
                        step(f(Ps[:, sl, 0:PAST], (G[0], WA)[sl][:, :], ACT.Exp,
                               bias=ms[:, sl, 3:4], accum_out=ms[:, sl, 4:5]))
                        did(f(Ps[:, sl, PAST:PAST + DT], WB[:, 512 + DT * sl:512 + DT * sl + DT], ACT.Exp,
                          bias=ms[:, sl, 3:4], accum_out=ms[:, sl, 5:6]), "s_exp")
                    if b >= 1:
                        v = b - 1
                        for x in range(2):
                            act.wait_ge(S("s_turned"), 3 * (l * DB + v) + x + 1)
                            if v and not x:
                                act.wait_ge(S("s_oa"), l * DB + v)
                            did(f(Pts[:, 512 * x:512 * x + 512], G[1][:, 512 * x:512 * x + 512], ACT.Copy), "s_Pt")
                        act.wait_ge(S("s_turned"), 3 * (l * DB + v + 1))
                        act.wait_ge(S("s_Pt"), 3 * (l * DB + v) + 2)
                        did(f(Pts[0:DT, 8 * P:9 * P], WB[0:DT, 0:P], ACT.Copy), "s_Pt")
                act.wait_ge(S("out"), 32 * (l + 1))
                for n in range(KD):
                    tt = t0 + T_OUT + n
                    c = squares(n0 + N_MIXPOST) + n
                    act.wait_ge(S(sq_free(c)[0]), sq_free(c)[1])
                    did(take(tt, two(sq[:, c % 2, :]), func=ACT.Square), "sq")
                    evac(tt, f(two(Y[:, n, :]), halves(G[tt % 2]), ACT.Copy))
                rstd(n0 + N_MIXPOST, WA, D, R)
                split_x(l, n0 + N_FFNPRE, C_FFNPRE, lambda k: act.wait_ge(S("x"), 2 * l * KD + k + 1))
                act.dma_start(cst[:, :], a["cst"][l]).then_inc(S("cst_in"), 16)
                rstd(n0 + N_FFNPRE, WA, D, R)
                for hf in range(2):
                    for i in range(FH + 1):
                        ff_ = l * KF + hf * FH + i
                        if i >= 1:
                            act.wait_ge(S("gv"), ff_)
                            if hf and i == 1:
                                act.wait_ge(S("tile"), t0 + T_DOWN[0] + KD)
                            did(f(gh[:, i - 1, :], tmp[:, (ff_ - 1) % 2, :], ACT.Copy), "gh")
                        if i < FH:
                            act.wait_ge(S("conv"), ff_ + 1)
                            if ff_ >= 2:
                                act.wait_ge(S("gl"), ff_ - 1)
                            d = tmp[:, ff_ % 2, :]
                            did(f(d[:, 0:PT], cc[:, 0:PT], ACT.Silu), "act")
                            did(f(samples(d[:, PT:T]), samples(cc[:, 2 + PT:EXT], DT + 2)[:, :, 0:DT], ACT.Silu), "silu")
                    for n in range(KD):
                        tt = t0 + T_DOWN[hf] + n
                        if hf == 0:
                            evac(tt, take(tt, two(Y[:, n, :])))
                        else:
                            act.wait_ge(S("y2"), l * KD + n + 1)
                            square_x(n0 + N_FFNPOST, n, Y[:, n, :])
                exp_table()
                rstd(n0 + N_FFNPOST, WA, D, R)
                act.dma_start(a["o_conv"][l], cout[:, :, :]).then_inc(S("conv_out"), 16)
                act.wait_ge(S("conv_out"), 16 * (l + 1))
            for k in range(KD):
                act.wait_ge(S("x"), (2 * DEPTH - 1) * KD + k + 1)
                square_x(DEPTH * N_NORM, k, X[:, k, :])
            rstd(DEPTH * N_NORM, WA, D, R)
            for k in range(KD):
                act.wait_ge(S("y_out"), k + 1)
                act.dma_start(a["o_y"][k], Y[:, k, :]).then_inc(S("out"), 16)
            act.wait_ge(S("out"), 16 * (2 * DEPTH + KD))

        @block.vector
        def _(dve):
            count, last = {}, []

            def did(ins, name, at=None):
                count[name] = at or count.get(name, 0) + 1
                last[:] = [name]
                ins.then_inc(S(name), 1)

            def prev():
                if last:
                    dve.wait_ge(S(last[0]), count[last[0]])

            def op(kind):
                def go(*args, **kw):
                    prev()
                    return kind(*args, **kw)
                return go

            tt_, ts, stt, cp = (op(k) for k in (dve.tensor_tensor, dve.tensor_scalar, dve.scalar_tensor_tensor,
                                                dve.tensor_copy))
            scan, fill, keep, rmax, rsum, recip, mark = (op(k) for k in (
                dve.tensor_tensor_scan, dve.memset, dve.copy_predicated, dve.reduce_max, dve.reduce_sum,
                dve.reciprocal, dve.engine_nop))

            def step(ins):
                did(ins, "dve")

            def evac(tt, ins):
                did(ins, f"evac{tt % 2}", slot_use(tt))

            step(fill(eps[:, :], EPS))
            step(fill(Am[:, :], 0.0))
            step(fill(G[1][:, 256:512], 0.0))
            dve.wait_ge(S("cols_in"), 16)
            did(tt_(lbs[:, 0, 0, :], cols[:, 0, C_LB1:C_LB1 + HG], cols[:, 0, C_LB0:C_LB0 + HG], ALU.subtract), "lbd")

            def add_square(n, k, first):
                c = squares(n) + k
                dve.wait_ge(S("sq"), c + 1)
                if first:
                    if sums(n):
                        dve.wait_ge(S("ssum"), sums(n))
                    did(cp(acc[:, :], sq[:, c % 2, :]), "sq_added")
                else:
                    did(tt_(acc[:, :], acc[:, :], sq[:, c % 2, :], ALU.add), "sq_added")

            def col(l, c):
                return cols[:, l, c:c + 1]

            def split_cq(l):
                for k in range(2):
                    did(stt(tmp[:, k, :], DE[:, k, :], col(l, C_QN + k), R2[:, :], ALU.mult, ALU.mult), "hf")
                for k in range(2):
                    dve.wait_ge(S("hh"), l * SPLITS + KD + k + 1)
                    did(tt_(cql[:, k, :], tmp[:, k, :], cqh[:, k, :], ALU.subtract), "hl")

            def rest_of_x(l, base, c_w, k):
                dve.wait_ge(S("hh"), base + k + 1)
                did(stt(Hl[:, k, :], X[:, k, :], col(l, c_w + k), Hh[:, k, :], ALU.mult, ALU.subtract), "hl")

            def rotate(tt, dst, scale=1.0, slot=0):
                ps = G[tt % 2]
                step(stt(two(tmp[64:96, slot, :]), halves(ps, HALF, 96, P), scale, two(rope[96:P, :]), ALU.mult, ALU.mult))
                evac(tt, stt(two(dst), halves(ps, HALF, 64, 96), scale, two(rope[64:96, :]), ALU.mult, ALU.mult))

            def residual(l, n, c_w, r, then):
                dve.wait_ge(S("rstd"), n + 1)
                for k in range(KD + 2):
                    if k < KD:
                        if k >= 2:
                            dve.wait_ge(S("x"), r * KD + k - 1)
                        did(stt(tmp[:, k % 2, :], Y[:, k, :], col(l, c_w + k), R[:, :], ALU.mult, ALU.mult), "dx")
                    if k >= 2 and then:
                        then(k - 2)
                did(mark(), "R_used")

            def scaled(tt, dst):
                dve.wait_ge(S("tile"), tt + 1)
                evac(tt, tt_(two(dst), halves(G[tt % 2]), two(R[:, :]), ALU.mult))

            def hg_diff(l, h, lv):
                n, m, G_, d = l * HG + h, LEVELS[lv], hG(h), DE[:, lv % 2, :]
                g1, g2, ref = sub_halves(G_, m)
                d1, d2, _ = sub_halves(d, m)
                step(tt_(d1, ref, g1, ALU.subtract))
                did(tt_(d2, g2, ref, ALU.subtract), "D")

            def hg_decayed(l, h, lv):
                n, m = l * HG + h, LEVELS[lv]
                dve.wait_ge(S("E"), n * (LV + 1) + lv + 1)
                e1, e2, _ = sub_halves(DE[:, lv % 2, :], m)
                z1, z2, _ = sub_halves(Z[:, lv % 2, :], m)
                k1, _, _ = sub_halves(hk(h), m)
                _, q2, _ = sub_halves(hq(h), m)
                step(tt_(z1, k1, e1, ALU.mult))
                did(tt_(z2, q2, e2, ALU.mult), "Z")

            def hg_take(l, h, lv):
                n, m, bank = (l * HG + h) * LV + lv, LEVELS[lv], 512 * (lv % 2)
                dve.wait_ge(S("A"), n + 1)
                mk = masks[:, lv, :]
                if m <= 8:
                    step(keep(Am[:, 512:640], mk, WB[:, bank:bank + P]))
                    step(keep(Am[0:META, 640:640 + META], mk[0:META, 0:META],
                                             WB[0:META, bank + P:bank + P + META]))
                did(keep(Am[:, 0:512].rearrange("p (j t) -> p j t", j=4),
                                    mk.rearrange("p (a t) -> p a t", a=1).broadcast_to([P, 4, P]),
                                    WA[:, bank:bank + 512].rearrange("p (j t) -> p j t", j=4)), "A_taken")

            for l in range(DEPTH):
                t0, n0 = l * TILES, l * N_NORM
                if l == 0:
                    for k in range(KD):
                        rest_of_x(l, 0, C_MIXPRE, k)
                if l == 0:
                    dve.wait_ge(S("const"), 16 * N_CONST)
                    step(cp(reset[:, :], reset_f))
                    step(cp(masks[:, :, :].rearrange("p (a b) t -> p a (b t)", a=2), mask_f))
                    dve.wait_ge(S("lb_sig"), 2)
                    step(fill(lbs[:, 0, 0, :], 0.0))
                    step(fill(lbs[:, 0, 1, :], 1.0))
                step(fill(Am[:, :], 0.0))
                dve.wait_ge(S("rstd"), n0 + N_MIXPRE + 1)
                for i, dst in enumerate((DE[:, 0, :], DE[:, 1, :], kvn[:, :])):
                    scaled(t0 + i, dst)
                add_square(n0 + N_CQ, 0, True)
                add_square(n0 + N_CQ, 1, False)
                dve.wait_ge(S("tile"), t0 + 4)
                rotate(t0 + 3, kpe[64:96, :])
                step(tt_(kpe[64:96, :], kpe[64:96, :], tmp[64:96, 0, :], ALU.add))
                did(tt_(kpe[64:96, :], kpe[64:96, :], R[64:96, :], ALU.mult), "kpe")
                scaled(t0 + T_HG, hv(0))
                dve.wait_ge(S("rstd"), n0 + N_CQ + 1)
                split_cq(l)
                did(mark(), "R2_used")
                add_square(n0 + N_CKV, 0, True)
                scaled(t0 + T_HG + 1, hk(0))
                scaled(t0 + T_HG + 2, hq(0))
                dve.wait_ge(S("rstd"), n0 + N_CKV + 1)
                did(stt(kvn[:, :], kvn[:, :], col(l, C_KVN), R2[:, :], ALU.mult, ALU.mult), "kvn")
                did(mark(), "R2_used")
                scaled(t0 + T_HG + 3, gate[:, 0, :])

                def gated(h):
                    n = l * HG + h
                    dve.wait_ge(S("sig"), 3 * (n + 1))
                    step(ts(hk(h), hk(h), lbs[:, l, 1, h:h + 1], None, ALU.mult))
                    did(tt_(hq(h), hq(h), tmp[:, 0, :], ALU.mult), "gated")
                    did(tt_(gate[:, h % 2, :], gate[:, h % 2, :], tmp[:, 1, :], ALU.mult), "gated")
                    dve.wait_ge(S("gl_"), n + 1)
                    step(scan(hG(h), reset[:, :], hG(h), 0.0, ALU.mult, ALU.add))

                def queries(h):
                    dve.wait_ge(S("q_nope"), l * HM + h + 1)
                    if h >= 2:
                        dve.wait_ge(S("rotated"), l * HM + h - 1)
                    rotate(t0 + T_UQ + h, Y[64:96, h, :], SCALE, h % 2)

                def new_state(h):
                    n = l * HG + h
                    dve.wait_ge(S("s0_decayed"), n + 1)
                    dve.wait_ge(S("dS_sample"), n + 1)
                    did(tt_(S0[:, h % 2, :], S0[:, h % 2, :], WB[:, :], ALU.add), "s0_new")

                def finish(h):
                    dve.wait_ge(S("rstd"), n0 + N_HG + h + 1)
                    did(tt_(ob[:, h, :], ob[:, h, :], R2[:, :], ALU.mult), "ob")
                    did(mark(), "R2_used")

                gated(0)
                for h in range(HG):
                    n, th = l * HG + h, t0 + T_HG + 4 * (h + 1)
                    for i in range(LV + 2):
                        if i < LV - 1:
                            hg_diff(l, h, i)
                        if i == 0 and h:
                            new_state(h - 1)
                        if 1 <= i < LV:
                            hg_decayed(l, h, i - 1)
                        if i == LV - 1:
                            G_, d = hG(h), DE[:, 0, :]
                            step(tt_(d[:, 0:META], G_[:, META - 1:META].broadcast_to([P, META]), G_[:, 0:META],
                                     ALU.subtract))
                            for lo, hi_, w in ((META, PT, P), (PT, T, DT)):
                                g3 = G_[:, lo:hi_].rearrange("p (b t) -> p b t", t=w)
                                e = tt_(d[:, lo:hi_].rearrange("p (b t) -> p b t", t=w),
                                        g3[:, :, w - 1:w].broadcast_to([P, (hi_ - lo) // w, w]), g3, ALU.subtract)
                                did(e, "dve" if lo == META else "D")
                        if i in (1, 3, 5, 8) and h + 1 < HG:
                            x = (1, 3, 5, 8).index(i)
                            scaled(th + x, (hv(h + 1), hk(h + 1), hq(h + 1), gate[:, (h + 1) % 2, :])[x])
                        elif i in (1, 3, 5):
                            queries(i // 2)
                            if i == 5:
                                queries(3)
                        if i == 3 and h:
                            finish(h - 1)
                        if i >= 2:
                            hg_take(l, h, i - 2)
                    dve.wait_ge(S("E"), n * (LV + 1) + LV + 1)
                    did(tt_(hk(h), hk(h), DE[:, 0, :], ALU.mult), "kG")
                    did(tt_(hq(h), hq(h), DE[:, 1, :], ALU.mult), "qG")
                    dve.wait_ge(S("tok"), 2 * n + 1)
                    did(tt_(Z[:, :, :].rearrange("p a n -> p (a n)")[:, 0:DB * P].rearrange("p (b v) -> p b v", b=DB),
                            vtok[:, 512:640].rearrange("p (a v) -> p a v", a=1).broadcast_to([P, DB, P]),
                            ind[:, :].rearrange("p (b a) -> p b a", a=1).broadcast_to([P, DB, P]), ALU.mult), "v_apart")
                    if h + 2 == HG:
                        did(mark(), "R_used")
                    dve.wait_ge(S("dS"), n + 1)
                    if n:
                        dve.wait_ge(S("pst_out"), 16 * n)
                    did(cp(st[:, 0, :], WA[:, 512:640]), "state")
                    for j in range(4):
                        dve.wait_ge(S("state"), 5 * n + j + 1)
                        e_ = META + P * (j + 1) - 1
                        did(stt(st[:, j + 1, :], st[:, j, :], DE[:, 1, e_:e_ + 1], WA[:, P * j:P * j + P], ALU.mult, ALU.add), "state")
                    if h + 1 < HG:
                        gated(h + 1)
                    c = squares(n0 + N_HG + h)
                    dve.wait_ge(S("o"), n + 1)
                    dve.wait_ge(S("sq"), c + 1)
                    gt = gate[:, h % 2, :]
                    for (p0, p1), (a0, a1) in (((0, 512), (META, PT)), ((512, 512 + META), (0, META))):
                        step(stt(ob[:, h, a0:a1], WA[:, p0:p1], col(l, C_HGN), gt[:, a0:a1], ALU.mult, ALU.mult))
                    step(stt(ob[:, h, PT:T], WA[:, 640:640 + SAMP], col(l, C_HGN), gt[:, PT:T], ALU.mult, ALU.mult))
                    if n:
                        dve.wait_ge(S("s0_decayed"), n)
                    did(cp(dec[:, :].rearrange("p (b a) -> p b a", a=1), samples(DE[:, 1, PT:T])[:, :, DT - 1:DT]), "dec")
                    dve.wait_ge(S("ssum"), sums(n0 + N_HG + h))
                    did(mark(), "o_taken")
                    did(cp(acc[:, :], sq[:, c % 2, :]), "sq_added")
                new_state(HG - 1)
                queries(HG)
                queries(HG + 1)
                finish(HG - 1)
                for h in range(HG + 2, HM):
                    queries(h)
                dve.wait_ge(S("sst_out0"), 16 * 2 * (l + 1))
                dve.wait_ge(S("sst_out1"), 16 * 2 * (l + 1))
                dve.wait_ge(S("pst_out"), 16 * HG * (l + 1))
                step(cp(KT[64:96, :, :], kpe[64:96, 0:PT].rearrange("p (a n) -> p a n", a=1).broadcast_to([32, HM, PT])))
                for i in range(5):
                    dve.wait_ge(S("values"), 5 * l + i + 1)
                    ps = (WA, WA, WB, WB, WA)[i]
                    c = (0, 512, 0, 512, 0)[i]
                    np_ = P if i < 4 else META
                    did(cp(vt[0:np_, i, :], ps[0:np_, c:c + 512]), "vt")
                dve.wait_ge(S("ql_ps"), 2 * l + 1)
                dve.wait_ge(S("rotated"), HM * (l + 1))
                did(cp(ql.rearrange("p (b h t) -> p h b t", h=HM, t=DT),
                       G[1][:, :].rearrange("p (h b t) -> p h b t", h=HM, t=DT)), "ql")
                for u in range(NU + 4):
                    if u < NU:
                        j = UNITS[u][1]
                        ps = (WA, G[0])[u % 2]
                        dve.wait_ge(S("scores"), l * NU + u + 1)
                        if j < 0:
                            s3 = ps[0:META, 0:P].rearrange("p (h k) -> p h k", h=HM)
                            p3 = Pp(0)[0:META, 0:P].rearrange("p (h k) -> p h k", h=HM)
                            step(rmax(mxm[:, 0, :], s3, AX_X))
                            did(tt_(p3, s3, mxm[:, 0, :].rearrange("p (h a) -> p h a", a=1)
                                    .broadcast_to([META, HM, META]), ALU.subtract), "max")
                        else:
                            did(rmax(mx[:, u % 4, 0:1], ps[:, 0:unit_keys(j)], AX_X, negate=True), "max")
                    if 1 <= u < NU + 1:
                        v = u - 1
                        dve.wait_ge(S("exp"), l * NU + v + 1)
                        if v == 0:
                            step(rsum(mxm[:, 1, :], p3, AX_X))
                            step(recip(mxm[:, 2, :], mxm[:, 1, :]))
                            did(tt_(p3, p3, mxm[:, 2, :].rearrange("p (h a) -> p h a", a=1)
                                    .broadcast_to([META, HM, META]), ALU.mult), "probs_meta")
                        else:
                            did(recip(mx[:, v % 4, 2:3], mx[:, v % 4, 1:2]), "inv_sum")
                    if u >= 4:
                        v = u - 4
                        h, j = UNITS[v]
                        dve.wait_ge(S("oa"), l * NU + v + 1)
                        o = (WB, G[1])[v % 2][0:VH, 640:640 + P]
                        if j < 0:
                            for par in range(2):
                                rows = slice(64 * par, 64 * par + 64)
                                o4 = o.rearrange("p (g a t) -> p a g t", g=4, a=2)[:, par, :, :]
                                step(cp(Hh[rows, 0:4, 0:META], o4))
                                did(tt_(Hl[rows, 0:4, 0:META], o4, Hh[rows, 0:4, 0:META], ALU.subtract),
                                    "oa_taken" if par else "dve")
                        else:
                            rows, q0 = slice(64 * (h % 2), 64 * (h % 2) + 64), META + P * j
                            step(cp(Hh[rows, h // 2, q0:q0 + P], o))
                            did(tt_(Hl[rows, h // 2, q0:q0 + P], o, Hh[rows, h // 2, q0:q0 + P], ALU.subtract), "oa_taken")
                for b in range(DB + 2):
                    sl = b % 2
                    if b < DB:
                        m = ms[:, sl, :]
                        dve.wait_ge(S("s_scores"), l * (DB - 1) + max(b, 1))
                        step(rmax(m[:, 1:2], WB[:, 512 + DT * sl:512 + DT * sl + DT], AX_X, negate=True))
                        step(rmax(m[:, 0:1], (G[0], WA)[sl][:, :], AX_X, negate=True))
                        did(tt_(m[:, 3:4], m[:, 0:1], m[:, 1:2], ALU.min), "s_max")
                    if b >= 2:
                        v = b - 2
                        dve.wait_ge(S("s_oa"), l * DB + v + 1)
                        did(cp(OL[:, :, DT * v:DT * v + DT], WB[:, P:2 * P].rearrange("p (h t) -> p h t", h=HM)), "ol_taken")
                    if b < DB:
                        dve.wait_ge(S("s_exp"), l * DB + b + 1)
                        step(tt_(m[:, 6:7], m[:, 4:5], m[:, 5:6], ALU.add))
                        step(recip(m[:, 7:8], m[:, 6:7]))
                        did(ts(Ps[:, sl, :], Ps[:, sl, :], m[:, 7:8], None, ALU.mult), "s_probs")
                dve.wait_ge(S("oas"), l + 1)
                for par in range(2):
                    rows = slice(64 * par, 64 * par + 64)
                    o = WA[0:VH, :].rearrange("p (g a t) -> p a g t", g=4, a=2)[:, par, :, :]
                    step(cp(Hh[rows, 0:4, PT:T], o))
                    e = tt_(Hl[rows, 0:4, PT:T], o, Hh[rows, 0:4, PT:T], ALU.subtract)
                    if par == 0:
                        step(e)
                did(e, "oas_taken")
                for n in range(KD):
                    add_square(n0 + N_MIXPOST, n, n == 0)
                dve.wait_ge(S(f"evac{(t0 + T_OUT + KD - 1) % 2}"), slot_use(t0 + T_OUT + KD - 1))
                residual(l, n0 + N_MIXPOST, C_MIXPOST, 2 * l,
                         lambda k: rest_of_x(l, l * SPLITS + KD + 2, C_FFNPRE, k))
                dve.wait_ge(S("rstd"), n0 + N_FFNPRE + 1)
                step(fill(ax[:, :, 0:2], 0.0))
                dve.wait_ge(S("cst_in"), 16 * (l + 1))
                for hf in range(2):
                    for i in range(FH + 1):
                        ff_ = l * KF + hf * FH + i
                        fc = hf * FH + i
                        if i < FH:
                            tt = t0 + T_UP[hf] + 2 * i
                            s_ = ax[:, ff_ % 2, :]
                            sv = samples(s_[:, 2 + PT:EXT], DT + 2)
                            step(cp(sv[:, :, 0:2], cst[:, 16 * fc:16 * fc + 16].rearrange("p (b t) -> p b t", t=2)))
                            dve.wait_ge(S("tile"), tt + 1)
                            ps = G[tt % 2]
                            step(tt_(s_[:, 2:2 + HALF], ps[:, 0:HALF], R[:, 0:HALF], ALU.mult))
                            step(tt_(s_[:, 2 + HALF:2 + PT], ps[:, 512:512 + PT - HALF], R[:, HALF:PT], ALU.mult))
                            evac(tt, tt_(sv[:, :, 2:], samples(ps[:, 512 + PT - HALF:512 + HALF]), samples(R[:, PT:T]),
                                         ALU.mult))
                            step(cp(cout[:, fc, 0:2], s_[:, PT:PT + 2]))
                            step(cp(cout[:, fc, 2:18].rearrange("p (b t) -> p b t", t=2), sv[:, :, DT:DT + 2]))
                            if ff_:
                                dve.wait_ge(S("silu"), ff_)
                            n_ = EXT - 2
                            step(ts(cc[:, 0:n_], s_[:, 0:n_], col(l, C_CW + fc), col(l, C_CB + fc), ALU.mult, ALU.add))
                            step(stt(cc[:, 0:n_], s_[:, 1:1 + n_], col(l, C_CW + KF + fc), cc[:, 0:n_], ALU.mult, ALU.add))
                            did(stt(cc[:, 0:n_], s_[:, 2:2 + n_], col(l, C_CW + 2 * KF + fc), cc[:, 0:n_], ALU.mult, ALU.add), "conv")
                        if i >= 1:
                            dve.wait_ge(S("gh"), ff_)
                            did(tt_(gl[:, i - 1, :], tmp[:, (ff_ - 1) % 2, :], gh[:, i - 1, :], ALU.subtract), "gl")
                        if i < FH:
                            tt = t0 + T_UP[hf] + 2 * i + 1
                            dve.wait_ge(S("silu"), ff_ + 1)
                            step(tt_(tmp[:, ff_ % 2, :], tmp[:, ff_ % 2, :], R[:, :], ALU.mult))
                            dve.wait_ge(S("tile"), tt + 1)
                            d = two(tmp[:, ff_ % 2, :])
                            step(tt_(d, halves(G[tt % 2]), d, ALU.mult))
                            did(mark(), "gv")
                            evac(tt, mark())
                    if hf:
                        did(mark(), "R_used")
                    for n in range(KD):
                        tt = t0 + T_DOWN[hf] + n
                        if hf:
                            dve.wait_ge(S("tile"), tt + 1)
                            step(tt_(two(Y[:, n, :]), two(Y[:, n, :]), halves(G[tt % 2]), ALU.add))
                            did(mark(), "y2")
                            evac(tt, mark())
                            add_square(n0 + N_FFNPOST, n, n == 0)
                if l + 1 < DEPTH:
                    residual(l, n0 + N_FFNPOST, C_FFNPOST, 2 * l + 1,
                             lambda k: rest_of_x(l + 1, (l + 1) * SPLITS, C_MIXPRE, k))
                else:
                    residual(l, n0 + N_FFNPOST, C_FFNPOST, 2 * l + 1,
                             None)
            dve.wait_ge(S("rstd"), DEPTH * N_NORM + 1)
            for k in range(KD):
                did(stt(Y[:, k, :], X[:, k, :], col(0, C_FIN + k), R[:, :], ALU.mult, ALU.mult), "y_out")


def layouts(x):
    f = np.float32
    ins = {}
    tokens = np.concatenate([x["meta_tokens"], x["x_prompt"][0], x["x_sample"].reshape(SAMP, D)], 0)
    ins["xT"] = tokens.T.reshape(KD, P, T)

    def blocks(w):
        k, n = w.shape
        return w.reshape(k // P, P, n // P, P).transpose(2, 1, 0, 3).reshape(n // P, P, k)

    in_cols = [np.arange(i * P, i * P + P) for i in range(3)]
    pe = QL + KL + np.arange(ROPE)
    swap = np.concatenate([pe[ROPE // 2:], pe[:ROPE // 2]])
    in_cols.append(np.concatenate([pe, pe, pe, swap]))
    base = QL + KL + ROPE
    for h in range(HG):
        for part in (2, 1, 0, 3):
            in_cols.append(base + part * HG * P + h * P + np.arange(P))
    in_cols = np.concatenate(in_cols)
    uq_cols = np.concatenate([h * (NOPE + ROPE) + np.concatenate(
        [np.arange(NOPE), NOPE + np.arange(ROPE), NOPE + ROPE // 2 + np.arange(ROPE // 2), NOPE + np.arange(ROPE // 2)])
        for h in range(HM)])
    stream = []
    for l in range(DEPTH):
        up = x["w_ffn_up"][l]
        av = np.stack([up[:, :FF].reshape(D, KF, P), up[:, FF:].reshape(D, KF, P)], 2).reshape(D, 2 * FF)
        uq = blocks(x["w_uq"][l][:, uq_cols])
        parts = [blocks(x["w_in"][l][:, in_cols]),
                 uq.reshape(2, 4, P, 256).transpose(0, 2, 1, 3).reshape(2, P, W_PIECE),
                 blocks(x["w_out"][l])]
        for hf in range(2):
            parts.append(blocks(av[:, hf * 2 * FH * P:(hf + 1) * 2 * FH * P]))
            dn = x["w_ffn_down"][l][hf * FH * P:(hf + 1) * FH * P].reshape(FH, P, KD, P)
            parts.append(dn.transpose(2, 0, 1, 3).reshape(FH, 8, P, P).transpose(0, 2, 1, 3).reshape(FH, P, W_PIECE))
        stream.append(np.concatenate(parts, 0))
    ins["wstream"] = np.stack(stream)
    ins["wA"] = np.concatenate([x["w_uk"].reshape(DEPTH, KL, 512), x["w_uv"].reshape(DEPTH, KL, 512)], 2)
    ins["wB"] = x["w_uk"].transpose(0, 3, 2, 1).reshape(DEPTH, NOPE, 1024)
    ins["ckT"] = x["cache_kv_latent"].transpose(0, 1, 3, 2)
    ins["cpe"] = x["cache_k_rope"].transpose(0, 1, 3, 2)
    ins["ctok"] = x["cache_kv_latent"].reshape(DEPTH, DB, PC, P, KL).transpose(0, 1, 3, 2, 4).reshape(DEPTH, DB, P, PAST)
    ins["s0"] = x["state_hgrn"].transpose(0, 2, 3, 1, 4).reshape(DEPTH, HG, P, DB * P)
    ins["cst"] = x["state_ffn_conv"].transpose(0, 3, 1, 2).reshape(DEPTH, KF, P, DB * 2).transpose(0, 2, 1, 3)\
        .reshape(DEPTH, P, KF * DB * 2)

    def col(v):
        return v.reshape(v.shape[0], -1, P)

    both = lambda v: np.stack([v, v])
    pack = np.concatenate([
        col(x["norm_mix_pre"]), col(x["norm_mix_post"]), col(x["norm_ffn_pre"]), col(x["norm_ffn_post"]),
        col(x["q_norm"]), col(x["kv_norm"]), col(x["hg_out_norm"]),
        both(x["hg_lower_bounds"][0].reshape(HG, P)), both(x["hg_lower_bounds"][1].reshape(HG, P)),
        both(x["final_norm"].reshape(KD, P)), col(x["ffn_conv_b"]), x["ffn_conv_w"].reshape(DEPTH, CONV * KF, P)], 1)
    ins["cols"] = pack.transpose(2, 0, 1)
    pos = np.concatenate([np.arange(PT) - META, PAST + np.tile(np.arange(DT), DB)]).astype(f)
    inv = f(10000.0) ** (-np.arange(ROPE // 2, dtype=f) / f(ROPE // 2))
    ang = (inv[:, None] * pos[None]).astype(f)
    tab = np.zeros((P, T), f)
    tab[64:80] = tab[80:96] = np.cos(ang)
    tab[96:112], tab[112:128] = -np.sin(ang), np.sin(ang)
    ins["rope"] = tab
    rs = np.ones((P, T), f)
    rs[:, [0] + [META + P * j for j in range(4)] + [PT + DT * b for b in range(DB)]] = 0
    ins["reset"] = rs
    s, t = np.arange(P)[:, None], np.arange(P)[None]
    ins["masks"] = np.stack([(s // (2 * m) == t // (2 * m)) & (s % (2 * m) < m) & (t % (2 * m) >= m) if m else s == t
                             for m in LEVELS], 1).astype(f).reshape(P, 2, -1)
    ins["ones"], ins["ident"] = np.ones((P, P), f), np.eye(P, dtype=f)
    ins["ind"] = (np.arange(P)[:, None] // DT == np.arange(DB)[None]).astype(f)
    q, k = np.zeros((4, T), f), np.zeros((4, PT), f)
    for j in range(4):
        q[j, META + P * j:META + P * j + CH] = 1
        k[j, META + P * j + CH:META + P * (j + 1)] = -BIG
    ins["qrows"] = np.repeat(q[:, None], HM, 1)
    ins["krows"] = np.repeat(k[:, None], HM, 1)
    return {n: np.ascontiguousarray(v) for n, v in ins.items()}


CONV = 3
OUTS = {
    "o_y": (KD, P, T), "o_kv": (DEPTH, P, T), "o_kpe": (DEPTH, ROPE, T), "o_pst": (DEPTH, HG, P, P),
    "o_sst": (DEPTH, HG, P, DB * P), "o_conv": (DEPTH, P, KF, 2 + DB * 2),
}


def kernel(**inputs):
    import concourse.bacc as bacc
    from concourse.bass_utils import run_bass_kernel_spmd

    arrays = {"in_" + n: v for n, v in layouts({k: np.asarray(v) for k, v in inputs.items()}).items()}
    nc = bacc.Bacc("TRN2", target_bir_lowering=False, num_devices=1)
    aps = {n[3:]: nc.dram_tensor(n, v.shape, mybir.dt.from_np(v.dtype), kind="ExternalInput").ap() for n, v in arrays.items()}
    for n, shape in OUTS.items():
        aps[n] = nc.dram_tensor(n, shape, F32, kind="ExternalOutput").ap()
    build(nc, aps)
    r = run_bass_kernel_spmd(nc, [arrays], core_ids=[0]).results[0]
    y = r["o_y"].reshape(D, T)
    kv, kpe, conv = r["o_kv"], r["o_kpe"], r["o_conv"]
    conv = conv.transpose(0, 2, 1, 3).reshape(DEPTH, FF, 2 + DB * 2)
    sst = r["o_sst"].reshape(DEPTH, HG, P, DB, P).transpose(0, 3, 1, 2, 4)

    def rows(v):
        v = v.transpose(0, 2, 1)
        return v[:, None, :PT], v[:, PT:].reshape(DEPTH, DB, DT, -1)

    (pkv, skv), (ppe, spe) = rows(kv), rows(kpe)
    out = (y[:, META:PT].T[None], y[:, PT:].T.reshape(DB, DT, D), pkv, ppe, r["o_pst"][:, None],
           conv[:, :, :2].transpose(0, 2, 1)[:, None], skv, spe, sst,
           conv[:, :, 2:].reshape(DEPTH, FF, DB, 2).transpose(0, 2, 3, 1))
    return tuple(np.ascontiguousarray(o) for o in out)
```
